# Optimizing a Trainium2 kernel written in Bass

```python
import jax, jax.numpy as jnp
from jax import lax
import numpy as np

D_MODEL = 1024
BATCH = 1
SEQ = 256
DEPTH = 1
DEC_BATCH = 8
DEC_SEQ = 8
PAST_LEN = 2048
PAGE_SIZE = 128

HEAD_DIM = 64
N_Q_HEADS = 8
N_KV_HEADS = 2
GROUP = N_Q_HEADS // N_KV_HEADS
ATTN_WIDTH = N_Q_HEADS * HEAD_DIM
KV_WIDTH = N_KV_HEADS * HEAD_DIM
WINDOW = 128
ROPE_THETA = 500000.0
ROPE_DIM = HEAD_DIM // 4
CONV_WIDTH = D_MODEL - ATTN_WIDTH
CONV_K = 31
MIX_WIDTH = ATTN_WIDTH + CONV_WIDTH
IN_WIDTH = ATTN_WIDTH + 2 * KV_WIDTH + 2 * CONV_WIDTH
N_EXPERTS = 32
TOP_K = 4
D_FF = D_MODEL
SWIGLU_LIMIT = 7.0
SWIGLU_ALPHA = 1.702
MOE_BLOCK = 256
RMS_EPS = 1e-5
LN_EPS = 1e-5

kernel_name = "hymba_swa_sink_conformer_conv_moe_step"

def rms_norm(x, g):
    xf = x.astype(jnp.float32)
    y = xf * lax.rsqrt(jnp.mean(xf * xf, axis=-1, keepdims=True) + RMS_EPS)
    return (y * g.astype(jnp.float32)).astype(x.dtype)

def layer_norm(x, g, b):
    xf = x.astype(jnp.float32)
    mu = jnp.mean(xf, axis=-1, keepdims=True)
    xc = xf - mu
    var = jnp.mean(xc * xc, axis=-1, keepdims=True)
    y = xc * lax.rsqrt(var + LN_EPS) * g.astype(jnp.float32) + b.astype(jnp.float32)
    return y.astype(x.dtype)

def partial_rotary(x, pos):
    half = ROPE_DIM // 2
    inv_freq = jnp.power(jnp.float32(ROPE_THETA), -jnp.arange(half, dtype=jnp.float32) * 2.0 / ROPE_DIM)
    ang = pos.astype(jnp.float32)[:, None] * inv_freq[None, :]
    cos = jnp.cos(ang)[:, None, :]
    sin = jnp.sin(ang)[:, None, :]
    xr = x[..., :ROPE_DIM].astype(jnp.float32)
    x1, x2 = xr[..., :half], xr[..., half:]
    rot = jnp.concatenate([x1 * cos - x2 * sin, x2 * cos + x1 * sin], axis=-1).astype(x.dtype)
    return jnp.concatenate([rot, x[..., ROPE_DIM:]], axis=-1)

def banded_sink_attention(q, k, v, q_pos, k_pos, sinks):
    scale = HEAD_DIM ** -0.5
    s = jnp.einsum('nbqhgd,nbkhd->nbhgqk', q.astype(jnp.float32), k.astype(jnp.float32)) * scale
    diff = q_pos[:, :, None] - k_pos[:, None, :]
    valid = (diff >= 0) & (diff < WINDOW) & (k_pos >= 0)[:, None, :]
    s = jnp.where(valid[None, :, None, None], s, -jnp.inf)
    sink = sinks.astype(jnp.float32).reshape(N_KV_HEADS, GROUP)[:, :, None, None]
    m = jnp.maximum(jnp.max(s, axis=-1, keepdims=True), sink)
    p = jnp.exp(s - m)
    p = p / (jnp.sum(p, axis=-1, keepdims=True) + jnp.exp(sink - m))
    o = jnp.einsum('nbhgqk,nbkhd->nbqhgd', p, v.astype(jnp.float32))
    return o.astype(v.dtype)

def prompt_window_attention(q, k, v, sinks):
    N, S = q.shape[0], q.shape[1]
    NB = S // WINDOW
    qb = q.reshape(N, NB, WINDOW, N_KV_HEADS, GROUP, HEAD_DIM)
    kb = k.reshape(N, NB, WINDOW, N_KV_HEADS, HEAD_DIM)
    vb = v.reshape(N, NB, WINDOW, N_KV_HEADS, HEAD_DIM)
    prev = lambda t: jnp.concatenate([jnp.zeros_like(t[:, :1]), t[:, :-1]], axis=1)
    kc = jnp.concatenate([prev(kb), kb], axis=2)
    vc = jnp.concatenate([prev(vb), vb], axis=2)
    base = jnp.arange(NB, dtype=jnp.int32)[:, None] * WINDOW
    q_pos = base + jnp.arange(WINDOW, dtype=jnp.int32)[None, :]
    k_pos = base - WINDOW + jnp.arange(2 * WINDOW, dtype=jnp.int32)[None, :]
    o = banded_sink_attention(qb, kc, vc, q_pos, k_pos, sinks)
    return o.reshape(N, S, ATTN_WIDTH)

def sample_window_attention(q, k, v, k_buf, v_buf, sinks):
    N, T = q.shape[0], q.shape[1]
    kc = jnp.concatenate([k_buf, k], axis=1)
    vc = jnp.concatenate([v_buf, v], axis=1)
    q_pos = PAST_LEN + jnp.arange(T, dtype=jnp.int32)[None, :]
    k_pos = PAST_LEN - WINDOW + jnp.arange(WINDOW + T, dtype=jnp.int32)[None, :]
    o = banded_sink_attention(q.reshape(N, 1, T, N_KV_HEADS, GROUP, HEAD_DIM),
                              kc[:, None], vc[:, None], q_pos, k_pos, sinks)
    return o.reshape(N, T, ATTN_WIDTH), kc[:, -WINDOW:], vc[:, -WINDOW:]

def conformer_conv(u, gate, ctx, w, b, ln_g, ln_b):
    a = u * jax.nn.sigmoid(gate)
    padded = jnp.concatenate([ctx.astype(a.dtype), a], axis=1)
    y = lax.conv_general_dilated(padded, w[:, None, :], window_strides=(1,), padding='VALID',
                                 dimension_numbers=('NWC', 'WIO', 'NWC'),
                                 feature_group_count=CONV_WIDTH) + b
    y = jax.nn.silu(layer_norm(y, ln_g, ln_b))
    return y, padded[:, -(CONV_K - 1):]

def clamped_swiglu(h):
    x_glu = jnp.minimum(h[..., :D_FF], SWIGLU_LIMIT)
    x_lin = jnp.clip(h[..., D_FF:], -SWIGLU_LIMIT, SWIGLU_LIMIT)
    return x_glu * jax.nn.sigmoid(SWIGLU_ALPHA * x_glu) * (x_lin + 1.0)

def moe(x, router_w, router_b, w1, b1, w2, b2):
    T = x.shape[0]
    logits = (x @ router_w + router_b).astype(jnp.float32)
    top_vals, top_idx = lax.top_k(logits, TOP_K)
    gates = jax.nn.softmax(top_vals, axis=-1).astype(x.dtype)
    A = T * TOP_K
    e_flat = top_idx.reshape(A)
    tok_flat = jnp.arange(A, dtype=jnp.int32) // TOP_K
    g_flat = gates.reshape(A)
    order = jnp.argsort(e_flat)
    e_sorted = e_flat[order]
    counts = jnp.bincount(e_flat, length=N_EXPERTS)
    starts = jnp.cumsum(counts) - counts
    padded = (counts + MOE_BLOCK - 1) // MOE_BLOCK * MOE_BLOCK
    pad_ends = jnp.cumsum(padded)
    pad_starts = pad_ends - padded
    dest = pad_starts[e_sorted] + jnp.arange(A, dtype=jnp.int32) - starts[e_sorted]
    n_blocks = -(-(A + N_EXPERTS * (MOE_BLOCK - 1)) // MOE_BLOCK)
    P = n_blocks * MOE_BLOCK
    row_tok = jnp.full((P,), T, dtype=jnp.int32).at[dest].set(tok_flat[order])
    row_gate = jnp.zeros((P,), dtype=x.dtype).at[dest].set(g_flat[order])
    blk_exp = jnp.minimum(jnp.searchsorted(pad_ends, jnp.arange(n_blocks, dtype=jnp.int32) * MOE_BLOCK,
                                           side='right'), N_EXPERTS - 1).astype(jnp.int32)
    x_pad = jnp.concatenate([x, jnp.zeros((1, x.shape[1]), x.dtype)], axis=0)

    def run_block(args):
        tok, e = args
        h = x_pad[tok] @ w1[e] + b1[e]
        return clamped_swiglu(h) @ w2[e] + b2[e]

    out = lax.map(run_block, (row_tok.reshape(n_blocks, MOE_BLOCK), blk_exp))
    out = out.reshape(P, -1) * row_gate[:, None]
    return jnp.zeros((T + 1, x.shape[1]), x.dtype).at[row_tok].add(out)[:T]

def split_in(z):
    N, S = z.shape[0], z.shape[1]
    k0 = ATTN_WIDTH
    v0 = k0 + KV_WIDTH
    u0 = v0 + KV_WIDTH
    g0 = u0 + CONV_WIDTH
    q = z[..., :k0].reshape(N, S, N_Q_HEADS, HEAD_DIM)
    k = z[..., k0:v0].reshape(N, S, N_KV_HEADS, HEAD_DIM)
    v = z[..., v0:u0].reshape(N, S, N_KV_HEADS, HEAD_DIM)
    return q, k, v, z[..., u0:g0], z[..., g0:]

def setup_inputs(seed: int = 0) -> dict:
    key = jax.random.key(seed)
    ks = jax.random.split(key, 24)
    f32 = jnp.float32
    nrm = lambda k, shape, s: jax.random.normal(k, shape, f32) * s
    return {
        "x_prompt": nrm(ks[0], (BATCH, SEQ, D_MODEL), 1.0),
        "x_sample": nrm(ks[1], (DEC_BATCH, DEC_SEQ, D_MODEL), 1.0),
        "cache_k": nrm(ks[2], (DEPTH, DEC_BATCH, WINDOW, N_KV_HEADS, HEAD_DIM), 1.0),
        "cache_v": nrm(ks[3], (DEPTH, DEC_BATCH, WINDOW, N_KV_HEADS, HEAD_DIM), 1.0),
        "state_conv": nrm(ks[4], (DEPTH, DEC_BATCH, CONV_K - 1, CONV_WIDTH), 0.5),
        "attn_norm_g": 1.0 + nrm(ks[5], (DEPTH, D_MODEL), 0.01),
        "w_in": nrm(ks[6], (DEPTH, D_MODEL, IN_WIDTH), D_MODEL ** -0.5),
        "attn_sinks": nrm(ks[7], (DEPTH, N_Q_HEADS), 0.5),
        "conv_w": nrm(ks[8], (DEPTH, CONV_K, CONV_WIDTH), CONV_K ** -0.5),
        "conv_b": nrm(ks[9], (DEPTH, CONV_WIDTH), 0.01),
        "conv_ln_g": 1.0 + nrm(ks[10], (DEPTH, CONV_WIDTH), 0.01),
        "conv_ln_b": nrm(ks[11], (DEPTH, CONV_WIDTH), 0.01),
        "w_out": nrm(ks[12], (DEPTH, MIX_WIDTH, D_MODEL), MIX_WIDTH ** -0.5),
        "ffn_norm_g": 1.0 + nrm(ks[13], (DEPTH, D_MODEL), 0.01),
        "router_w": nrm(ks[14], (DEPTH, D_MODEL, N_EXPERTS), D_MODEL ** -0.5),
        "router_b": nrm(ks[15], (DEPTH, N_EXPERTS), 0.01),
        "w1": nrm(ks[16], (DEPTH, N_EXPERTS, D_MODEL, 2 * D_FF), D_MODEL ** -0.5),
        "b1": nrm(ks[17], (DEPTH, N_EXPERTS, 2 * D_FF), 0.01),
        "w2": nrm(ks[18], (DEPTH, N_EXPERTS, D_FF, D_MODEL), D_FF ** -0.5),
        "b2": nrm(ks[19], (DEPTH, N_EXPERTS, D_MODEL), 0.01),
        "final_norm_g": 1.0 + nrm(ks[20], (D_MODEL,), 0.01),
    }

def reference(x_prompt, x_sample, cache_k, cache_v, state_conv, attn_norm_g, w_in, attn_sinks,
              conv_w, conv_b, conv_ln_g, conv_ln_b, w_out, ffn_norm_g, router_w, router_b,
              w1, b1, w2, b2, final_norm_g):
    xp, xs = x_prompt, x_sample
    Bp, Sp = xp.shape[0], xp.shape[1]
    Bs, Ss = xs.shape[0], xs.shape[1]
    pos_p = jnp.arange(Sp, dtype=jnp.int32)
    pos_s = PAST_LEN + jnp.arange(Ss, dtype=jnp.int32)
    kp_l, vp_l, cp_l, ks_l, vs_l, cs_l = [], [], [], [], [], []
    for l in range(DEPTH):
        qp, kp, vp, up, gp = split_in(rms_norm(xp, attn_norm_g[l]) @ w_in[l])
        qs, ks_, vs_, us, gs = split_in(rms_norm(xs, attn_norm_g[l]) @ w_in[l])
        qp, kp = partial_rotary(qp, pos_p), partial_rotary(kp, pos_p)
        qs, ks_ = partial_rotary(qs, pos_s), partial_rotary(ks_, pos_s)
        att_p = prompt_window_attention(qp, kp, vp, attn_sinks[l])
        att_s, nk_s, nv_s = sample_window_attention(qs, ks_, vs_, cache_k[l], cache_v[l], attn_sinks[l])
        zero_ctx = jnp.zeros((Bp, CONV_K - 1, CONV_WIDTH), up.dtype)
        cv_p, nc_p = conformer_conv(up, gp, zero_ctx, conv_w[l], conv_b[l], conv_ln_g[l], conv_ln_b[l])
        cv_s, nc_s = conformer_conv(us, gs, state_conv[l], conv_w[l], conv_b[l], conv_ln_g[l], conv_ln_b[l])
        xp = xp + jnp.concatenate([att_p, cv_p], axis=-1) @ w_out[l]
        xs = xs + jnp.concatenate([att_s, cv_s], axis=-1) @ w_out[l]
        kp_l.append(kp[:, -WINDOW:]); vp_l.append(vp[:, -WINDOW:]); cp_l.append(nc_p)
        ks_l.append(nk_s); vs_l.append(nv_s); cs_l.append(nc_s)
        hf = jnp.concatenate([rms_norm(xp, ffn_norm_g[l]).reshape(Bp * Sp, D_MODEL),
                              rms_norm(xs, ffn_norm_g[l]).reshape(Bs * Ss, D_MODEL)], axis=0)
        mo = moe(hf, router_w[l], router_b[l], w1[l], b1[l], w2[l], b2[l])
        xp = xp + mo[:Bp * Sp].reshape(Bp, Sp, D_MODEL)
        xs = xs + mo[Bp * Sp:].reshape(Bs, Ss, D_MODEL)
    y_prompt = rms_norm(xp, final_norm_g)
    y_sample = rms_norm(xs, final_norm_g)
    return (y_prompt, y_sample, jnp.stack(kp_l), jnp.stack(vp_l), jnp.stack(cp_l),
            jnp.stack(ks_l), jnp.stack(vs_l), jnp.stack(cs_l))


_drawn_inputs = setup_inputs


def setup_inputs(seed=0):
    import zlib

    import numpy as np

    out = dict(_drawn_inputs(seed))
    spreads = {}
    factors = {'attn_sinks': 8.0, 'b1': 8.0, 'b2': 8.0, 'final_norm_g': 5.882}
    for name, (base, spread) in spreads.items():
        noise = np.random.default_rng([zlib.crc32(name.encode()), seed]).standard_normal(out[name].shape)
        drawn = base * np.exp(spread * noise) if base else spread * noise
        out[name] = __import__('jax').numpy.asarray(drawn.astype(out[name].dtype))
    for name, factor in factors.items():
        out[name] = (out[name] * factor).astype(out[name].dtype)
    return out
```

```python
from contextlib import ExitStack

import concourse.bass as bass
from concourse import mybir

F32 = mybir.dt.float32
U32 = mybir.dt.uint32
I32 = mybir.dt.int32
ALU = mybir.AluOpType
ACT = mybir.ActivationFunctionType
AX = mybir.AxisListType

P = 128
D = 1024
KD = D // P
NT = 3
TOK = 320
TPAD = NT * P
PROMPT = 256
NB = 8
NS = 8
W = 128
HD = 64
G = 4
CW = 512
CJ = CW // P
TAPS = 31
CTX = TAPS - 1
E = 32
F = 1024
FT = F // P
SLOTS = 64
TOPK = 4
XB = 4
MAXB = 54
TRASH = 2 * TOK
EPS = 1e-5
LIMIT = 7.0
ALPHA = 1.702

C_ID, C_UP, C_ONE, C_ROT, C_IS = 0, 128, 256, 384, 512
C_IM = 640
C_IE = C_IM + MAXB
C_TK = C_IE + E
C_PAD = C_TK + NT
C_S1 = C_PAD + NT
C_S2 = C_S1 + 1
C_SG = C_S2 + 1
C_N = C_SG + G
A_COS, A_SIN = 0, TOK
A_CK = 2 * TOK
A_SK = A_CK + NT * 8
A_MP = A_SK + NT * 8
A_MS = A_MP + 2 * W
A_N = A_MS + 2 * 192

OUTS = 3 + 2 * (1 + NB) + 1 + NB
GROUPS = [(0, 4, 128, 0, 0), (1, 4, 128, 512, 1), (0, 4, 256, 1024, 2), (1, 4, 256, 2048, 4),
          (0, 2, 192, 3072, 6), (1, 2, 192, 3584, 7)]


def tables():
    import numpy as np
    c = np.zeros((P, C_N), np.float32)
    p = np.arange(P)
    c[:, C_ID:C_ID + P] = np.eye(P)
    c[:, C_UP:C_UP + P] = p[:, None] < p[None, :]
    c[:, C_ONE:C_ONE + P] = 1
    for o in (0, HD):
        for i in range(8):
            c[o + 8 + i, C_ROT + o + i] = -1
            c[o + i, C_ROT + o + 8 + i] = 1
    c[:, C_IS:C_IS + P] = p[None, :] % SLOTS
    c[:, C_IM:C_IM + MAXB] = np.arange(MAXB)[None, :]
    c[:, C_IE:C_IE + E] = np.arange(E)[None, :]
    tok = np.arange(NT)[None, :] * P + p[:, None]
    c[:, C_TK:C_TK + NT] = tok + 1
    c[:, C_PAD:C_PAD + NT] = np.where(tok < TOK, 0, -1000)
    half = p // SLOTS
    c[:, C_S1] = TRASH + p - half + 2
    c[:, C_S2] = half - 2
    c[:, C_SG:C_SG + G] = (p[:, None] // NS) % G == np.arange(G)[None, :]
    a = np.zeros((P, A_N), np.float32)
    pos = np.concatenate([np.arange(PROMPT), np.tile(2048 + np.arange(NS), NB)]).astype(np.float32)
    inv = np.power(np.float32(500000.0), -np.arange(8, dtype=np.float32) * np.float32(2.0) / np.float32(16))
    ang = (pos[:, None] * inv[None, :].astype(np.float32)).astype(np.float32)
    cos, sin = np.cos(ang.astype(np.float64)), np.sin(ang.astype(np.float64))
    scale = HD ** -0.5
    a[:, A_COS:A_COS + TOK] = scale
    for o in (0, 8, HD, HD + 8):
        a[o:o + 8, A_COS:A_COS + TOK] = (cos.astype(np.float32) * scale).T
        a[o:o + 8, A_SIN:A_SIN + TOK] = (sin.astype(np.float32) * scale).T
    for t in range(NT):
        n = min(P, TOK - t * P)
        a[:n, A_CK + 8 * t:A_CK + 8 * t + 8] = cos[t * P:t * P + n]
        a[:n, A_SK + 8 * t:A_SK + 8 * t + 8] = sin[t * P:t * P + n]
    no = -1e30
    j = np.arange(W)
    a[:, A_MP:A_MP + W] = np.where(j[None, :] > p[:, None], 0, no)
    a[:, A_MP + W:A_MP + 2 * W] = np.where(j[None, :] <= p[:, None], 0, no)
    b4, t = p // 32, p % 8
    for q in range(2):
        m = a[:, A_MS + 192 * q:A_MS + 192 * q + 192]
        m[:, :W] = np.where(j[None, :] > t[:, None], 0, no)
        n = np.arange(64)
        m[:, W:] = np.where((n[None, :] // 8 == (4 * q + b4)[:, None]) & (n[None, :] % 8 <= t[:, None]), 0, no)
    return c, a


def hybrid_step(nc, x_prompt, x_sample, cache_k, cache_v, state_conv, attn_norm_g, w_in, attn_sinks,
                conv_w, conv_b, conv_ln_g, conv_ln_b, w_out, ffn_norm_g, router_w, router_b,
                w1, b1, w2, b2, final_norm_g, consts, aconsts,
                y_prompt, y_sample, nk_p, nv_p, nc_p, nk_s, nv_s, nc_s, h_dram, acc_dram):
    with ExitStack() as ctx:
        def sb(name, shape, dt=F32):
            return ctx.enter_context(nc.sbuf_tensor(name, shape, dt))

        def sem(name):
            return ctx.enter_context(nc.semaphore(name))

        def bc(ap, n):
            return ap.unsqueeze(len(ap.shape)).to_broadcast([*ap.shape, n])

        WA = sb("WA", [P, 16384])
        WB = sb("WB", [P, 16384])
        W2 = sb("W2", [P, 8192])
        w1buf = [WA[:, :].rearrange("p (c k n) -> p c k n", c=4, k=4),
                 WB[:, :].rearrange("p (c k n) -> p c k n", c=4, k=4)]
        w2buf = W2[:, :].rearrange("p (k n) -> p k n", k=KD)
        win = WB[:, 0:KD * 1792].rearrange("p (k n) -> p k n", k=KD)
        ck_rows = WB[:, 14336:15360].rearrange("p (b n) -> p b n", b=NB)
        cv_rows = WB[:, 15360:16384].rearrange("p (b n) -> p b n", b=NB)
        wout = w2buf
        aP = W2[:, 0:4 * 286].rearrange("p (j t) -> p j t", j=CJ)
        aS = W2[:, 1144:1144 + 4 * 304].rearrange("p (j b t) -> p j b t", j=CJ, b=NB)
        c2 = WA[:, 8192:12288]
        c3 = WA[:, 12288:16384]
        xn = c2[:, 0:3072].rearrange("p (i n) -> p i n", i=NT)
        qT = c2[:, 0:1024].rearrange("p (g t) -> p g t", g=G)
        qS = c2[:, 1024:1280].rearrange("p (b g t) -> p b g t", b=NB, g=G)
        yc = c2[:, 1280:2560].rearrange("p (j t) -> p j t", j=CJ)
        kcT = c2[:, 2560:3584].rearrange("p (b n) -> p b n", b=NB)
        kT = c2[:, 3584:3968]
        st_rows = c3[0:120, 2048:3072].rearrange("p (q n) -> p q n", q=2)
        cw_rows = c3[0:TAPS, 3072:3584]
        par_rows = c3[0:28, 3584:3712]
        q_sb = c3[:, 0:1280].rearrange("p (g t) -> p g t", g=G)
        rq_sb = c3[:, 1280:2560].rearrange("p (g t) -> p g t", g=G)
        krt = c3[:, 2560:2560 + 192].rearrange("p (n i h d) -> p n i h d", n=4, i=NT, h=2)
        a_new = c3[:, 2752:3008].rearrange("p (j n) -> p j n", j=CJ)
        SALL = c3

        C = sb("C", [P, C_N])
        ident = C[:, C_ID:C_ID + P]
        ones = C[:, C_ONE:C_ONE + P]
        X = sb("X", [P, NT, D])
        XT = sb("XT", [P, KD, TPAD])
        mixT = XT
        M1 = sb("M1", [P, 2752])
        A = M1[:, 0:A_N]
        kv = M1[:, 1344:2112].rearrange("p (i n) -> p i n", i=NT)
        sg = M1[:, 2112:2752].rearrange("p (j t) -> p j t", j=2)
        H = [M1[:, 0:1024], M1[:, 1024:2048]]
        hTr = sb("hTr", [P, KD, P])
        ct_out = hTr[:, :, :].rearrange("p k t -> p (k t)")
        junk2 = M1[:, 2112:2752].bitcast(mybir.dt.bfloat16)[:, 0:D]
        par = sb("par", [P, 28])
        cwT = sb("cwT", [P, CJ, TAPS])
        b1q = sb("b1q", [P, 512])
        rw = sb("rw", [P, KD, E])
        rb = sb("rb", [P, E])
        sinks = sb("sinks", [P, 6, 4])
        GT = M1[0:E, 2112:2112 + TPAD]
        small = sb("small", [P, 160])
        ssq, var, std, rstd = (small[:, 3 * n:3 * n + 3] for n in range(4))
        sinks8 = small[:, 136:144]
        picked = small[:, 144:152].rearrange("p (h g) -> p h g", h=2)
        mx, nm, sd, rs, den = (small[:, 16 + 24 * n:40 + 24 * n].rearrange("p (g r) -> p g r", g=6) for n in range(5))
        cnt_i = sb("cnt_i", [1, 2 * E + 1], I32)
        gtab = sb("gtab", [SLOTS, MAXB], U32)
        stab = sb("stab", [P, MAXB], U32)
        wtab = sb("wtab", [P, MAXB])
        gcol = sb("gcol", [SLOTS, 1], U32)
        scol = sb("scol", [P, 1], U32)
        XTf = XT[:, :, :].rearrange("p k t -> p (k t)")
        Xf = X[:, :, :].rearrange("p i n -> p (i n)")
        lg = XTf[:, 0:96].rearrange("p (i e) -> p i e", i=NT)
        v8 = XTf[:, 96:120].rearrange("p (i k) -> p i k", i=NT)
        i8 = sb("i8", [P, NT, 8], U32)
        idf = XTf[:, 120:132].rearrange("p (i k) -> p i k", i=NT)
        ge = XTf[:, 132:144].rearrange("p (i k) -> p i k", i=NT)
        gs = XTf[:, 144:147]
        mk = XTf[:, 148:160].rearrange("p (k i) -> p k i", k=TOPK)
        sk = XTf[:, 160:172].rearrange("p (k i) -> p k i", k=TOPK)
        oh = XTf[:, 192:576].rearrange("p (k i e) -> p k i e", k=TOPK, i=NT)
        tmp4 = XTf[:, 576:960].rearrange("p (k i e) -> p k i e", k=TOPK, i=NT)
        Mm = XTf[:, 960:1056].rearrange("p (i e) -> p i e", i=NT)
        Gg = XTf[:, 1056:1152].rearrange("p (i e) -> p i e", i=NT)
        rk = XTf[:, 1152:1248].rearrange("p (i e) -> p i e", i=NT)
        fl = XTf[:, 1248:1344].rearrange("p (i e) -> p i e", i=NT)
        bk = XTf[:, 1344:1440].rearrange("p (i e) -> p i e", i=NT)
        nb, inc, first, zero, cn = (XTf[:, 1440 + 32 * n:1472 + 32 * n] for n in range(5))
        ohm = XTf[:, 1600:1600 + 12 * MAXB].rearrange("p (k i m) -> p k i m", k=TOPK, i=NT)
        rhs = Xf[:, 0:24 * MAXB].rearrange("p (k i v m) -> p k i v m", k=TOPK, i=NT, v=2)
        ohs = Xf[:, 1296:2832].rearrange("p (k i s) -> p k i s", k=TOPK, i=NT)
        t1, inv, t2 = (XTf[:, 2300 + MAXB * n:2300 + MAXB * (n + 1)] for n in range(3))
        xg = Xf[0:SLOTS, 0:1024]
        xTe = Xf[:, 1024:1536]
        gate, lin = Xf[:, 1536:2048], Xf[:, 2048:2560]
        sig = Xf[:, 2560:3072]
        ysb = XTf[:, 0:512]
        swi = XTf[:, 512:1024]
        act_h = XTf[:, 1024:1536]
        hT = XTf[:, 1536:2048].rearrange("p (s h t) -> p s h t", s=4, h=2)
        sel = XTf[:, 2048:2304].rearrange("p (q s) -> p q s", q=4)
        fin = WA[:, 0:3072].rearrange("p (i n) -> p i n", i=NT)
        junk = WA[:, 3072:4096]
        gfin = WA[:, 4096:5120]
        b2_sb = WA[0:E, 5120:6144]

        PS = ctx.enter_context(nc.psum_tensor("PS", [P, 8, 512], F32))
        KVP = PS[:, 0:2, :].rearrange("p b n -> p (b n)")[:, 0:768].rearrange("p (i n) -> p i n", i=NT)

        consts_in, aconsts_in, x_in, rows_in = sem("consts_in"), sem("aconsts_in"), sem("x_in"), sem("rows_in")
        caches_in, late_in = sem("caches_in"), sem("late_in")
        ug_in = [sem("ug_in0"), sem("ug_in1")]
        kv_in, q_in, wout_in = sem("kv_in"), sem("q_in"), sem("wout_in")
        w1_in = [[sem(f"w1_in{u}{c}") for c in range(4)] for u in range(2)]
        w2_in = [sem("w2_in0"), sem("w2_in1")]
        tail_in = sem("tail_in")
        out_done, acc_init, y_out = sem("out_done"), sem("acc_init"), sem("y_out")
        h_out = [sem(f"h_out{i}") for i in range(NT)]
        names = ("pads early_tp par_ok st_ok pad_ok ssq_ok var_ok std_ok xn_ok xt_tp xt_v xt_a ug_done sg_ok a_ok "
                 "conv_ok kv_done kv_ok q_done q_ok rot_done rq_ok qT_ok krot_ok kT_tp kT_ok kc_tp kc_ok s_done s_evac nm_ok "
                 "exp_ok p_ok pt_done pt_ok o_done o_ok ln1 xc_ok sq_ok ln2 lnv_ok lns_ok z_ok mixc_ok "
                 "ct_tp ct_ok op_done x2_ok ssq2_ok var2_ok std2_ok h_ok h_tp hT_ok hT_used lg_done lgs_ok d_ok ge_ok m_ok g_ok rk_done an_ok "
                 "route_ok tab_done tab_ok gt_tp gt_ok vec act pool").split()
        S = {n: sem(n) for n in names}
        xg_ready, pool_step, xtp_ready, xT_ready = sem("xg_ready"), sem("pool_step"), sem("xtp_ready"), sem("xT_ready")
        gate_done, lin_done, g_ready, sig_ready = sem("gate_done"), sem("lin_done"), sem("g_ready"), sem("sig_ready")
        h_ready, htp_ready, hT_ready = sem("h_ready"), sem("htp_ready"), sem("hT_ready")
        sel_ready, yp_ready, y_ready, y_free, added = sem("sel_ready"), sem("yp_ready"), sem("y_ready"), sem("y_free"), sem("added")
        b1_in, vstep, turn, all_added, b2_in = (sem(n) for n in ("b1_in", "vstep", "turn", "all_added", "b2_in"))
        turned = sem("turned")
        fssq, fvar, fstd, b2_done, y_ok = sem("fssq"), sem("fvar"), sem("fstd"), sem("b2_done"), sem("y_ok")

        w1_v = w1.rearrange("l e (k p) n -> p (l e) k n", p=P)
        w2_v = w2.rearrange("l e (k p) n -> p (l e) k n", p=P)
        win_v = w_in[0].rearrange("(k p) n -> p k n", p=P)
        acc_t = acc_dram.rearrange("(i p h) n -> p i (h n)", p=P, h=2)
        nk_sv = nk_s[0].rearrange("b w h d -> b w (h d)")
        nv_sv = nv_s[0].rearrange("b w h d -> b w (h d)")

        def load_w1(eng, u, e, chunks=range(4)):
            for c in chunks:
                k0, n0 = 4 * (c % 2), F * (c // 2)
                src = w1_v[:, e, k0:k0 + 4, n0:n0 + F] if isinstance(e, int) else \
                    w1_v[:, bass.ds(e, 1), k0:k0 + 4, n0:n0 + F].rearrange("p o k n -> p (o k) n")
                eng.dma_start(w1buf[u][:, c], src).then_inc(w1_in[u][c], 16)

        def load_w2(eng, e):
            for c in range(2):
                src = w2_v[:, e, 4 * c:4 * c + 4, :] if isinstance(e, int) else \
                    w2_v[:, bass.ds(e, 1), 4 * c:4 * c + 4, :].rearrange("p o k n -> p (o k) n")
                eng.dma_start(w2buf[:, 4 * c:4 * c + 4, :], src).then_inc(w2_in[c], 16)

        def Hs(i):
            return H[i % 2]

        PT_ORDER = [(0, 0), (1, 0), (2, 0), (2, 1), (3, 0), (3, 1), (4, 0), (5, 0)]
        PT_BANK = [0, 1, 2, 3, 4, 3, 6, 7]
        PT_N = len(PT_ORDER)

        def pt_moves(n):
            g, kb = PT_ORDER[n]
            o, b = GROUPS[g][3], PT_BANK[n]
            if g < 4:
                return [(SALL[:, o + 512 * kb:o + 512 * kb + 512], PS[:, b, :])]
            return [(SALL[:, o:o + 256], PS[:, b, 0:256]), (SALL[0:64, o + 256:o + 512], PS[0:64, b, 256:512])]

        OB = [(1, 3), (4, 5), (0, 2)]
        BB = [(1, 2), (4, 5), (6, 7)]

        block = ctx.enter_context(nc.Block())

        @block.sync
        def _(sp):
            sp.dma_start(X[:, 0:2, :], x_prompt[0].rearrange("(i p) n -> p i n", p=P)).then_inc(x_in, 16)
            sp.dma_start(X[0:64, 2, :], x_sample.rearrange("b t n -> (b t) n")).then_inc(x_in, 16)
            for n in range(2):
                for o in (768, 1280):
                    o += 256 * n
                    sp.dma_start(win[:, :, o:o + 256], win_v[:, :, o:o + 256]).then_inc(ug_in[n], 16)
            sp.dma_start(win[:, :, 512:768], win_v[:, :, 512:768]).then_inc(kv_in, 16)
            sp.dma_start(win[:, :, 0:512], win_v[:, :, 0:512]).then_inc(q_in, 16)
            load_w1(sp, 0, 0, range(2))
            sp.wait_ge(S["q_done"], 4)
            load_w1(sp, 1, 1, range(3))
            sp.wait_ge(S["conv_ok"], CJ)
            sp.wait_ge(S["ct_tp"], 2)
            for h in range(2):
                sp.dma_start(wout[64 * h:64 * h + 64, 0:G, :],
                             w_out[0, 256 * h:256 * h + 256, :].rearrange("(g d) n -> d g n", g=G)).then_inc(wout_in, 16)
            sp.dma_start(wout[:, G:KD, :], w_out[0, 512:1024, :].rearrange("(j p) n -> p j n", p=P)).then_inc(wout_in, 16)
            sp.wait_ge(S["o_done"], 6)
            sp.wait_ge(S["mixc_ok"], CJ)
            load_w1(sp, 0, 0, range(2, 4))
            load_w1(sp, 1, 1, range(3, 4))
            sp.wait_ge(S["op_done"], NT)
            load_w2(sp, 0)
            sp.wait_ge(S["tab_ok"], 6)
            with sp.Fori(0, E // 2 - 1) as i:
                for u in range(2):
                    end = sp.value_load(cnt_i[0:1, bass.ds(2 * i + (E + u + 1), 1)], min_val=1, max_val=MAXB - 2)
                    sp.wait_ge(lin_done, end)
                    load_w1(sp, u, 2 * i + u + 2)
                    sp.wait_ge(yp_ready, end)
                    load_w2(sp, 2 * i + u + 1)
            end = sp.value_load(cnt_i[0:1, 2 * E - 1:2 * E], min_val=1, max_val=MAXB - 2)
            sp.wait_ge(lin_done, end)
            sp.wait_ge(yp_ready, end)
            load_w2(sp, E - 1)
            sp.dma_start(gfin, final_norm_g.partition_broadcast(P)).then_inc(tail_in, 16)
            sp.dma_start(b2_sb, b2[0]).then_inc(b2_in, 16)
            sp.wait_ge(all_added, 1)
            sp.dma_start(fin, acc_t).then_inc(tail_in, 16)
            for i in range(NT):
                sp.wait_ge(y_ok, i + 1)
                if i < 2:
                    sp.dma_start(y_prompt[0, P * i:P * i + P, :], fin[:, i, :]).then_inc(y_out, 16)
                else:
                    sp.dma_start(y_sample.rearrange("b t n -> (b t) n"), fin[0:64, i, :]).then_inc(y_out, 16)
            sp.wait_ge(y_out, 16 * NT)

        @block.scalar
        def _(act):
            step = [0]

            def own(ins):
                step[0] += 1
                ins.then_inc(S["act"], 1)
                act.wait_ge(S["act"], step[0])

            act.dma_start(C[:, :], consts).then_inc(consts_in, 16)
            rows = [(par_rows[0:8, :], attn_norm_g[0].rearrange("(k p) -> k p", p=P)),
                    (par_rows[8:16, :], ffn_norm_g[0].rearrange("(k p) -> k p", p=P)),
                    (par_rows[16:20, :], conv_b[0].rearrange("(k p) -> k p", p=P)),
                    (par_rows[20:24, :], conv_ln_g[0].rearrange("(k p) -> k p", p=P)),
                    (par_rows[24:28, :], conv_ln_b[0].rearrange("(k p) -> k p", p=P)),
                    (cw_rows, conv_w[0]),
                    (st_rows, state_conv[0].rearrange("b t n -> (b t) n").rearrange("(q p) n -> p q n", q=2))]
            for dst, src in rows:
                act.dma_start(dst, src).then_inc(rows_in, 16)
            act.dma_start(A, aconsts).then_inc(aconsts_in, 16)
            act.dma_start(ck_rows, cache_k[0].rearrange("b w h d -> w b (h d)")).then_inc(caches_in, 16)
            act.dma_start(cv_rows, cache_v[0].rearrange("b w h d -> w b (h d)")).then_inc(caches_in, 16)
            act.dma_start(sinks8, attn_sinks[0].partition_broadcast(P)).then_inc(caches_in, 16)
            act.dma_start(rw[:, :, :], router_w[0].rearrange("(k p) e -> p k e", p=P)).then_inc(late_in, 16)
            act.dma_start(rb[:, :], router_b[0].partition_broadcast(P)).then_inc(late_in, 16)
            act.dma_start(b1q[:, :], b1[0].rearrange("e (q n) -> (e q) n", n=512)).then_inc(b1_in, 16)

            for i in range(NT):
                if i == 0:
                    act.wait_ge(x_in, 32)
                if i == 2:
                    act.wait_ge(S["pads"], 1)
                act.activation(XTf[:, 0:1024], X[:, i, :], ACT.Square, accum_out=ssq[:, i:i + 1]).then_inc(S["ssq_ok"], 1)
                act.wait_ge(S["ssq_ok"], i + 1)
            act.wait_ge(S["var_ok"], 1)
            act.activation(std, var, ACT.Sqrt).then_inc(S["std_ok"], 1)
            act.wait_ge(S["early_tp"], 1)
            act.copy(par[:, :], PS[:, 7, 0:28]).then_inc(S["par_ok"], 1)
            act.copy(cwT[:, :, :], PS[:, 7, 32:32 + CJ * TAPS].rearrange("p (j t) -> p j t", j=CJ)).then_inc(S["par_ok"], 1)
            for j in range(CJ):
                act.copy(aS[:, j, :, 0:CTX],
                         PS[:, 5 + j // 2, 256 * (j % 2):256 * (j % 2) + 240].rearrange("p (b t) -> p b t", b=NB))\
                    .then_inc(S["st_ok"], 1)
            act.wait_ge(S["par_ok"], 2)
            for k in range(1, KD, 2):
                act.wait_ge(S["xt_tp"], k + 1)
                act.activation(XT[:, k, :], PS[:, k, 0:TPAD], ACT.Copy, scale=par[:, k:k + 1]).then_inc(S["xt_a"], 1)
            for j in range(CJ):
                act.wait_ge(S["ug_done"], j + 1)
                if j >= 2:
                    act.wait_ge(S["a_ok"], j - 1)
                act.activation(sg[:, j % 2, :], PS[:, 2 * j + 1, 0:TOK], ACT.Sigmoid).then_inc(S["sg_ok"], 1)
            act.wait_ge(S["kv_done"], 1)
            act.copy(kv[:, :, :], KVP).then_inc(S["kv_ok"], 1)
            for g in range(G):
                act.wait_ge(S["q_done"], g + 1)
                act.copy(q_sb[:, g, :], PS[:, 2 + g, 0:TOK]).then_inc(S["q_ok"], 1)
            act.wait_ge(S["kc_tp"], 1)
            act.copy(kcT[:, :, :], PS[:, 0:2, :].rearrange("p b n -> p (b n)").rearrange("p (b n) -> p b n", b=NB))\
                .then_inc(S["kc_ok"], 1)
            for g in range(G):
                act.wait_ge(S["rot_done"], g + 1)
                act.copy(rq_sb[:, g, :], PS[:, 2 + g, 0:TOK]).then_inc(S["rq_ok"], 1)
            act.wait_ge(S["kT_tp"], 1)
            act.copy(kT, PS[:, 6, 0:TPAD]).then_inc(S["kT_ok"], 1)
            for g, (h, R, K, o, _) in enumerate(GROUPS):
                act.wait_ge(S["nm_ok"], g + 1)
                for r in range(R):
                    s = SALL[:, o + K * r:o + K * r + K]
                    act.activation(s, s, ACT.Exp, bias=nm[:, g, r:r + 1], accum_out=rs[:, g, r:r + 1])
                act.activation(sd[:, g, 0:R], sd[:, g, 0:R], ACT.Exp).then_inc(S["exp_ok"], 1)
            for j in range(CJ):
                act.wait_ge(S["xc_ok"], j + 1)
                if j >= 2:
                    act.wait_ge(S["ln2"], j - 1)
                act.activation(sg[:, j % 2, :], yc[:, j, :], ACT.Square).then_inc(S["sq_ok"], 1)
            act.wait_ge(S["lnv_ok"], 1)
            act.activation(sg[:, 0, :], sg[:, 0, :], ACT.Sqrt).then_inc(S["lns_ok"], 1)
            for j in range(CJ):
                act.wait_ge(S["z_ok"], j + 1)
                act.activation(mixT[:, G + j, 0:TOK], yc[:, j, :], ACT.Silu, scale=par[:, 20 + j:21 + j],
                               bias=par[:, 24 + j:25 + j]).then_inc(S["mixc_ok"], 1)
            for n in range(PT_N):
                act.wait_ge(S["pt_done"], n + 2 if n in (2, 4) else n + 1)
                for dst, src in pt_moves(n):
                    last = act.copy(dst, src)
                last.then_inc(S["pt_ok"], 1)
            for i in range(NT):
                act.wait_ge(S["x2_ok"], 2 * i + 2)
                act.activation(junk2, X[:, i, :], ACT.Square, accum_out=ssq[:, i:i + 1]).then_inc(S["ssq2_ok"], 1)
                act.wait_ge(S["var2_ok"], i + 1)
                act.activation(std[:, i:i + 1], var[:, i:i + 1], ACT.Sqrt).then_inc(S["std2_ok"], 1)
            act.wait_ge(S["d_ok"], 1)
            act.activation(ge, ge, ACT.Exp).then_inc(S["ge_ok"], 1)
            act.wait_ge(S["gt_tp"], 1)
            act.copy(GT[:, :], PS[0:E, 5, 0:TPAD]).then_inc(S["gt_ok"], 1)

            act.wait_ge(S["tab_ok"], 6)
            total = act.value_load(cnt_i[0:1, 2 * E:2 * E + 1], min_val=E, max_val=MAXB - 2)
            with act.Fori(0, total) as m:
                act.wait_ge(g_ready, m + 1)
                act.activation(sig, gate, ACT.Sigmoid, scale=ALPHA).then_inc(sig_ready, 1)
                for c in range(2):
                    act.wait_ge(htp_ready, 2 * m + c + 1)
                    act.copy(hT[:, 2 * c:2 * c + 2], PS[:, 4 + c, 0:256].rearrange("p (s h t) -> p s h t", s=2, h=2))\
                        .then_inc(hT_ready, 1)
                act.wait_ge(y_free, m + 1)
                act.wait_ge(yp_ready, m + 1)
                act.activation(ysb, PS[:, 3, :], ACT.Copy, scale=wtab[:, bass.ds(m, 1)]).then_inc(y_ready, 1)

            for i in range(NT):
                act.wait_ge(fssq, 2 * i + 2)
                act.activation(junk, fin[:, i, :], ACT.Square, accum_out=ssq[:, i:i + 1]).then_inc(fvar, 1)
                act.wait_ge(fvar, 2 * i + 2)
                act.activation(std[:, i:i + 1], var[:, i:i + 1], ACT.Sqrt).then_inc(fstd, 1)

        @block.tensor
        def _(pe):
            mm = nc.tensor.matmul
            tp = nc.tensor.transpose

            def router(i):
                pe.wait_ge(S["h_ok"], i + 1)
                if i == 1:
                    pe.wait_ge(S["x2_ok"], 2)
                pair = [6, 7]
                if i:
                    pe.wait_ge(S["hT_ok"], i)
                for k in range(KD):
                    last = nc.tensor.transpose(PS[:, pair[k // 4], P * (k % 4):P * (k % 4) + P], Hs(i)[:, P * k:P * k + P], ident)
                last.then_inc(S["h_tp"], 1)
                pe.wait_ge(S["hT_ok"], i + 1)
                if i == 0:
                    pe.wait_ge(late_in, 32)
                    pe.wait_ge(S["x2_ok"], 2)
                for k in range(KD):
                    last = nc.tensor.matmul(PS[:, 1, E * i:E * i + E], hTr[:, k, :], rw[:, k, :], start=(k == 0), stop=(k == KD - 1))
                last.then_inc(S["lg_done"], 1)

            def turn_x():
                for k in range(KD):
                    last = tp(PS[:, 0, SLOTS * k:SLOTS * k + SLOTS], xg[:, P * k:P * k + P], ident[0:SLOTS, 0:SLOTS])
                last.then_inc(xtp_ready, 1)

            pe.wait_ge(consts_in, 16)
            pe.wait_ge(rows_in, 16 * 7)
            tp(PS[:, 7, 0:28], par_rows, ident[0:28, 0:28])
            for j in range(CJ):
                tp(PS[:, 7, 32 + TAPS * j:32 + TAPS * (j + 1)], cw_rows[:, P * j:P * j + P], ident[0:TAPS, 0:TAPS])
            for j in range(CJ):
                for q in range(2):
                    o = 256 * (j % 2) + 120 * q
                    last = tp(PS[:, 5 + j // 2, o:o + 120], st_rows[:, q, P * j:P * j + P], ident[0:120, 0:120])
            last.then_inc(S["early_tp"], 1)
            pe.wait_ge(S["xn_ok"], NT)
            for k in range(KD):
                if k == 4:
                    pe.wait_ge(S["st_ok"], CJ)
                    pe.wait_ge(S["par_ok"], 2)
                for i in range(NT):
                    last = tp(PS[:, k, P * i:P * i + P], xn[:, i, P * k:P * k + P], ident)
                last.then_inc(S["xt_tp"], 1)
            pe.wait_ge(S["xt_v"], KD // 2)
            pe.wait_ge(S["xt_a"], KD // 2)
            for j in range(CJ):
                if j % 2 == 0:
                    pe.wait_ge(ug_in[j // 2], 32)
                for n, o in enumerate((768, 1280)):
                    for k in range(KD):
                        last = mm(PS[:, 2 * j + n, 0:TOK], win[:, k, o + P * j:o + P * j + P], XT[:, k, 0:TOK],
                                  start=(k == 0), stop=(k == KD - 1))
                last.then_inc(S["ug_done"], 1)
            pe.wait_ge(kv_in, 16)
            pe.wait_ge(S["a_ok"], 1)
            for i in range(NT):
                for k in range(KD):
                    last = mm(KVP[:, i, :], XT[:, k, P * i:P * i + P], win[:, k, 512:768], start=(k == 0), stop=(k == KD - 1))
            last.then_inc(S["kv_done"], 1)
            pe.wait_ge(q_in, 16)
            for g in range(G):
                pe.wait_ge(S["a_ok"], (2 + g) // 2 + 1)
                for k in range(KD):
                    for h in range(2):
                        o = 256 * h + 64 * g
                        last = mm(PS[64 * h:64 * h + 64, 2 + g, 0:TOK], win[:, k, o:o + 64], XT[:, k, 0:TOK],
                                  start=(k == 0), stop=(k == KD - 1))
                last.then_inc(S["q_done"], 1)
            pe.wait_ge(caches_in, 16 * 3)
            pe.wait_ge(S["kv_ok"], 1)
            for b in range(NB):
                last = tp(PS[:, b // 4, P * (b % 4):P * (b % 4) + P], ck_rows[:, b, :], ident)
            last.then_inc(S["kc_tp"], 1)
            for g in range(G):
                pe.wait_ge(S["q_ok"], g + 1)
                mm(PS[:, 2 + g, 0:TOK], C[:, C_ROT:C_ROT + P], q_sb[:, g, :], start=True, stop=True).then_inc(S["rot_done"], 1)
            pe.wait_ge(S["krot_ok"], 1)
            pe.wait_ge(S["a_ok"], CJ)
            for i in range(NT):
                last = tp(PS[:, 6, P * i:P * i + P], kv[:, i, 0:P], ident)
            last.then_inc(S["kT_tp"], 1)
            for j in range(CJ):
                last = tp(PS[0:CTX, 7, P * j:P * j + P], aP[:, j, PROMPT:PROMPT + CTX], ident)
            last.then_inc(S["ct_tp"], 1)
            pe.wait_ge(S["ct_ok"], 1)
            pe.wait_ge(S["an_ok"], CJ)
            for j in range(CJ):
                last = tp(PS[0:64, 7, P * j:P * j + P], a_new[:, j, :], ident)
            last.then_inc(S["ct_tp"], 1)
            pe.wait_ge(S["qT_ok"], G)
            pe.wait_ge(S["kT_ok"], 1)
            pe.wait_ge(S["kc_ok"], 1)
            pe.wait_ge(S["rq_ok"], G)
            for n, (h, R, K, o, bank) in enumerate(GROUPS):
                hp = slice(64 * h, 64 * h + 64)
                if n < 4:
                    blk = n // 2
                    out = PS[:, bank:bank + 2, :].rearrange("p b n -> p (b n)") if blk else PS[:, bank, :]
                    for g in range(G):
                        last = mm(out[:, K * g:K * g + K], qT[hp, g, W * blk:W * blk + W], kT[hp, 0:K], start=True, stop=True)
                else:
                    if n == 5:
                        pe.wait_ge(S["ct_ok"], 2)
                    for q in range(2):
                        for b in range(4):
                            mm(PS[32 * b:32 * b + 32, bank, 192 * q:192 * q + W],
                               qS[hp, 4 * q + b].rearrange("p g t -> p (g t)"),
                               kcT[hp, 4 * q + b, :], start=True, stop=True)
                    for q in range(2):
                        last = mm(PS[:, bank, 192 * q + W:192 * q + 192],
                                  qS[hp, 4 * q:4 * q + 4].rearrange("p b g t -> p (b g t)"),
                                  kT[hp, PROMPT:TOK], start=True, stop=True)
                last.then_inc(S["s_done"], 1)
            pe.wait_ge(S["conv_ok"], CJ)
            pe.wait_ge(S["s_evac"], 4)
            for j in range(CJ):
                last = mm(PS[:, 5, 0:TOK], ones, yc[:, j, :], start=(j == 0), stop=(j == CJ - 1))
            last.then_inc(S["ln1"], 1)
            pe.wait_ge(S["xc_ok"], CJ)
            for j in range(CJ):
                pe.wait_ge(S["sq_ok"], j + 1)
                mm(PS[:, 5, 0:TOK], ones, sg[:, j % 2, :], start=(j == 0), stop=(j == CJ - 1)).then_inc(S["ln2"], 1)

            def turn_p(n):
                g, kb = PT_ORDER[n]
                _, R, K, o, _ = GROUPS[g]
                pe.wait_ge(S["p_ok"], g + 1)
                pe.wait_ge(S["s_evac"], g + 1)
                if n == 5:
                    pe.wait_ge(S["pt_ok"], 4)
                b = PT_BANK[n]
                if g < 4:
                    for r in range(R):
                        last = tp(PS[:, b, P * r:P * r + P], SALL[:, o + K * r + P * kb:o + K * r + P * kb + P], ident)
                else:
                    for q in range(2):
                        tp(PS[:, b, P * q:P * q + P], SALL[:, o + K * q:o + K * q + P], ident)
                        last = tp(PS[0:64, b, 256 + P * q:256 + P * q + P], SALL[:, o + K * q + P:o + K * q + 192], ident)
                last.then_inc(S["pt_done"], 1)

            def values(n, bank, first_kb, last_kb):
                g, kb = PT_ORDER[n]
                h, o = GROUPS[g][0], GROUPS[g][3]
                hp = slice(64 * h, 64 * h + 64)
                pe.wait_ge(S["pt_ok"], n + 1)
                return mm(PS[hp, bank, :], kv[:, kb, P + 64 * h:P + 64 * h + 64], SALL[:, o + 512 * kb:o + 512 * kb + 512],
                          start=first_kb, stop=last_kb)

            for n in range(2):
                turn_p(n)
            for n in range(2):
                values(n, 0, True, True).then_inc(S["o_done"], 1)
            for n in range(2, 4):
                turn_p(n)
            for n in range(2, 4):
                last = values(n, 2, n == 2, n == 3)
            last.then_inc(S["o_done"], 1)
            for n in range(4, 6):
                turn_p(n)
            for n in range(4, 6):
                last = values(n, 2, n == 4, n == 5)
            last.then_inc(S["o_done"], 1)
            for n in range(6, 8):
                turn_p(n)
            for n in range(6, 8):
                g, _ = PT_ORDER[n]
                h, o = GROUPS[g][0], GROUPS[g][3]
                hp = slice(64 * h, 64 * h + 64)
                pe.wait_ge(S["pt_ok"], n + 1)
                for q in range(2):
                    mm(PS[hp, 6, P * q:P * q + P], kv[0:64, 2, P + 64 * h:P + 64 * h + 64],
                       SALL[0:64, o + 256 + P * q:o + 256 + P * q + P], start=True, stop=False, skip_group_check=True)
                    for b in range(4):
                        last = mm(PS[hp, 6, P * q + 32 * b:P * q + 32 * b + 32], cv_rows[:, 4 * q + b, 64 * h:64 * h + 64],
                                  SALL[:, o + P * q + 32 * b:o + P * q + 32 * b + 32], start=False, stop=(b == 3),
                                  skip_group_check=True)
                last.then_inc(S["o_done"], 1)
            pe.wait_ge(wout_in, 48)
            pe.wait_ge(S["o_ok"], 4)
            pe.wait_ge(S["mixc_ok"], CJ)
            for i in range(NT):
                for n in range(2):
                    for k in range(KD):
                        last = mm(PS[:, OB[i][n], :], mixT[:, k, P * i:P * i + P], wout[:, k, 512 * n:512 * n + 512],
                                  start=(k == 0), stop=(k == KD - 1))
                last.then_inc(S["op_done"], 1)
                if i >= 1:
                    router(i - 1)
            router(NT - 1)
            pe.wait_ge(S["m_ok"], 1)
            for i in range(NT):
                for j in range(i):
                    mm(PS[:, 0, E * i:E * i + E], ones, Mm[:, j, :], start=(j == 0), stop=False)
                mm(PS[:, 0, E * i:E * i + E], C[:, C_UP:C_UP + P], Mm[:, i, :], start=(i == 0), stop=True)
            for j in range(NT):
                last = mm(PS[:, 0, 96:96 + E], ones, Mm[:, j, :], start=(j == 0), stop=(j == NT - 1))
            last.then_inc(S["rk_done"], 1)
            pe.wait_ge(S["g_ok"], 1)
            for i in range(NT):
                last = tp(PS[0:E, 5, P * i:P * i + P], Gg[:, i, :], ident)
            last.then_inc(S["gt_tp"], 1)
            pe.wait_ge(S["route_ok"], 1)
            for n in range(TOPK * NT):
                k, i = n // NT, n % NT
                last = mm(PS[:, 1, 0:2 * MAXB], ohs[:, k, i, :], rhs[:, k, i, :, :].rearrange("p v m -> p (v m)"),
                          start=(n == 0), stop=(n == TOPK * NT - 1))
            last.then_inc(S["tab_done"], 1)

            pe.wait_ge(S["tab_ok"], 6)
            pe.wait_ge(b1_in, 16)
            pe.wait_ge(xg_ready, 16)
            turn_x()
            with pe.Fori(0, E // 2) as i:
                for u in range(2):
                    nblk = pe.value_load(cnt_i[0:1, bass.ds(2 * i + u, 1)], min_val=1, max_val=XB + 1)
                    at = pe.value_load(cnt_i[0:1, bass.ds(E + 2 * i + u, 1)], min_val=0, max_val=MAXB - 3)
                    with pe.Fori(0, nblk) as b:
                        m = at + b
                        pe.wait_ge(xT_ready, m + 1)
                        pe.wait_ge(xg_ready, 16 * m + 32)
                        pe.sem_inc(turned, 1)
                        turn_x()
                        pe.wait_ge(sel_ready, m + 1)
                        for s, done in ((0, gate_done), (1, lin_done)):
                            for n in range(2):
                                mm(PS[64 * n:64 * n + 64, 1 + s, :], sel[:, 2 * s + n, :], b1q[:, :], start=True, stop=False)
                            for k in range(KD):
                                c = 2 * s + k // 4
                                if k % 4 == 0:
                                    pe.wait_ge(w1_in[u][c], 16 * i + 16)
                                for n in range(2):
                                    last = mm(PS[64 * n:64 * n + 64, 1 + s, :], xTe[:, SLOTS * k:SLOTS * k + SLOTS],
                                              w1buf[u][:, c, k % 4, 512 * n:512 * n + 512], start=False, stop=(k == KD - 1))
                            last.then_inc(done, 1)
                        for c in range(2):
                            pe.wait_ge(h_ready, 2 * m + c + 1)
                            for s in range(2):
                                o = P * (2 * c + s)
                                last = tp(PS[:, 4 + c, P * s:P * s + P], act_h[:, o:o + P], ident)
                            last.then_inc(htp_ready, 1)
                        for c in range(2):
                            pe.wait_ge(w2_in[c], 16 * (2 * i + u) + 16)
                        for s in range(4):
                            if s % 2 == 0:
                                pe.wait_ge(hT_ready, 2 * m + s // 2 + 1)
                            for h in range(2):
                                for n in range(2):
                                    last = mm(PS[64 * n:64 * n + 64, 3, :], hT[:, s, h, :], w2buf[:, 4 * h + s, 512 * n:512 * n + 512],
                                              start=(s == 0 and h == 0), stop=(s == 3 and h == 1))
                        last.then_inc(yp_ready, 1)
            pe.wait_ge(S["gt_ok"], 1)
            pe.wait_ge(b2_in, 16)
            for i in range(NT):
                for n in range(2):
                    last = mm(PS[:, BB[i][n], :], GT[:, P * i:P * i + P], b2_sb[:, 512 * n:512 * n + 512], start=True, stop=True)
                last.then_inc(b2_done, 1)


        @block.vector
        def _(dve):
            v = nc.vector
            step = [0]

            def own(ins):
                step[0] += 1
                ins.then_inc(S["vec"], 1)
                dve.wait_ge(S["vec"], step[0])

            v.memset(X[64:128, 2, :], 0.0).then_inc(S["pads"], 1)
            v.memset(aP[:, :, 0:CTX], 0.0).then_inc(S["pad_ok"], 1)
            dve.wait_ge(S["ssq_ok"], NT)
            v.tensor_scalar(var, ssq, 1.0 / D, EPS, ALU.mult, ALU.add).then_inc(S["var_ok"], 1)
            dve.wait_ge(S["std_ok"], 1)
            own(v.reciprocal(rstd, std))
            dve.wait_ge(x_in, 32)
            for i in range(NT):
                v.tensor_scalar(xn[:, i, :], X[:, i, :], rstd[:, i:i + 1], None, ALU.mult).then_inc(S["xn_ok"], 1)
            dve.wait_ge(S["par_ok"], 2)
            for k in range(0, KD, 2):
                dve.wait_ge(S["xt_tp"], k + 1)
                v.tensor_scalar(XT[:, k, :], PS[:, k, 0:TPAD], par[:, k:k + 1], None, ALU.mult).then_inc(S["xt_v"], 1)
            dve.wait_ge(caches_in, 16 * 3)
            for n in range(4):
                v.tensor_copy(sinks[:, n, :], sinks8[:, 4 * (n % 2):4 * (n % 2) + 4])
            own(v.tensor_tensor(picked, sinks8.rearrange("p (h g) -> p h g", h=2),
                                C[:, C_SG:C_SG + G].unsqueeze(1).to_broadcast([P, 2, G]), ALU.mult))
            for n in range(2):
                last = v.tensor_reduce(sinks[:, 4:6, n], picked, AX.X, ALU.add)
            own(last)
            dve.wait_ge(S["pad_ok"], 1)
            dve.wait_ge(S["st_ok"], CJ)
            ys = yc[:, :, PROMPT:TOK].rearrange("p j (b t) -> p j b t", b=NB)

            def gated(j):
                dve.wait_ge(S["sg_ok"], j + 1)
                v.tensor_tensor(aP[:, j, CTX:CTX + PROMPT], PS[:, 2 * j, 0:PROMPT], sg[:, j % 2, 0:PROMPT], ALU.mult)
                v.tensor_tensor(aS[:, j, :, CTX:CTX + NS], PS[:, 2 * j, PROMPT:TOK].rearrange("p (b t) -> p b t", b=NB),
                                sg[:, j % 2, PROMPT:TOK].rearrange("p (b t) -> p b t", b=NB), ALU.mult).then_inc(S["a_ok"], 1)

            gated(0)
            for j in range(CJ):
                dve.wait_ge(S["a_ok"], j + 1)
                for t in range(TAPS):
                    pin, sin = aP[:, j, t:t + PROMPT], aS[:, j, :, t:t + NS]
                    w = cwT[:, j, t:t + 1]
                    if t == 0:
                        bias = par[:, 16 + j:17 + j]
                        v.tensor_scalar(yc[:, j, 0:PROMPT], pin, w, bias, ALU.mult, ALU.add).then_inc(S["vec"], 1)
                        v.tensor_scalar(ys[:, j], sin, w, bias, ALU.mult, ALU.add).then_inc(S["vec"], 1)
                    else:
                        last = t == TAPS - 1
                        dve.wait_ge(S["vec"], step[0] - 1)
                        v.scalar_tensor_tensor(yc[:, j, 0:PROMPT], pin, w, yc[:, j, 0:PROMPT], ALU.mult, ALU.add)\
                            .then_inc(S["vec"], 1)
                        dve.wait_ge(S["vec"], step[0])
                        v.scalar_tensor_tensor(ys[:, j], sin, w, ys[:, j], ALU.mult, ALU.add)\
                            .then_inc(S["conv_ok"] if last else S["vec"], 1)
                        if last:
                            step[0] -= 1
                    step[0] += 2
                    if t == 5 and j + 1 < CJ:
                        gated(j + 1)
            dve.wait_ge(S["vec"], step[0])
            dve.wait_ge(S["ct_tp"], 1)
            v.tensor_copy(ct_out[0:CTX, 0:512], PS[0:CTX, 7, :]).then_inc(S["ct_ok"], 1)
            dve.wait_ge(S["ct_tp"], 2)
            v.tensor_copy(ct_out[0:64, 512:1024], PS[0:64, 7, :]).then_inc(S["ct_ok"], 1)

            dve.wait_ge(caches_in, 16 * 3)
            dve.wait_ge(aconsts_in, 16)

            for g, (h, R, K, o, bank) in enumerate(GROUPS):
                s = SALL[:, o:o + R * K].rearrange("p (r k) -> p r k", r=R)
                dve.wait_ge(S["s_done"], g + 1)
                if g < 4:
                    src = PS[:, bank:bank + 2, :].rearrange("p b n -> p (b n)")[:, 0:R * K].rearrange("p (r k) -> p r k", r=R)
                    mask = A[:, A_MP + 2 * W - K:A_MP + 2 * W].unsqueeze(1).to_broadcast([P, R, K])
                else:
                    src = PS[:, bank, 0:R * K].rearrange("p (r k) -> p r k", r=R)
                    mask = A[:, A_MS:A_MS + 384].rearrange("p (r k) -> p r k", r=2)
                v.tensor_tensor(s, src, mask, ALU.add).then_inc(S["s_evac"], 1)
                dve.wait_ge(S["s_evac"], g + 1)
                own(v.tensor_reduce(mx[:, g, 0:R], s, AX.X, ALU.max))
                own(v.tensor_tensor(mx[:, g, 0:R], mx[:, g, 0:R], sinks[:, g, 0:R], ALU.max))
                v.tensor_tensor(sd[:, g, 0:R], sinks[:, g, 0:R], mx[:, g, 0:R], ALU.subtract)
                v.tensor_scalar(nm[:, g, 0:R], mx[:, g, 0:R], -1.0, None, ALU.mult).then_inc(S["nm_ok"], 1)
            dve.wait_ge(S["ln1"], 1)
            for j in range(CJ):
                v.scalar_tensor_tensor(yc[:, j, :], PS[:, 5, 0:TOK], -1.0 / CW, yc[:, j, :], ALU.mult, ALU.add)\
                    .then_inc(S["xc_ok"], 1)
            dve.wait_ge(S["ln2"], CJ)
            v.tensor_scalar(sg[:, 0, :], PS[:, 5, 0:TOK], 1.0 / CW, EPS, ALU.mult, ALU.add).then_inc(S["lnv_ok"], 1)
            dve.wait_ge(S["lns_ok"], 1)
            own(v.reciprocal(sg[:, 1, :], sg[:, 0, :]))
            dve.wait_ge(S["xc_ok"], CJ)
            for j in range(CJ):
                v.tensor_tensor(yc[:, j, :], yc[:, j, :], sg[:, 1, :], ALU.mult).then_inc(S["z_ok"], 1)
            for g, (h, R, K, o, bank) in enumerate(GROUPS):
                s = SALL[:, o:o + R * K].rearrange("p (r k) -> p r k", r=R)
                dve.wait_ge(S["exp_ok"], g + 1)
                own(v.tensor_tensor(den[:, g, 0:R], rs[:, g, 0:R], sd[:, g, 0:R], ALU.add))
                own(v.reciprocal(den[:, g, 0:R], den[:, g, 0:R]))
                v.tensor_tensor(s, s, bc(den[:, g, 0:R], K), ALU.mult).then_inc(S["p_ok"], 1)
            for n, bank in enumerate((0, 2)):
                dve.wait_ge(S["o_done"], 2 * n + 2)
                v.tensor_copy(mixT[:, 0:G, W * n:W * n + W], PS[:, bank, :].rearrange("p (g t) -> p g t", g=G)).then_inc(S["o_ok"], 1)
            dve.wait_ge(S["o_done"], 6)
            for q in range(2):
                t0 = PROMPT + 32 * q
                v.tensor_copy(mixT[:, 0:G, t0:t0 + 32].rearrange("p g (b t) -> p b g t", b=4),
                              PS[:, 6, P * q:P * q + P].rearrange("p (b g t) -> p b g t", b=4, g=G)).then_inc(S["o_ok"], 1)
            dve.wait_ge(out_done, 16 * OUTS)

            def finish_rows(i):
                for n in range(2):
                    v.tensor_tensor(X[:, i, 512 * n:512 * n + 512], PS[:, OB[i][n], :], X[:, i, 512 * n:512 * n + 512], ALU.add)\
                        .then_inc(S["x2_ok"], 1)
                dve.wait_ge(S["ssq2_ok"], i + 1)
                v.tensor_scalar(var[:, i:i + 1], ssq[:, i:i + 1], 1.0 / D, EPS, ALU.mult, ALU.add).then_inc(S["var2_ok"], 1)
                dve.wait_ge(S["std2_ok"], i + 1)
                own(v.reciprocal(rstd[:, i:i + 1], std[:, i:i + 1]))
                if i == 2:
                    dve.wait_ge(h_out[0], 16)
                    dve.wait_ge(S["h_tp"], 1)
                v.tensor_scalar(Hs(i), X[:, i, :], rstd[:, i:i + 1], None, ALU.mult).then_inc(S["h_ok"], 1)

            def turn_rows(i):
                dve.wait_ge(S["h_tp"], i + 1)
                if i:
                    dve.wait_ge(S["lg_done"], i)
                v.tensor_tensor(hTr[:, :, :], PS[:, 6:8, :].rearrange("p b (k t) -> p (b k) t", k=4), bc(par[:, 8:16], P), ALU.mult)\
                    .then_inc(S["hT_ok"], 1)

            for i in range(NT):
                dve.wait_ge(S["op_done"], i + 1)
                finish_rows(i)
                turn_rows(i)
            dve.wait_ge(S["lg_done"], NT)
            own(v.tensor_tensor(lg, PS[:, 1, 0:96].rearrange("p (i e) -> p i e", i=NT),
                                rb[:, :].unsqueeze(1).to_broadcast([P, NT, E]), ALU.add))
            for i in range(NT):
                last = v.max(v8[:, i, :], lg[:, i, :])
            own(last)
            for i in range(NT):
                last = v.max_index(i8[:, i, :], v8[:, i, :], lg[:, i, :])
            last.then_inc(S["vec"], 1)
            step[0] += 1
            v.tensor_tensor(ge, v8[:, :, 0:TOPK], v8[:, :, 0:1].to_broadcast([P, NT, TOPK]), ALU.subtract).then_inc(S["d_ok"], 1)
            dve.wait_ge(S["vec"], step[0])
            own(v.tensor_copy(idf, i8[:, :, 0:TOPK]))
            own(v.tensor_tensor(idf, idf, bc(C[:, C_PAD:C_PAD + NT], TOPK), ALU.add))
            for k in range(TOPK):
                last = v.tensor_tensor(oh[:, k], C[:, C_IE:C_IE + E].unsqueeze(1).to_broadcast([P, NT, E]), bc(idf[:, :, k], E),
                                       ALU.is_equal)
            own(last)
            v.tensor_tensor(tmp4[:, 0], oh[:, 0], oh[:, 1], ALU.add)
            own(v.tensor_tensor(tmp4[:, 1], oh[:, 2], oh[:, 3], ALU.add))
            v.tensor_tensor(Mm, tmp4[:, 0], tmp4[:, 1], ALU.add).then_inc(S["m_ok"], 1)
            dve.wait_ge(S["m_ok"], 1)
            dve.wait_ge(S["ge_ok"], 1)
            own(v.tensor_reduce(gs, ge, AX.X, ALU.add))
            own(v.reciprocal(gs, gs))
            own(v.tensor_tensor(ge, ge, bc(gs, TOPK), ALU.mult))
            for k in range(TOPK):
                last = v.tensor_tensor(tmp4[:, k], oh[:, k], bc(ge[:, :, k], E), ALU.mult)
            own(last)
            v.tensor_reduce(Gg, tmp4[:, :, :, :].rearrange("p k i e -> p i e k"), AX.X, ALU.add).then_inc(S["g_ok"], 1)
            dve.wait_ge(S["g_ok"], 1)
            dve.wait_ge(S["rk_done"], 1)
            v.tensor_copy(rk, PS[:, 0, 0:96].rearrange("p (i e) -> p i e", i=NT))
            v.memset(zero, 0.0)
            own(v.tensor_copy(cn, PS[:, 0, 96:96 + E]))
            v.tensor_scalar(fl, rk, float(SLOTS), None, ALU.is_ge)
            own(v.tensor_scalar(nb, cn, float(SLOTS), 1.0, ALU.is_gt, ALU.add))
            for b in range(2, XB + 1):
                v.scalar_tensor_tensor(fl, rk, float(SLOTS * b), fl, ALU.is_ge, ALU.add).then_inc(S["vec"], 1)
                v.scalar_tensor_tensor(nb, cn, float(SLOTS * b), nb, ALU.is_gt, ALU.add).then_inc(S["vec"], 1)
                step[0] += 2
                dve.wait_ge(S["vec"], step[0])
            own(v.tensor_tensor_scan(inc, nb, zero, 0.0, ALU.add, ALU.add))
            own(v.tensor_tensor(first, inc, nb, ALU.subtract))
            v.tensor_copy(cnt_i[0:1, 0:E], nb[0:1, :]).then_inc(S["tab_ok"], 1)
            v.tensor_copy(cnt_i[0:1, E:2 * E], first[0:1, :]).then_inc(S["tab_ok"], 1)
            v.tensor_copy(cnt_i[0:1, 2 * E:2 * E + 1], inc[0:1, E - 1:E]).then_inc(S["tab_ok"], 1)
            v.tensor_tensor(bk, fl, first.unsqueeze(1).to_broadcast([P, NT, E]), ALU.add)
            own(v.scalar_tensor_tensor(rk, fl, -float(SLOTS), rk, ALU.mult, ALU.add))
            for k in range(TOPK):
                last = v.tensor_tensor(tmp4[:, k], oh[:, k], bk, ALU.mult)
            own(last)
            own(v.tensor_reduce(mk, tmp4[:, :, :, :], AX.X, ALU.add))
            for k in range(TOPK):
                last = v.tensor_tensor(tmp4[:, k], oh[:, k], rk, ALU.mult)
            own(last)
            v.tensor_reduce(sk, tmp4[:, :, :, :], AX.X, ALU.add)
            own(v.tensor_tensor(mk, mk, C[:, C_PAD:C_PAD + NT].unsqueeze(1).to_broadcast([P, TOPK, NT]), ALU.add))
            dve.wait_ge(added, 16)
            dve.wait_ge(acc_init, 16 * (NT - 1))
            for k in range(TOPK):
                v.tensor_tensor(ohm[:, k], C[:, C_IM:C_IM + MAXB].unsqueeze(1).to_broadcast([P, NT, MAXB]), bc(mk[:, k, :], MAXB),
                                ALU.is_equal)
                last = v.tensor_tensor(ohs[:, k], C[:, C_IS:C_IS + P].unsqueeze(1).to_broadcast([P, NT, P]), bc(sk[:, k, :], P),
                                       ALU.is_equal)
            own(last)
            for k in range(TOPK):
                v.tensor_tensor(rhs[:, k, :, 0, :], ohm[:, k], bc(C[:, C_TK:C_TK + NT], MAXB), ALU.mult)
                last = v.tensor_tensor(rhs[:, k, :, 1, :], ohm[:, k], bc(ge[:, :, k], MAXB), ALU.mult)
            last.then_inc(S["route_ok"], 1)
            dve.wait_ge(S["tab_done"], 1)
            v.tensor_copy(wtab[:, :], PS[:, 1, MAXB:2 * MAXB]).then_inc(S["tab_ok"], 1)
            own(v.tensor_copy(t1, PS[:, 1, 0:MAXB]))
            v.tensor_scalar(inv, t1, 0.0, C[:, C_S1:C_S1 + 1], ALU.is_equal, ALU.mult)
            v.tensor_scalar(gtab[:, :], t1[0:SLOTS], -1.0, 0.0, ALU.add, ALU.max).then_inc(S["tab_ok"], 1)
            own(v.tensor_scalar(t2, t1, 2.0, C[:, C_S2:C_S2 + 1], ALU.mult, ALU.add))
            v.tensor_tensor(stab[:, :], t2, inv, ALU.add).then_inc(S["tab_ok"], 1)
            dve.wait_ge(S["tab_ok"], 6)

            def gain_x():
                v.tensor_tensor(xTe.rearrange("p (k s) -> p k s", k=KD), PS[:, 0, :].rearrange("p (k s) -> p k s", k=KD),
                                bc(par[:, 8:16], SLOTS), ALU.mult).then_inc(xT_ready, 1)

            dve.wait_ge(xtp_ready, 1)
            gain_x()
            with dve.Fori(0, E) as e:
                nblk = dve.value_load(cnt_i[0:1, bass.ds(e, 1)], min_val=1, max_val=XB + 1)
                at = dve.value_load(cnt_i[0:1, bass.ds(E + e, 1)], min_val=0, max_val=MAXB - 3)
                with dve.Fori(0, nblk) as b:
                    m = at + b
                    v.tensor_copy(sel, bc(C[:, bass.ds(4 * e + C_ID, 4)], SLOTS)).then_inc(sel_ready, 1)
                    dve.wait_ge(gate_done, m + 1)
                    v.tensor_scalar(gate, PS[:, 1, :], LIMIT, None, ALU.min).then_inc(g_ready, 1)
                    dve.wait_ge(sig_ready, m + 1)
                    v.tensor_tensor(swi, gate, sig, ALU.mult).then_inc(vstep, 1)
                    dve.wait_ge(lin_done, m + 1)
                    for c in range(2):
                        o = slice(256 * c, 256 * c + 256)
                        v.tensor_scalar(lin[:, o], PS[:, 2, o], LIMIT, -LIMIT, ALU.min, ALU.max).then_inc(vstep, 1)
                    for c in range(2):
                        o = slice(256 * c, 256 * c + 256)
                        dve.wait_ge(vstep, 3 * m + c + 2)
                        v.scalar_tensor_tensor(act_h[:, o], lin[:, o], 1.0, swi[:, o], ALU.add, ALU.mult).then_inc(h_ready, 1)
                    dve.wait_ge(xtp_ready, m + 2)
                    gain_x()

            dve.wait_ge(tail_in, 32)
            for i in range(NT):
                dve.wait_ge(b2_done, i + 1)
                for n in range(2):
                    f = fin[:, i, 512 * n:512 * n + 512]
                    v.tensor_tensor(f, PS[:, BB[i][n], :], f, ALU.add).then_inc(fssq, 1)
                dve.wait_ge(fvar, 2 * i + 1)
                v.tensor_scalar(var[:, i:i + 1], ssq[:, i:i + 1], 1.0 / D, EPS, ALU.mult, ALU.add).then_inc(fvar, 1)
                dve.wait_ge(fstd, i + 1)
                own(v.reciprocal(rstd[:, i:i + 1], std[:, i:i + 1]))
                v.scalar_tensor_tensor(fin[:, i, :], fin[:, i, :], rstd[:, i:i + 1], gfin, ALU.mult, ALU.mult).then_inc(y_ok, 1)

        @block.gpsimd
        def _(pool):
            g = nc.gpsimd
            for src, dst in ((cache_k, nk_s), (cache_v, nv_s)):
                pool.dma_start(dst[0, :, 0:W - NS].rearrange("b w h d -> b (w h d)"),
                               src[0, :, NS:W].rearrange("b w h d -> b (w h d)")).then_inc(out_done, 16)
            pool.dma_start(nc_s[0, :, 0:CTX - NS, :].rearrange("b t n -> b (t n)"),
                           state_conv[0, :, NS:CTX, :].rearrange("b t n -> b (t n)")).then_inc(out_done, 16)
            pool.wait_ge(aconsts_in, 16)
            pool.wait_ge(S["kv_ok"], 1)
            k4 = kv[:, :, 0:P].rearrange("p i (h d) -> p i h d", h=2)
            x1, x2 = k4[:, :, :, 0:8], k4[:, :, :, 8:16]
            cs, sn = (A[:, o:o + 24].rearrange("p (i d) -> p i d", i=NT).unsqueeze(2).to_broadcast([P, NT, 2, 8]) for o in (A_CK, A_SK))
            for n, (a, c) in enumerate(((x1, cs), (x2, sn), (x2, cs), (x1, sn))):
                g.tensor_tensor(krt[:, n], a, c, ALU.mult).then_inc(S["pool"], 1)
            pool.wait_ge(S["pool"], 4)
            g.tensor_tensor(x1, krt[:, 0], krt[:, 1], ALU.subtract).then_inc(S["pool"], 1)
            pool.wait_ge(S["pool"], 5)
            g.tensor_tensor(x2, krt[:, 2], krt[:, 3], ALU.add).then_inc(S["krot_ok"], 1)
            for n in range(G):
                pool.wait_ge(S["rq_ok"], n + 1)
                g.tensor_tensor(q_sb[:, n, :], q_sb[:, n, :], A[:, A_COS:A_COS + TOK], ALU.mult).then_inc(S["pool"], 1)
                g.tensor_tensor(rq_sb[:, n, :], rq_sb[:, n, :], A[:, A_SIN:A_SIN + TOK], ALU.mult).then_inc(S["pool"], 1)
                pool.wait_ge(S["pool"], 5 + 2 * n + 2)
                g.tensor_tensor(qT[:, n, :], q_sb[:, n, 0:PROMPT], rq_sb[:, n, 0:PROMPT], ALU.add)
                g.tensor_tensor(qS[:, :, n, :], *(x[:, n, PROMPT:TOK].rearrange("p (b t) -> p b t", b=NB) for x in (q_sb, rq_sb)),
                                ALU.add).then_inc(S["qT_ok"], 1)
            for j in range(CJ):
                pool.wait_ge(S["a_ok"], j + 1)
                g.tensor_copy(a_new[:, j, :].rearrange("p (b t) -> p b t", b=NB), aS[:, j, :, CTX:CTX + NS]).then_inc(S["an_ok"], 1)
            pool.wait_ge(S["krot_ok"], 1)
            for n, (dst_p, dst_s) in enumerate(((nk_p, nk_sv), (nv_p, nv_sv))):
                pool.dma_start(dst_p[0, 0].rearrange("w h d -> w (h d)"), kv[:, 1, P * n:P * n + P]).then_inc(out_done, 16)
                for b in range(NB):
                    pool.dma_start(dst_s[b, W - NS:W, :], kv[NS * b:NS * b + NS, 2, P * n:P * n + P]).then_inc(out_done, 16)
            pool.wait_ge(S["ct_ok"], 2)
            pool.dma_start(nc_p[0, 0], ct_out[0:CTX, 0:512]).then_inc(out_done, 16)
            for b in range(NB):
                pool.dma_start(nc_s[0, b, CTX - NS:CTX, :], ct_out[NS * b:NS * b + NS, 512:1024]).then_inc(out_done, 16)
            pool.wait_ge(out_done, 16 * OUTS)
            pool.sem_inc(turn, 1)
            for i in range(NT):
                pool.wait_ge(S["x2_ok"], 2 * i + 2)
                pool.dma_start(acc_t[:, i, :], X[:, i, :]).then_inc(acc_init if i < NT - 1 else added, 16)
                pool.wait_ge(S["h_ok"], i + 1)
                pool.dma_start(h_dram[P * i:P * i + P, :], Hs(i)).then_inc(h_out[i], 16)

            pool.wait_ge(S["tab_ok"], 6)
            for i in range(NT):
                pool.wait_ge(h_out[i], 16)
            pool.wait_ge(acc_init, 16 * (NT - 1))
            total = pool.value_load(cnt_i[0:1, 2 * E:2 * E + 1], min_val=E, max_val=MAXB - 2)
            hmax = pool.to_reg(TPAD - 1)
            amax = pool.to_reg(2 * TPAD - 1)

            def gather(m):
                g.indirect_dma_start(out=xg, out_offset=None, in_=h_dram[:, :],
                                     in_offset=bass.IndirectOffsetOnAxis(ap=gcol[:, 0:1], axis=0),
                                     bounds_check=hmax, oob_is_err=True).then_inc(xg_ready, 16)

            for m in range(2):
                if m:
                    pool.wait_ge(xg_ready, 16)
                    pool.wait_ge(xtp_ready, 1)
                g.tensor_copy(gcol[:, :], gtab[:, m:m + 1]).then_inc(turn, 1)
                pool.wait_ge(turn, m + 2)
                gather(m)
            with pool.Fori(0, total) as m:
                pool.wait_ge(xg_ready, 16 * m + 32)
                pool.wait_ge(xtp_ready, m + 2)
                pool.sem_inc(turn, 1)
                g.tensor_copy(gcol[:, :], gtab[:, bass.ds(m + 2, 1)]).then_inc(turn, 1)
                pool.wait_ge(turn, 3 * m + 5)
                pool.sem_inc(pool_step, 1)
                gather(m + 2)
                pool.wait_ge(added, 16 * m + 16)
                pool.sem_inc(y_free, 1)
                g.tensor_copy(scol[:, :], stab[:, bass.ds(m, 1)]).then_inc(turn, 1)
                pool.wait_ge(turn, 3 * m + 6)
                pool.wait_ge(y_ready, m + 1)
                pool.sem_inc(pool_step, 1)
                g.indirect_dma_start(out=acc_dram[:, :], out_offset=bass.IndirectOffsetOnAxis(ap=scol[:, 0:1], axis=0),
                                     in_=ysb, in_offset=None, bounds_check=amax, oob_is_err=True,
                                     compute_op=ALU.add).then_inc(added, 16)
            pool.wait_ge(added, 16 * total + 16)
            pool.wait_ge(xg_ready, 16 * total + 32)
            pool.sem_inc(all_added, 1)


_INS = ["x_prompt", "x_sample", "cache_k", "cache_v", "state_conv", "attn_norm_g", "w_in", "attn_sinks",
        "conv_w", "conv_b", "conv_ln_g", "conv_ln_b", "w_out", "ffn_norm_g", "router_w", "router_b",
        "w1", "b1", "w2", "b2", "final_norm_g"]
_OUTS = [(1, PROMPT, D), (NB, NS, D), (1, 1, W, 2, HD), (1, 1, W, 2, HD), (1, 1, CTX, CW),
         (1, NB, W, 2, HD), (1, NB, W, 2, HD), (1, NB, CTX, CW)]


def kernel(**inputs):
    import numpy as _np
    import concourse.bacc as _bacc
    from concourse import mybir as _mybir
    from concourse.bass_utils import run_bass_kernel_spmd as _run

    nc = _bacc.Bacc("TRN2", target_bir_lowering=False, num_devices=1)
    arrays, args = {}, []
    consts, aconsts = tables()
    for name, a in [*((n, inputs[n]) for n in _INS), ("consts", consts), ("aconsts", aconsts)]:
        a = _np.ascontiguousarray(a)
        arrays[f"in_{name}_dram"] = a
        args.append(nc.dram_tensor(f"in_{name}_dram", a.shape, _mybir.dt.from_np(a.dtype), kind="ExternalInput").ap())
    for i, shape in enumerate(_OUTS):
        args.append(nc.dram_tensor(f"out_{i}_dram", shape, F32, kind="ExternalOutput").ap())
    args.append(nc.dram_tensor("h_rows", (TPAD, D), F32, kind="Internal").ap())
    args.append(nc.dram_tensor("acc_rows", (2 * TPAD, D // 2), F32, kind="Internal").ap())
    hybrid_step(nc, *args)
    r = _run(nc, [arrays], core_ids=[0])
    return tuple(r.results[0][f"out_{i}_dram"] for i in range(len(_OUTS)))
```

```python
from contextlib import ExitStack

import concourse.bass as bass
from concourse import mybir

F32 = mybir.dt.float32
U32 = mybir.dt.uint32
I32 = mybir.dt.int32
ALU = mybir.AluOpType
ACT = mybir.ActivationFunctionType
AX = mybir.AxisListType

P = 128
D = 1024
KD = D // P
NT = 3
TOK = 320
TPAD = NT * P
PROMPT = 256
NB = 8
NS = 8
W = 128
HD = 64
G = 4
CW = 512
CJ = CW // P
TAPS = 31
CTX = TAPS - 1
TAP3 = 16
E = 32
F = 1024
FT = F // P
SLOTS = 64
TOPK = 4
XB = 4
MAXB = 54
TRASH = 2 * TOK
EPS = 1e-5
LIMIT = 7.0
ALPHA = 1.702

C_ID, C_UP, C_ONE, C_ROT, C_IS = 0, 128, 256, 384, 512
C_IM = 640
C_IE = C_IM + MAXB
C_TK = C_IE + E
C_PAD = C_TK + NT
C_S1 = C_PAD + NT
C_S2 = C_S1 + 1
C_SG = C_S2 + 1
C_N = C_SG + G
A_COS, A_SIN = 0, TOK
A_CK = 2 * TOK
A_SK = A_CK + NT * 8
A_MP = A_SK + NT * 8
A_MS = A_MP + 2 * W
A_N = A_MS + 2 * 192

OUTS = 2 * (1 + NB) + 1 + NB
GROUPS = [(0, 4, 128, 0, 0), (1, 4, 128, 512, 1), (0, 4, 256, 1024, 2), (1, 4, 256, 2048, 4),
          (0, 2, 192, 3072, 6), (1, 2, 192, 3584, 7)]


def tables():
    import numpy as np
    c = np.zeros((P, C_N), np.float32)
    p = np.arange(P)
    c[:, C_ID:C_ID + P] = np.eye(P)
    c[:, C_UP:C_UP + P] = p[:, None] < p[None, :]
    c[:, C_ONE:C_ONE + P] = 1
    for o in (0, HD):
        for i in range(8):
            c[o + 8 + i, C_ROT + o + i] = -1
            c[o + i, C_ROT + o + 8 + i] = 1
    c[:, C_IS:C_IS + P] = p[None, :] % SLOTS
    c[:, C_IM:C_IM + MAXB] = np.arange(MAXB)[None, :]
    c[:, C_IE:C_IE + E] = np.arange(E)[None, :]
    tok = np.arange(NT)[None, :] * P + p[:, None]
    c[:, C_TK:C_TK + NT] = tok + 1
    c[:, C_PAD:C_PAD + NT] = np.where(tok < TOK, 0, -1000)
    half = p // SLOTS
    c[:, C_S1] = TRASH + p - half + 2
    c[:, C_S2] = half - 2
    c[:, C_SG:C_SG + G] = (p[:, None] // NS) % G == np.arange(G)[None, :]
    a = np.zeros((P, A_N), np.float32)
    pos = np.concatenate([np.arange(PROMPT), np.tile(2048 + np.arange(NS), NB)]).astype(np.float32)
    inv = np.power(np.float32(500000.0), -np.arange(8, dtype=np.float32) * np.float32(2.0) / np.float32(16))
    ang = (pos[:, None] * inv[None, :].astype(np.float32)).astype(np.float32)
    cos, sin = np.cos(ang.astype(np.float64)), np.sin(ang.astype(np.float64))
    scale = HD ** -0.5
    a[:, A_COS:A_COS + TOK] = scale
    for o in (0, 8, HD, HD + 8):
        a[o:o + 8, A_COS:A_COS + TOK] = (cos.astype(np.float32) * scale).T
        a[o:o + 8, A_SIN:A_SIN + TOK] = (sin.astype(np.float32) * scale).T
    for t in range(NT):
        n = min(P, TOK - t * P)
        a[:n, A_CK + 8 * t:A_CK + 8 * t + 8] = cos[t * P:t * P + n]
        a[:n, A_SK + 8 * t:A_SK + 8 * t + 8] = sin[t * P:t * P + n]
    no = -1e30
    j = np.arange(W)
    a[:, A_MP:A_MP + W] = np.where(j[None, :] > p[:, None], 0, no)
    a[:, A_MP + W:A_MP + 2 * W] = np.where(j[None, :] <= p[:, None], 0, no)
    b4, t = p // 32, p % 8
    for q in range(2):
        m = a[:, A_MS + 192 * q:A_MS + 192 * q + 192]
        m[:, :W] = np.where(j[None, :] > t[:, None], 0, no)
        n = np.arange(64)
        m[:, W:] = np.where((n[None, :] // 8 == (4 * q + b4)[:, None]) & (n[None, :] % 8 <= t[:, None]), 0, no)
    return c, a


def hybrid_step(nc, x_prompt, x_sample, cache_k, cache_v, state_conv, attn_norm_g, w_in, attn_sinks,
                conv_w, conv_b, conv_ln_g, conv_ln_b, w_out, ffn_norm_g, router_w, router_b,
                w1, b1, w2, b2, final_norm_g, consts, aconsts,
                y_prompt, y_sample, nk_p, nv_p, nc_p, nk_s, nv_s, nc_s, h_dram, acc_dram):
    with ExitStack() as ctx:
        def sb(name, shape, dt=F32):
            return ctx.enter_context(nc.sbuf_tensor(name, shape, dt))

        def sem(name):
            return ctx.enter_context(nc.semaphore(name))

        def bc(ap, n):
            return ap.unsqueeze(len(ap.shape)).to_broadcast([*ap.shape, n])

        WA = sb("WA", [P, 16384])
        WB = sb("WB", [P, 16384])
        W2 = sb("W2", [P, 8192])
        w1buf = [WA[:, :].rearrange("p (c k n) -> p c k n", c=4, k=4),
                 WB[:, :].rearrange("p (c k n) -> p c k n", c=4, k=4)]
        w2buf = W2[:, :].rearrange("p (k n) -> p k n", k=KD)
        win = WB[:, 0:KD * 1792].rearrange("p (k n) -> p k n", k=KD)
        ck_rows = WB[:, 14336:15360].rearrange("p (b n) -> p b n", b=NB)
        cv_rows = WB[:, 15360:16384].rearrange("p (b n) -> p b n", b=NB)
        wout = w2buf
        aP = W2[:, 0:4 * 286].rearrange("p (j t) -> p j t", j=CJ)
        aS = W2[:, 1144:1144 + 4 * 304].rearrange("p (j b t) -> p j b t", j=CJ, b=NB)
        c2 = WA[:, 8192:12288]
        c3 = WA[:, 12288:16384]
        xn = c2[:, 0:3072].rearrange("p (i n) -> p i n", i=NT)
        qT = c2[:, 0:1024].rearrange("p (g t) -> p g t", g=G)
        qS = c2[:, 1024:1280].rearrange("p (b g t) -> p b g t", b=NB, g=G)
        yc = c2[:, 1280:2560].rearrange("p (j t) -> p j t", j=CJ)
        kcT = c2[:, 2560:3584].rearrange("p (b n) -> p b n", b=NB)
        kT = c2[:, 3584:3968]
        st_rows = c3[0:120, 2048:3072].rearrange("p (q n) -> p q n", q=2)
        cw_rows = c3[0:TAPS, 3072:3584]
        par_rows = c3[0:28, 3584:3712]
        q_sb = c3[:, 0:1280].rearrange("p (g t) -> p g t", g=G)
        rq_sb = c3[:, 1280:2560].rearrange("p (g t) -> p g t", g=G)
        krt = c3[:, 2560:2560 + 192].rearrange("p (n i h d) -> p n i h d", n=4, i=NT, h=2)
        a_new = c3[:, 2752:3008].rearrange("p (j n) -> p j n", j=CJ)
        SALL = c3

        C = sb("C", [P, C_N])
        ident = C[:, C_ID:C_ID + P]
        ones = C[:, C_ONE:C_ONE + P]
        X = sb("X", [P, NT, D])
        XT = sb("XT", [P, KD, TPAD])
        mixT = XT
        M1 = sb("M1", [P, 2752])
        A = M1[:, 0:A_N]
        kv = M1[:, 1344:2112].rearrange("p (i n) -> p i n", i=NT)
        sg = M1[:, 2112:2752].rearrange("p (j t) -> p j t", j=2)
        part3 = sg[:, 0, :]
        H = [M1[:, 0:1024], M1[:, 1024:2048]]
        hTr = sb("hTr", [P, KD, P])
        ct_out = hTr[:, :, :].rearrange("p k t -> p (k t)")
        junk2 = M1[:, 2112:2752].bitcast(mybir.dt.bfloat16)[:, 0:D]
        prod = hTr[:, :, :].rearrange("p k t -> p (k t)")[:, 0:3 * TOK].rearrange("p (r t) -> p r t", r=3)
        par = sb("par", [P, 28])
        cwT = sb("cwT", [P, CJ, TAPS])
        b1q = sb("b1q", [P, 512])
        rw = sb("rw", [P, KD, E])
        rb = sb("rb", [P, E])
        sinks = sb("sinks", [P, 6, 4])
        GT = M1[0:E, 2112:2112 + TPAD]
        small = sb("small", [P, 160])
        ssq, var, std, rstd = (small[:, 3 * n:3 * n + 3] for n in range(4))
        sinks8 = small[:, 136:144]
        picked = small[:, 144:152].rearrange("p (h g) -> p h g", h=2)
        mx, nm, sd, rs, den = (small[:, 16 + 24 * n:40 + 24 * n].rearrange("p (g r) -> p g r", g=6) for n in range(5))
        cnt_i = sb("cnt_i", [1, 2 * E + 1], I32)
        gtab = sb("gtab", [SLOTS, MAXB], U32)
        stab = sb("stab", [P, MAXB], U32)
        wtab = sb("wtab", [P, MAXB])
        gcol = sb("gcol", [SLOTS, 1], U32)
        scol = sb("scol", [P, 1], U32)
        XTf = XT[:, :, :].rearrange("p k t -> p (k t)")
        Xf = X[:, :, :].rearrange("p i n -> p (i n)")
        lg = XTf[:, 0:96].rearrange("p (i e) -> p i e", i=NT)
        v8 = XTf[:, 96:120].rearrange("p (i k) -> p i k", i=NT)
        i8 = sb("i8", [P, NT, 8], U32)
        idf = XTf[:, 120:132].rearrange("p (i k) -> p i k", i=NT)
        ge = XTf[:, 132:144].rearrange("p (i k) -> p i k", i=NT)
        gs = XTf[:, 144:147]
        mk = XTf[:, 148:160].rearrange("p (k i) -> p k i", k=TOPK)
        sk = XTf[:, 160:172].rearrange("p (k i) -> p k i", k=TOPK)
        oh = XTf[:, 192:576].rearrange("p (k i e) -> p k i e", k=TOPK, i=NT)
        tmp4 = XTf[:, 576:960].rearrange("p (k i e) -> p k i e", k=TOPK, i=NT)
        Mm = XTf[:, 960:1056].rearrange("p (i e) -> p i e", i=NT)
        Gg = XTf[:, 1056:1152].rearrange("p (i e) -> p i e", i=NT)
        rk = XTf[:, 1152:1248].rearrange("p (i e) -> p i e", i=NT)
        fl = XTf[:, 1248:1344].rearrange("p (i e) -> p i e", i=NT)
        bk = XTf[:, 1344:1440].rearrange("p (i e) -> p i e", i=NT)
        cum = XTf[:, 2600:2600 + (NT + 1) * E].rearrange("p (i e) -> p i e", i=NT + 1)
        nb, inc, first, zero, cn = (XTf[:, 1440 + 32 * n:1472 + 32 * n] for n in range(5))
        ohm = XTf[:, 1600:1600 + 12 * MAXB].rearrange("p (k i m) -> p k i m", k=TOPK, i=NT)
        rhs = Xf[:, 0:24 * MAXB].rearrange("p (k i v m) -> p k i v m", k=TOPK, i=NT, v=2)
        ohs = Xf[:, 1296:2832].rearrange("p (k i s) -> p k i s", k=TOPK, i=NT)
        t1, inv, t2 = (XTf[:, 2300 + MAXB * n:2300 + MAXB * (n + 1)] for n in range(3))
        xg = Xf[0:SLOTS, 0:1024]
        xTe = Xf[:, 1024:1536]
        gate, lin = Xf[:, 1536:2048], Xf[:, 2048:2560]
        sig = Xf[:, 2560:3072]
        ysb = XTf[:, 0:512]
        swi = XTf[:, 512:1024]
        act_h = XTf[:, 1024:1536]
        hT = XTf[:, 1536:2048].rearrange("p (s h t) -> p s h t", s=4, h=2)
        sel = XTf[:, 2048:2304].rearrange("p (q s) -> p q s", q=4)
        fin = WA[:, 0:3072].rearrange("p (i n) -> p i n", i=NT)
        junk = WA[:, 6144:9216].rearrange("p (i n) -> p i n", i=NT)
        gfin = WA[:, 4096:5120]
        b2_sb = WA[0:E, 5120:6144]

        PS = ctx.enter_context(nc.psum_tensor("PS", [P, 8, 512], F32))
        KVP = PS[:, 0:2, :].rearrange("p b n -> p (b n)")[:, 0:768].rearrange("p (i n) -> p i n", i=NT)

        consts_in, aconsts_in, x_in, rows_in = sem("consts_in"), sem("aconsts_in"), sem("x_in"), sem("rows_in")
        caches_in, late_in = sem("caches_in"), sem("late_in")
        ug_in = [sem("ug_in0"), sem("ug_in1")]
        kv_in, q_in, wout_in = sem("kv_in"), sem("q_in"), sem("wout_in")
        w1_in = [[sem(f"w1_in{u}{c}") for c in range(4)] for u in range(2)]
        w2_in = [sem("w2_in0"), sem("w2_in1")]
        tail_in = sem("tail_in")
        fin_in = [sem(f"fin_in{i}") for i in range(NT)]
        out_done, new_out, acc_init, y_out = sem("out_done"), sem("new_out"), sem("acc_init"), sem("y_out")
        h_out = [sem(f"h_out{i}") for i in range(NT)]
        names = ("pads early_tp par_ok st_ok pad_ok ssq_ok var_ok std_ok xn_ok xt_tp xt_v xt_a ug_done sg_ok a_ok "
                 "conv_prod conv_add part_ok conv_ok kv_done kv_ok q_done q_ok rot_done rq_ok qT_ok krot_ok kT_tp kT_ok kc_tp kc_ok s_done s_evac nm_ok "
                 "exp_ok p_ok pt_done pt_ok pt_ok2 o_done o_ok ln1 xc_ok sq_ok ln2 lnv_ok lns_ok z_ok mixc_ok "
                 "ct_tp ct_ok op_done x2_ok ssq2_ok var2_ok std2_ok h_ok h_tp hT_ok hT_used lg_done lgs_ok d_ok ge_ok m_ok g_ok rk_done an_ok "
                 "route_ok tab_done tab_ok gt_tp gt_ok vec act pool").split()
        S = {n: sem(n) for n in names}
        xg_ready, pool_step, xtp_ready, xT_ready = sem("xg_ready"), sem("pool_step"), sem("xtp_ready"), sem("xT_ready")
        gate_done, lin_done, g_ready, sig_ready = sem("gate_done"), sem("lin_done"), sem("g_ready"), sem("sig_ready")
        h_ready, htp_ready, hT_ready = sem("h_ready"), sem("htp_ready"), sem("hT_ready")
        sel_ready, yp_ready, y_ready, y_free, added = sem("sel_ready"), sem("yp_ready"), sem("y_ready"), sem("y_free"), sem("added")
        b1_in, vstep, turn, all_added, b2_in = (sem(n) for n in ("b1_in", "vstep", "turn", "all_added", "b2_in"))
        turned = sem("turned")
        fsum, fssq, fvar, fstd, b2_done, y_ok = sem("fsum"), sem("fssq"), sem("fvar"), sem("fstd"), sem("b2_done"), sem("y_ok")

        w1_v = w1.rearrange("l e (k p) n -> p (l e) k n", p=P)
        w2_v = w2.rearrange("l e (k p) n -> p (l e) k n", p=P)
        win_v = w_in[0].rearrange("(k p) n -> p k n", p=P)
        acc_t = acc_dram.rearrange("(i p h) n -> p i (h n)", p=P, h=2)
        nk_sv = nk_s[0].rearrange("b w h d -> b w (h d)")
        nv_sv = nv_s[0].rearrange("b w h d -> b w (h d)")

        def load_w1(eng, u, e, chunks=range(4)):
            for c in chunks:
                k0, n0 = 4 * (c % 2), F * (c // 2)
                src = w1_v[:, e, k0:k0 + 4, n0:n0 + F] if isinstance(e, int) else \
                    w1_v[:, bass.ds(e, 1), k0:k0 + 4, n0:n0 + F].rearrange("p o k n -> p (o k) n")
                eng.dma_start(w1buf[u][:, c], src).then_inc(w1_in[u][c], 16)

        def load_w2(eng, e):
            for c in range(2):
                src = w2_v[:, e, 4 * c:4 * c + 4, :] if isinstance(e, int) else \
                    w2_v[:, bass.ds(e, 1), 4 * c:4 * c + 4, :].rearrange("p o k n -> p (o k) n")
                eng.dma_start(w2buf[:, 4 * c:4 * c + 4, :], src).then_inc(w2_in[c], 16)

        rows = [(par_rows[0:8, :], attn_norm_g[0].rearrange("(k p) -> k p", p=P)),
                (par_rows[8:16, :], ffn_norm_g[0].rearrange("(k p) -> k p", p=P)),
                (par_rows[16:20, :], conv_b[0].rearrange("(k p) -> k p", p=P)),
                (par_rows[20:24, :], conv_ln_g[0].rearrange("(k p) -> k p", p=P)),
                (par_rows[24:28, :], conv_ln_b[0].rearrange("(k p) -> k p", p=P)),
                (cw_rows, conv_w[0]),
                (st_rows, state_conv[0].rearrange("b t n -> (b t) n").rearrange("(q p) n -> p q n", q=2))]

        def Hs(i):
            return H[i % 2]

        PT_ORDER = [(0, 0), (1, 0), (2, 0), (2, 1), (3, 0), (3, 1), (4, 0), (5, 0)]
        PT_BANK = [0, 1, 6, 7, 6, 7, 6, 7]
        PT_N = len(PT_ORDER)

        def pt_moves(n):
            g, kb = PT_ORDER[n]
            o, b = GROUPS[g][3], PT_BANK[n]
            if g < 4:
                return [(SALL[:, o + 512 * kb:o + 512 * kb + 512], PS[:, b, :])]
            return [(SALL[:, o:o + 256], PS[:, b, 0:256]), (SALL[0:64, o + 256:o + 512], PS[0:64, b, 256:512])]

        def turned_p(eng, copy, n):
            eng.wait_ge(S["pt_done"], n + 2 if n in (2, 4) else n + 1)
            for dst, src in pt_moves(n):
                last = copy(dst, src)
            return last

        OB = [(2, 3), (4, 5), (0, 2)]
        BB = [(1, 2), (4, 5), (6, 7)]

        block = ctx.enter_context(nc.Block())

        @block.sync
        def _(sp):
            sp.dma_start(X[:, 0:2, :], x_prompt[0].rearrange("(i p) n -> p i n", p=P)).then_inc(x_in, 16)
            sp.dma_start(X[0:64, 2, :], x_sample.rearrange("b t n -> (b t) n")).then_inc(x_in, 16)
            for dst, src in rows:
                sp.dma_start(dst, src).then_inc(rows_in, 16)
            for n in range(2):
                for o in (768, 1280):
                    o += 256 * n
                    sp.dma_start(win[:, :, o:o + 256], win_v[:, :, o:o + 256]).then_inc(ug_in[n], 16)
            sp.dma_start(win[:, :, 512:768], win_v[:, :, 512:768]).then_inc(kv_in, 16)
            sp.dma_start(win[:, :, 0:512], win_v[:, :, 0:512]).then_inc(q_in, 16)
            load_w1(sp, 0, 0, range(2))
            sp.wait_ge(S["q_done"], 4)
            load_w1(sp, 1, 1, range(2))
            sp.wait_ge(S["conv_ok"], CJ)
            sp.wait_ge(S["ct_tp"], 2)
            for h in range(2):
                sp.dma_start(wout[64 * h:64 * h + 64, 0:G, :],
                             w_out[0, 256 * h:256 * h + 256, :].rearrange("(g d) n -> d g n", g=G)).then_inc(wout_in, 16)
            sp.dma_start(wout[:, G:KD, :], w_out[0, 512:1024, :].rearrange("(j p) n -> p j n", p=P)).then_inc(wout_in, 16)
            load_w1(sp, 1, 1, range(2, 3))
            sp.wait_ge(S["krot_ok"], 1)
            for n, (dst_p, dst_s) in enumerate(((nk_p, nk_sv), (nv_p, nv_sv))):
                sp.dma_start(dst_p[0, 0].rearrange("w h d -> w (h d)"), kv[:, 1, P * n:P * n + P]).then_inc(new_out, 16)
                for b in range(NB):
                    sp.dma_start(dst_s[b, W - NS:W, :], kv[NS * b:NS * b + NS, 2, P * n:P * n + P]).then_inc(new_out, 16)
            sp.wait_ge(S["ct_ok"], 2)
            sp.dma_start(nc_p[0, 0], ct_out[0:CTX, 0:512]).then_inc(new_out, 16)
            for b in range(NB):
                sp.dma_start(nc_s[0, b, CTX - NS:CTX, :], ct_out[NS * b:NS * b + NS, 512:1024]).then_inc(new_out, 16)
            sp.wait_ge(S["o_done"], 6)
            sp.wait_ge(S["mixc_ok"], CJ)
            load_w1(sp, 0, 0, range(2, 4))
            load_w1(sp, 1, 1, range(3, 4))
            sp.wait_ge(S["op_done"], NT)
            load_w2(sp, 0)
            sp.wait_ge(S["tab_ok"], 6)
            with sp.Fori(0, E // 2 - 1) as i:
                for u in range(2):
                    end = sp.value_load(cnt_i[0:1, bass.ds(2 * i + (E + u + 1), 1)], min_val=1, max_val=MAXB - 2)
                    sp.wait_ge(gate_done, end)
                    load_w1(sp, u, 2 * i + u + 2, range(2))
                    sp.wait_ge(lin_done, end)
                    load_w1(sp, u, 2 * i + u + 2, range(2, 4))
                    sp.wait_ge(yp_ready, end)
                    load_w2(sp, 2 * i + u + 1)
            end = sp.value_load(cnt_i[0:1, 2 * E - 1:2 * E], min_val=1, max_val=MAXB - 2)
            sp.wait_ge(lin_done, end)
            sp.wait_ge(yp_ready, end)
            load_w2(sp, E - 1)
            sp.dma_start(gfin, final_norm_g.partition_broadcast(P)).then_inc(tail_in, 16)
            sp.dma_start(b2_sb, b2[0]).then_inc(b2_in, 16)
            sp.wait_ge(all_added, 1)
            for i in range(NT):
                sp.dma_start(fin[:, i, :], acc_t[:, i, :]).then_inc(fin_in[i], 16)
            for i in range(NT):
                sp.wait_ge(y_ok, i + 1)
                if i < 2:
                    sp.dma_start(y_prompt[0, P * i:P * i + P, :], fin[:, i, :]).then_inc(y_out, 16)
                else:
                    sp.dma_start(y_sample.rearrange("b t n -> (b t) n"), fin[0:64, i, :]).then_inc(y_out, 16)
            sp.wait_ge(y_out, 16 * NT)

        @block.scalar
        def _(act):
            step = [0]

            def own(ins):
                step[0] += 1
                ins.then_inc(S["act"], 1)
                act.wait_ge(S["act"], step[0])

            act.dma_start(C[:, :], consts).then_inc(consts_in, 16)
            act.wait_ge(rows_in, 16 * 7)
            act.dma_start(A, aconsts).then_inc(aconsts_in, 16)
            act.dma_start(ck_rows, cache_k[0].rearrange("b w h d -> w b (h d)")).then_inc(caches_in, 16)
            act.dma_start(cv_rows, cache_v[0].rearrange("b w h d -> w b (h d)")).then_inc(caches_in, 16)
            act.dma_start(sinks8, attn_sinks[0].partition_broadcast(P)).then_inc(caches_in, 16)
            act.dma_start(rw[:, :, :], router_w[0].rearrange("(k p) e -> p k e", p=P)).then_inc(late_in, 16)
            act.dma_start(rb[:, :], router_b[0].partition_broadcast(P)).then_inc(late_in, 16)
            act.dma_start(b1q[:, :], b1[0].rearrange("e (q n) -> (e q) n", n=512)).then_inc(b1_in, 16)

            for i in range(NT):
                if i == 0:
                    act.wait_ge(x_in, 32)
                if i == 2:
                    act.wait_ge(S["pads"], 1)
                act.activation(XTf[:, 0:1024], X[:, i, :], ACT.Square, accum_out=ssq[:, i:i + 1]).then_inc(S["ssq_ok"], 1)
                act.wait_ge(S["ssq_ok"], i + 1)
            act.wait_ge(S["var_ok"], 1)
            act.activation(std, var, ACT.Sqrt).then_inc(S["std_ok"], 1)
            act.wait_ge(S["early_tp"], 1)
            act.copy(par[:, :], PS[:, 7, 0:28]).then_inc(S["par_ok"], 1)
            act.copy(cwT[:, :, :], PS[:, 7, 32:32 + CJ * TAPS].rearrange("p (j t) -> p j t", j=CJ)).then_inc(S["par_ok"], 1)
            for j in range(CJ):
                act.copy(aS[:, j, :, 0:CTX],
                         PS[:, 5 + j // 2, 256 * (j % 2):256 * (j % 2) + 240].rearrange("p (b t) -> p b t", b=NB))\
                    .then_inc(S["st_ok"], 1)
            act.wait_ge(S["par_ok"], 2)
            for k in range(1, KD, 2):
                act.wait_ge(S["xt_tp"], k + 1)
                act.activation(XT[:, k, :], PS[:, k, 0:TPAD], ACT.Copy, scale=par[:, k:k + 1]).then_inc(S["xt_a"], 1)
            def products(n0, n1):
                for n in range(n0, n1):
                    j, t = (0, n) if n < TAPS else (CJ - 1, TAP3 + n - TAPS)
                    first = n in (0, TAPS)
                    dst = prod[:, n % 3, :] if not first else part3 if n else yc[:, 0, :]
                    if n == TAPS:
                        act.wait_ge(S["a_ok"], CJ)
                    if n > 3:
                        act.wait_ge(S["conv_add"], n - 3 - (n - 3 >= TAPS))
                    for d, a in ((dst[:, 0:PROMPT], aP[:, j, t:t + PROMPT]),
                                 (dst[:, PROMPT:TOK].rearrange("p (b t) -> p b t", b=NB), aS[:, j, :, t:t + NS])):
                        if n == 0:
                            last = act.activation(d, a, ACT.Identity, scale=cwT[:, 0, t:t + 1], bias=par[:, 16:17])
                        else:
                            last = act.activation(d, a, ACT.Copy, scale=cwT[:, j, t:t + 1])
                    last.then_inc(S["conv_prod"], 1)

            for j in range(CJ):
                act.wait_ge(S["ug_done"], j + 1)
                if j >= 2:
                    act.wait_ge(S["a_ok"], j - 1)
                act.activation(sg[:, j % 2, :], PS[:, 2 * j + 1, 0:TOK], ACT.Sigmoid).then_inc(S["sg_ok"], 1)
                if j == 0:
                    act.wait_ge(S["a_ok"], 1)
                if j < 3:
                    products(TAPS * j // 3, TAPS * (j + 1) // 3)
            products(TAPS, 2 * TAPS - TAP3)
            act.wait_ge(S["kv_done"], 1)
            act.copy(kv[:, :, :], KVP).then_inc(S["kv_ok"], 1)
            for g in range(G):
                act.wait_ge(S["q_done"], g + 1)
                act.copy(q_sb[:, g, :], PS[:, 2 + g, 0:TOK]).then_inc(S["q_ok"], 1)
            act.wait_ge(S["kc_tp"], 1)
            act.copy(kcT[:, :, :], PS[:, 0:2, :].rearrange("p b n -> p (b n)").rearrange("p (b n) -> p b n", b=NB))\
                .then_inc(S["kc_ok"], 1)
            for g in range(G):
                act.wait_ge(S["rot_done"], g + 1)
                act.copy(rq_sb[:, g, :], PS[:, 2 + g, 0:TOK]).then_inc(S["rq_ok"], 1)
            act.wait_ge(S["kT_tp"], 1)
            act.copy(kT, PS[:, 6, 0:TPAD]).then_inc(S["kT_ok"], 1)
            act.wait_ge(S["conv_add"], 2 * TAPS - TAP3 - 2)
            act.wait_ge(S["ct_tp"], 1)
            act.copy(ct_out[0:CTX, 0:512], PS[0:CTX, 7, :]).then_inc(S["ct_ok"], 1)
            act.wait_ge(S["ct_tp"], 2)
            act.copy(ct_out[0:64, 512:1024], PS[0:64, 7, :]).then_inc(S["ct_ok"], 1)
            for j in range(CJ):
                act.wait_ge(S["xc_ok"], j + 1)
                if j >= 2:
                    act.wait_ge(S["ln2"], j - 1)
                act.activation(sg[:, j % 2, :], yc[:, j, :], ACT.Square).then_inc(S["sq_ok"], 1)
            act.wait_ge(S["lnv_ok"], 1)
            act.activation(sg[:, 0, :], sg[:, 0, :], ACT.Sqrt).then_inc(S["lns_ok"], 1)
            for j in range(CJ):
                act.wait_ge(S["z_ok"], j + 1)
                act.activation(mixT[:, G + j, 0:TOK], yc[:, j, :], ACT.Silu, scale=par[:, 20 + j:21 + j],
                               bias=par[:, 24 + j:25 + j]).then_inc(S["mixc_ok"], 1)
            for g, (h, R, K, o, _) in enumerate(GROUPS):
                act.wait_ge(S["nm_ok"], g + 1)
                for r in range(R):
                    s = SALL[:, o + K * r:o + K * r + K]
                    act.activation(s, s, ACT.Exp, bias=nm[:, g, r:r + 1], accum_out=rs[:, g, r:r + 1])
                act.activation(sd[:, g, 0:R], sd[:, g, 0:R], ACT.Exp).then_inc(S["exp_ok"], 1)
            for n in range(4, PT_N):
                turned_p(act, act.copy, n).then_inc(S["pt_ok2"], 1)
            for i in range(NT):
                act.wait_ge(S["x2_ok"], 2 * i + 2)
                act.activation(junk2, X[:, i, :], ACT.Square, accum_out=ssq[:, i:i + 1]).then_inc(S["ssq2_ok"], 1)
                act.wait_ge(S["var2_ok"], i + 1)
                act.activation(std[:, i:i + 1], var[:, i:i + 1], ACT.Sqrt).then_inc(S["std2_ok"], 1)
            act.wait_ge(S["d_ok"], 1)
            act.activation(ge, ge, ACT.Exp).then_inc(S["ge_ok"], 1)
            act.wait_ge(S["gt_tp"], 1)
            act.copy(GT[:, :], PS[0:E, 5, 0:TPAD]).then_inc(S["gt_ok"], 1)

            act.wait_ge(S["tab_ok"], 6)
            total = act.value_load(cnt_i[0:1, 2 * E:2 * E + 1], min_val=E, max_val=MAXB - 2)
            with act.Fori(0, total) as m:
                act.wait_ge(g_ready, m + 1)
                act.activation(sig, gate, ACT.Sigmoid, scale=ALPHA).then_inc(sig_ready, 1)
                for c in range(2):
                    act.wait_ge(htp_ready, 2 * m + c + 1)
                    act.copy(hT[:, 2 * c:2 * c + 2], PS[:, 4 + c, 0:256].rearrange("p (s h t) -> p s h t", s=2, h=2))\
                        .then_inc(hT_ready, 1)
                act.wait_ge(y_free, m + 1)
                act.wait_ge(yp_ready, m + 1)
                act.activation(ysb, PS[:, 3, :], ACT.Copy, scale=wtab[:, bass.ds(m, 1)]).then_inc(y_ready, 1)

            for i in range(NT + 1):
                if i < NT:
                    act.wait_ge(fsum, 2 * i + 2)
                    act.activation(junk[:, i, :], fin[:, i, :], ACT.Square, accum_out=ssq[:, i:i + 1]).then_inc(fssq, 1)
                if i:
                    act.wait_ge(fvar, i)
                    act.activation(std[:, i - 1:i], var[:, i - 1:i], ACT.Sqrt).then_inc(fstd, 1)

        @block.tensor
        def _(pe):
            mm = nc.tensor.matmul
            tp = nc.tensor.transpose

            def router(i):
                pe.wait_ge(S["x2_ok"], 2 * i + 2)
                pair = [6, 7]
                if i:
                    pe.wait_ge(S["hT_ok"], i)
                for k in range(KD):
                    last = nc.tensor.transpose(PS[:, pair[k // 4], P * (k % 4):P * (k % 4) + P], X[:, i, P * k:P * k + P], ident)
                last.then_inc(S["h_tp"], 1)
                pe.wait_ge(S["hT_ok"], i + 1)
                if i == 0:
                    pe.wait_ge(late_in, 32)
                for k in range(KD):
                    last = nc.tensor.matmul(PS[:, 1, E * i:E * i + E], hTr[:, k, :], rw[:, k, :], start=(k == 0), stop=(k == KD - 1))
                last.then_inc(S["lg_done"], 1)

            def turn_x():
                for k in range(KD):
                    last = tp(PS[:, 0, SLOTS * k:SLOTS * k + SLOTS], xg[:, P * k:P * k + P], ident[0:SLOTS, 0:SLOTS])
                last.then_inc(xtp_ready, 1)

            pe.wait_ge(consts_in, 16)
            pe.wait_ge(rows_in, 16 * 7)
            tp(PS[:, 7, 0:28], par_rows, ident[0:28, 0:28])
            for j in range(CJ):
                tp(PS[:, 7, 32 + TAPS * j:32 + TAPS * (j + 1)], cw_rows[:, P * j:P * j + P], ident[0:TAPS, 0:TAPS])
            for j in range(CJ):
                for q in range(2):
                    o = 256 * (j % 2) + 120 * q
                    last = tp(PS[:, 5 + j // 2, o:o + 120], st_rows[:, q, P * j:P * j + P], ident[0:120, 0:120])
            last.then_inc(S["early_tp"], 1)
            pe.wait_ge(S["xn_ok"], NT)
            for k in range(KD):
                if k == 4:
                    pe.wait_ge(S["st_ok"], CJ)
                    pe.wait_ge(S["par_ok"], 2)
                for i in range(NT):
                    last = tp(PS[:, k, P * i:P * i + P], xn[:, i, P * k:P * k + P], ident)
                last.then_inc(S["xt_tp"], 1)
            pe.wait_ge(S["xt_v"], KD // 2)
            pe.wait_ge(S["xt_a"], KD // 2)
            for j in range(CJ):
                if j % 2 == 0:
                    pe.wait_ge(ug_in[j // 2], 32)
                for n, o in enumerate((768, 1280)):
                    for k in range(KD):
                        last = mm(PS[:, 2 * j + n, 0:TOK], win[:, k, o + P * j:o + P * j + P], XT[:, k, 0:TOK],
                                  start=(k == 0), stop=(k == KD - 1))
                last.then_inc(S["ug_done"], 1)
            pe.wait_ge(kv_in, 16)
            pe.wait_ge(S["a_ok"], 1)
            for i in range(NT):
                for k in range(KD):
                    last = mm(KVP[:, i, :], XT[:, k, P * i:P * i + P], win[:, k, 512:768], start=(k == 0), stop=(k == KD - 1))
            last.then_inc(S["kv_done"], 1)
            pe.wait_ge(q_in, 16)
            for g in range(G):
                pe.wait_ge(S["a_ok"], (2 + g) // 2 + 1)
                for k in range(KD):
                    for h in range(2):
                        o = 256 * h + 64 * g
                        last = mm(PS[64 * h:64 * h + 64, 2 + g, 0:TOK], win[:, k, o:o + 64], XT[:, k, 0:TOK],
                                  start=(k == 0), stop=(k == KD - 1))
                last.then_inc(S["q_done"], 1)
            pe.wait_ge(caches_in, 16 * 3)
            pe.wait_ge(S["kv_ok"], 1)
            for b in range(NB):
                last = tp(PS[:, b // 4, P * (b % 4):P * (b % 4) + P], ck_rows[:, b, :], ident)
            last.then_inc(S["kc_tp"], 1)
            for g in range(G):
                pe.wait_ge(S["q_ok"], g + 1)
                mm(PS[:, 2 + g, 0:TOK], C[:, C_ROT:C_ROT + P], q_sb[:, g, :], start=True, stop=True).then_inc(S["rot_done"], 1)
            pe.wait_ge(S["krot_ok"], 1)
            pe.wait_ge(S["a_ok"], CJ)
            for i in range(NT):
                last = tp(PS[:, 6, P * i:P * i + P], kv[:, i, 0:P], ident)
            last.then_inc(S["kT_tp"], 1)
            for j in range(CJ):
                last = tp(PS[0:CTX, 7, P * j:P * j + P], aP[:, j, PROMPT:PROMPT + CTX], ident)
            last.then_inc(S["ct_tp"], 1)
            pe.wait_ge(S["ct_ok"], 1)
            pe.wait_ge(S["an_ok"], CJ)
            for j in range(CJ):
                last = tp(PS[0:64, 7, P * j:P * j + P], a_new[:, j, :], ident)
            last.then_inc(S["ct_tp"], 1)
            pe.wait_ge(S["conv_ok"], CJ)
            pe.wait_ge(S["rq_ok"], G)
            for j in range(CJ):
                last = mm(PS[:, 5, 0:TOK], ones, yc[:, j, :], start=(j == 0), stop=(j == CJ - 1))
            last.then_inc(S["ln1"], 1)
            pe.wait_ge(S["xc_ok"], CJ)
            for j in range(CJ):
                pe.wait_ge(S["sq_ok"], j + 1)
                mm(PS[:, 5, 0:TOK], ones, sg[:, j % 2, :], start=(j == 0), stop=(j == CJ - 1)).then_inc(S["ln2"], 1)
            pe.wait_ge(S["qT_ok"], G)
            pe.wait_ge(S["kT_ok"], 1)
            pe.wait_ge(S["kc_ok"], 1)
            pe.wait_ge(S["rq_ok"], G)
            for n, (h, R, K, o, bank) in enumerate(GROUPS):
                hp = slice(64 * h, 64 * h + 64)
                if n == 3:
                    pe.wait_ge(S["lnv_ok"], 1)
                if n < 4:
                    blk = n // 2
                    out = PS[:, bank:bank + 2, :].rearrange("p b n -> p (b n)") if blk else PS[:, bank, :]
                    for g in range(G):
                        last = mm(out[:, K * g:K * g + K], qT[hp, g, W * blk:W * blk + W], kT[hp, 0:K], start=True, stop=True)
                else:
                    if n == 5:
                        pe.wait_ge(S["ct_ok"], 2)
                    for q in range(2):
                        for b in range(4):
                            mm(PS[32 * b:32 * b + 32, bank, 192 * q:192 * q + W],
                               qS[hp, 4 * q + b].rearrange("p g t -> p (g t)"),
                               kcT[hp, 4 * q + b, :], start=True, stop=True)
                    for q in range(2):
                        last = mm(PS[:, bank, 192 * q + W:192 * q + 192],
                                  qS[hp, 4 * q:4 * q + 4].rearrange("p b g t -> p (b g t)"),
                                  kT[hp, PROMPT:TOK], start=True, stop=True)
                last.then_inc(S["s_done"], 1)
            def turn_p(n):
                g, kb = PT_ORDER[n]
                _, R, K, o, _ = GROUPS[g]
                pe.wait_ge(S["p_ok"], g + 1)
                if n < 4:
                    pe.wait_ge(S["s_evac"], n + 1 if n < 2 else n + 3)
                elif n < 6:
                    pe.wait_ge(S["pt_ok"], n - 1)
                else:
                    pe.wait_ge(S["pt_ok2"], n - 5)
                b = PT_BANK[n]
                if g < 4:
                    for r in range(R):
                        last = tp(PS[:, b, P * r:P * r + P], SALL[:, o + K * r + P * kb:o + K * r + P * kb + P], ident)
                else:
                    for q in range(2):
                        tp(PS[:, b, P * q:P * q + P], SALL[:, o + K * q:o + K * q + P], ident)
                        last = tp(PS[0:64, b, 256 + P * q:256 + P * q + P], SALL[:, o + K * q + P:o + K * q + 192], ident)
                last.then_inc(S["pt_done"], 1)

            def wait_turned(n):
                if n < 4:
                    pe.wait_ge(S["pt_ok"], n + 1)
                else:
                    pe.wait_ge(S["pt_ok2"], n - 3)

            def values(n, bank, first_kb, last_kb):
                g, kb = PT_ORDER[n]
                h, o = GROUPS[g][0], GROUPS[g][3]
                hp = slice(64 * h, 64 * h + 64)
                wait_turned(n)
                return mm(PS[hp, bank, :], kv[:, kb, P + 64 * h:P + 64 * h + 64], SALL[:, o + 512 * kb:o + 512 * kb + 512],
                          start=first_kb, stop=last_kb)

            def out_projection(i, ks):
                for n in range(2):
                    for k in ks:
                        last = mm(PS[:, OB[i][n], :], mixT[:, k, P * i:P * i + P], wout[:, k, 512 * n:512 * n + 512],
                                  start=(k == G), stop=(k == G - 1))
                return last

            pe.wait_ge(wout_in, 48)
            pe.wait_ge(S["mixc_ok"], CJ)
            pe.wait_ge(S["s_evac"], 3)
            out_projection(0, range(G, KD))
            for n in range(2):
                turn_p(n)
            pe.wait_ge(S["s_evac"], 4)
            out_projection(1, range(G, KD))
            for n in range(2):
                values(n, 0, True, True).then_inc(S["o_done"], 1)
            for n in range(2, 4):
                turn_p(n)
            for n in range(2, 4):
                last = values(n, 1, n == 2, n == 3)
            last.then_inc(S["o_done"], 1)
            for n in range(4, 6):
                turn_p(n)
            for n in range(4, 6):
                last = values(n, 1, n == 4, n == 5)
            last.then_inc(S["o_done"], 1)
            for n in range(6, 8):
                turn_p(n)
            pe.wait_ge(S["o_ok"], 1)
            for n in range(6, 8):
                g, _ = PT_ORDER[n]
                h, o = GROUPS[g][0], GROUPS[g][3]
                hp = slice(64 * h, 64 * h + 64)
                wait_turned(n)
                for q in range(2):
                    mm(PS[hp, 0, P * q:P * q + P], kv[0:64, 2, P + 64 * h:P + 64 * h + 64],
                       SALL[0:64, o + 256 + P * q:o + 256 + P * q + P], start=True, stop=False, skip_group_check=True)
                    for b in range(4):
                        last = mm(PS[hp, 0, P * q + 32 * b:P * q + 32 * b + 32], cv_rows[:, 4 * q + b, 64 * h:64 * h + 64],
                                  SALL[:, o + P * q + 32 * b:o + P * q + 32 * b + 32], start=False, stop=(b == 3),
                                  skip_group_check=True)
                last.then_inc(S["o_done"], 1)
            pe.wait_ge(S["o_ok"], 4)
            for i in range(NT):
                if i == 2:
                    pe.wait_ge(S["x2_ok"], 2)
                last = out_projection(i, range(G) if i < 2 else [*range(G, KD), *range(G)])
                last.then_inc(S["op_done"], 1)
                if i >= 1:
                    router(i - 1)
            router(NT - 1)
            pe.wait_ge(S["m_ok"], 1)
            mm(PS[:, 0, 0:E * (NT + 1)], ones, cum[:, :, :].rearrange("p i e -> p (i e)"), start=True, stop=False, skip_group_check=True)
            last = mm(PS[:, 0, 0:E * NT], C[:, C_UP:C_UP + P], Mm[:, :, :].rearrange("p i e -> p (i e)"), start=False, stop=True,
                      skip_group_check=True)
            last.then_inc(S["rk_done"], 1)
            pe.wait_ge(S["g_ok"], 1)
            for i in range(NT):
                last = tp(PS[0:E, 5, P * i:P * i + P], Gg[:, i, :], ident)
            last.then_inc(S["gt_tp"], 1)
            pe.wait_ge(S["route_ok"], 1)
            for n in range(TOPK * NT):
                k, i = n // NT, n % NT
                last = mm(PS[:, 1, 0:2 * MAXB], ohs[:, k, i, :], rhs[:, k, i, :, :].rearrange("p v m -> p (v m)"),
                          start=(n == 0), stop=(n == TOPK * NT - 1))
            last.then_inc(S["tab_done"], 1)

            pe.wait_ge(S["tab_ok"], 6)
            pe.wait_ge(b1_in, 16)
            pe.wait_ge(xg_ready, 16)
            turn_x()
            with pe.Fori(0, E // 2) as i:
                for u in range(2):
                    nblk = pe.value_load(cnt_i[0:1, bass.ds(2 * i + u, 1)], min_val=1, max_val=XB + 1)
                    at = pe.value_load(cnt_i[0:1, bass.ds(E + 2 * i + u, 1)], min_val=0, max_val=MAXB - 3)
                    with pe.Fori(0, nblk) as b:
                        m = at + b
                        pe.wait_ge(xT_ready, m + 1)
                        pe.wait_ge(sel_ready, m + 1)
                        for s, done in ((0, gate_done), (1, lin_done)):
                            if s:
                                pe.wait_ge(xg_ready, 16 * m + 32)
                                pe.sem_inc(turned, 1)
                                turn_x()
                            for n in range(2):
                                mm(PS[64 * n:64 * n + 64, 1 + s, :], sel[:, 2 * s + n, :], b1q[:, :], start=True, stop=False)
                            for k in range(KD):
                                c = 2 * s + k // 4
                                if k % 4 == 0:
                                    pe.wait_ge(w1_in[u][c], 16 * i + 16)
                                for n in range(2):
                                    last = mm(PS[64 * n:64 * n + 64, 1 + s, :], xTe[:, SLOTS * k:SLOTS * k + SLOTS],
                                              w1buf[u][:, c, k % 4, 512 * n:512 * n + 512], start=False, stop=(k == KD - 1))
                            last.then_inc(done, 1)
                        for c in range(2):
                            pe.wait_ge(h_ready, 2 * m + c + 1)
                            for s in range(2):
                                o = P * (2 * c + s)
                                last = tp(PS[:, 4 + c, P * s:P * s + P], act_h[:, o:o + P], ident)
                            last.then_inc(htp_ready, 1)
                        for c in range(2):
                            pe.wait_ge(w2_in[c], 16 * (2 * i + u) + 16)
                        for s in range(4):
                            if s % 2 == 0:
                                pe.wait_ge(hT_ready, 2 * m + s // 2 + 1)
                            for h in range(2):
                                for n in range(2):
                                    last = mm(PS[64 * n:64 * n + 64, 3, :], hT[:, s, h, :], w2buf[:, 4 * h + s, 512 * n:512 * n + 512],
                                              start=(s == 0 and h == 0), stop=(s == 3 and h == 1))
                        last.then_inc(yp_ready, 1)
            pe.wait_ge(S["gt_ok"], 1)
            pe.wait_ge(b2_in, 16)
            for i in range(NT):
                for n in range(2):
                    last = mm(PS[:, BB[i][n], :], GT[:, P * i:P * i + P], b2_sb[:, 512 * n:512 * n + 512], start=True, stop=True)
                last.then_inc(b2_done, 1)


        @block.vector
        def _(dve):
            v = nc.vector
            step = [0]

            def own(ins):
                step[0] += 1
                ins.then_inc(S["vec"], 1)
                dve.wait_ge(S["vec"], step[0])

            v.memset(X[64:128, 2, :], 0.0).then_inc(S["pads"], 1)
            v.memset(aP[:, :, 0:CTX], 0.0).then_inc(S["pad_ok"], 1)
            dve.wait_ge(S["ssq_ok"], NT)
            v.tensor_scalar(var, ssq, 1.0 / D, EPS, ALU.mult, ALU.add).then_inc(S["var_ok"], 1)
            dve.wait_ge(S["std_ok"], 1)
            own(v.reciprocal(rstd, std))
            dve.wait_ge(x_in, 32)
            for i in range(NT):
                v.tensor_scalar(xn[:, i, :], X[:, i, :], rstd[:, i:i + 1], None, ALU.mult).then_inc(S["xn_ok"], 1)
            dve.wait_ge(S["par_ok"], 2)
            for k in range(0, KD, 2):
                dve.wait_ge(S["xt_tp"], k + 1)
                v.tensor_scalar(XT[:, k, :], PS[:, k, 0:TPAD], par[:, k:k + 1], None, ALU.mult).then_inc(S["xt_v"], 1)
            dve.wait_ge(S["pad_ok"], 1)
            dve.wait_ge(S["st_ok"], CJ)
            ys = yc[:, :, PROMPT:TOK].rearrange("p j (b t) -> p j b t", b=NB)

            def gated(j):
                dve.wait_ge(S["sg_ok"], j + 1)
                v.tensor_tensor(aP[:, j, CTX:CTX + PROMPT], PS[:, 2 * j, 0:PROMPT], sg[:, j % 2, 0:PROMPT], ALU.mult)
                v.tensor_tensor(aS[:, j, :, CTX:CTX + NS], PS[:, 2 * j, PROMPT:TOK].rearrange("p (b t) -> p b t", b=NB),
                                sg[:, j % 2, PROMPT:TOK].rearrange("p (b t) -> p b t", b=NB), ALU.mult).then_inc(S["a_ok"], 1)

            gated(0)
            gated(1)
            for j in range(1, CJ):
                dve.wait_ge(S["a_ok"], j + 1)
                taps = TAP3 if j == CJ - 1 else TAPS
                for t in range(taps):
                    pin, sin = aP[:, j, t:t + PROMPT], aS[:, j, :, t:t + NS]
                    w = cwT[:, j, t:t + 1]
                    if t == 0:
                        bias = par[:, 16 + j:17 + j]
                        v.tensor_scalar(yc[:, j, 0:PROMPT], pin, w, bias, ALU.mult, ALU.add).then_inc(S["vec"], 1)
                        v.tensor_scalar(ys[:, j], sin, w, bias, ALU.mult, ALU.add).then_inc(S["vec"], 1)
                    else:
                        last = t == TAPS - 1
                        dve.wait_ge(S["vec"], step[0] - 1)
                        v.scalar_tensor_tensor(yc[:, j, 0:PROMPT], pin, w, yc[:, j, 0:PROMPT], ALU.mult, ALU.add)\
                            .then_inc(S["vec"], 1)
                        dve.wait_ge(S["vec"], step[0])
                        v.scalar_tensor_tensor(ys[:, j], sin, w, ys[:, j], ALU.mult, ALU.add)\
                            .then_inc(S["conv_ok"] if last else S["vec"], 1)
                        if last:
                            step[0] -= 1
                    step[0] += 2
                    if j == 1 and t in (13, 26):
                        gated(t // 13 + 1)
            dve.wait_ge(S["vec"], step[0])
            dve.wait_ge(S["part_ok"], 1)
            v.tensor_tensor(yc[:, CJ - 1, :], yc[:, CJ - 1, :], part3, ALU.add).then_inc(S["conv_ok"], 1)
            dve.wait_ge(aconsts_in, 16)
            dve.wait_ge(caches_in, 16 * 3)
            for n in range(4):
                v.tensor_copy(sinks[:, n, :], sinks8[:, 4 * (n % 2):4 * (n % 2) + 4])
            own(v.tensor_tensor(picked, sinks8.rearrange("p (h g) -> p h g", h=2),
                                C[:, C_SG:C_SG + G].unsqueeze(1).to_broadcast([P, 2, G]), ALU.mult))
            for n in range(2):
                last = v.tensor_reduce(sinks[:, 4:6, n], picked, AX.X, ALU.add)
            own(last)

            dve.wait_ge(S["ln1"], 1)
            for j in range(CJ):
                v.scalar_tensor_tensor(yc[:, j, :], PS[:, 5, 0:TOK], -1.0 / CW, yc[:, j, :], ALU.mult, ALU.add)\
                    .then_inc(S["xc_ok"], 1)
            dve.wait_ge(S["ln2"], CJ)
            v.tensor_scalar(sg[:, 0, :], PS[:, 5, 0:TOK], 1.0 / CW, EPS, ALU.mult, ALU.add).then_inc(S["lnv_ok"], 1)
            dve.wait_ge(S["lns_ok"], 1)
            own(v.reciprocal(sg[:, 1, :], sg[:, 0, :]))
            dve.wait_ge(S["xc_ok"], CJ)
            for j in range(CJ):
                v.tensor_tensor(yc[:, j, :], yc[:, j, :], sg[:, 1, :], ALU.mult).then_inc(S["z_ok"], 1)
            def scores(g):
                h, R, K, o, bank = GROUPS[g]
                s = SALL[:, o:o + R * K].rearrange("p (r k) -> p r k", r=R)
                dve.wait_ge(S["s_done"], g + 1)
                if g < 4:
                    src = PS[:, bank:bank + 2, :].rearrange("p b n -> p (b n)")[:, 0:R * K].rearrange("p (r k) -> p r k", r=R)
                    mask = A[:, A_MP + 2 * W - K:A_MP + 2 * W].unsqueeze(1).to_broadcast([P, R, K])
                else:
                    src = PS[:, bank, 0:R * K].rearrange("p (r k) -> p r k", r=R)
                    mask = A[:, A_MS:A_MS + 384].rearrange("p (r k) -> p r k", r=2)
                v.tensor_tensor(s, src, mask, ALU.add).then_inc(S["s_evac"], 1)
                dve.wait_ge(S["s_evac"], g + 1)
                own(v.tensor_reduce(mx[:, g, 0:R], s, AX.X, ALU.max))
                own(v.tensor_tensor(mx[:, g, 0:R], mx[:, g, 0:R], sinks[:, g, 0:R], ALU.max))
                v.tensor_tensor(sd[:, g, 0:R], sinks[:, g, 0:R], mx[:, g, 0:R], ALU.subtract)
                v.tensor_scalar(nm[:, g, 0:R], mx[:, g, 0:R], -1.0, None, ALU.mult).then_inc(S["nm_ok"], 1)
            def probs(g):
                h, R, K, o, bank = GROUPS[g]
                s = SALL[:, o:o + R * K].rearrange("p (r k) -> p r k", r=R)
                dve.wait_ge(S["exp_ok"], g + 1)
                own(v.tensor_tensor(den[:, g, 0:R], rs[:, g, 0:R], sd[:, g, 0:R], ALU.add))
                own(v.reciprocal(den[:, g, 0:R], den[:, g, 0:R]))
                v.tensor_tensor(s, s, bc(den[:, g, 0:R], K), ALU.mult).then_inc(S["p_ok"], 1)
            for g in range(len(GROUPS)):
                scores(g)
                if g >= 2:
                    probs(g - 2)
                if g >= 4:
                    turned_p(dve, v.tensor_copy, g - 4).then_inc(S["pt_ok"], 1)
            for n in range(2, 4):
                turned_p(dve, v.tensor_copy, n).then_inc(S["pt_ok"], 1)
            for g in range(4, 6):
                probs(g)
            for n, bank in enumerate((0, 1)):
                dve.wait_ge(S["o_done"], 2 * n + 2)
                v.tensor_copy(mixT[:, 0:G, W * n:W * n + W], PS[:, bank, :].rearrange("p (g t) -> p g t", g=G)).then_inc(S["o_ok"], 1)
            dve.wait_ge(S["o_done"], 6)
            for q in range(2):
                t0 = PROMPT + 32 * q
                v.tensor_copy(mixT[:, 0:G, t0:t0 + 32].rearrange("p g (b t) -> p b g t", b=4),
                              PS[:, 0, P * q:P * q + P].rearrange("p (b g t) -> p b g t", b=4, g=G)).then_inc(S["o_ok"], 1)
            dve.wait_ge(new_out, 16 * OUTS)

            def finish_rows(i):
                for n in range(2):
                    v.tensor_tensor(X[:, i, 512 * n:512 * n + 512], PS[:, OB[i][n], :], X[:, i, 512 * n:512 * n + 512], ALU.add)\
                        .then_inc(S["x2_ok"], 1)
                dve.wait_ge(S["ssq2_ok"], i + 1)
                v.tensor_scalar(var[:, i:i + 1], ssq[:, i:i + 1], 1.0 / D, EPS, ALU.mult, ALU.add).then_inc(S["var2_ok"], 1)
                dve.wait_ge(S["h_tp"], i + 1)
                if i:
                    dve.wait_ge(S["lg_done"], i)
                v.tensor_tensor(hTr[:, :, :], PS[:, 6:8, :].rearrange("p b (k t) -> p (b k) t", k=4), bc(par[:, 8:16], P), ALU.mult)\
                    .then_inc(S["hT_ok"], 1)
                dve.wait_ge(S["std2_ok"], i + 1)
                own(v.reciprocal(rstd[:, i:i + 1], std[:, i:i + 1]))
                if i == 2:
                    dve.wait_ge(h_out[0], 16)
                v.tensor_scalar(Hs(i), X[:, i, :], rstd[:, i:i + 1], None, ALU.mult).then_inc(S["h_ok"], 1)

            for i in range(NT):
                dve.wait_ge(S["op_done"], i + 1)
                finish_rows(i)
            dve.wait_ge(S["lg_done"], NT)
            for i in range(NT):
                last = v.scalar_tensor_tensor(lg[:, i, :], PS[:, 1, E * i:E * i + E], rstd[:, i:i + 1], rb[:, :], ALU.mult, ALU.add)
            own(last)
            for i in range(NT):
                last = v.max(v8[:, i, :], lg[:, i, :])
            own(last)
            for i in range(NT):
                last = v.max_index(i8[:, i, :], v8[:, i, :], lg[:, i, :])
            last.then_inc(S["vec"], 1)
            step[0] += 1
            v.tensor_tensor(ge, v8[:, :, 0:TOPK], v8[:, :, 0:1].to_broadcast([P, NT, TOPK]), ALU.subtract).then_inc(S["d_ok"], 1)
            dve.wait_ge(S["vec"], step[0])
            own(v.tensor_copy(idf, i8[:, :, 0:TOPK]))
            own(v.tensor_tensor(idf, idf, bc(C[:, C_PAD:C_PAD + NT], TOPK), ALU.add))
            for k in range(TOPK):
                last = v.tensor_tensor(oh[:, k], C[:, C_IE:C_IE + E].unsqueeze(1).to_broadcast([P, NT, E]), bc(idf[:, :, k], E),
                                       ALU.is_equal)
            own(last)
            v.tensor_tensor(tmp4[:, 0], oh[:, 0], oh[:, 1], ALU.add)
            own(v.tensor_tensor(tmp4[:, 1], oh[:, 2], oh[:, 3], ALU.add))
            v.memset(cum[:, 0, :], 0.0)
            own(v.tensor_tensor(Mm, tmp4[:, 0], tmp4[:, 1], ALU.add))
            v.tensor_copy(cum[:, 1, :], Mm[:, 0, :])
            own(v.tensor_tensor(cum[:, 2, :], Mm[:, 0, :], Mm[:, 1, :], ALU.add))
            v.tensor_tensor(cum[:, 3, :], cum[:, 2, :], Mm[:, 2, :], ALU.add).then_inc(S["m_ok"], 1)
            dve.wait_ge(S["m_ok"], 1)
            dve.wait_ge(S["ge_ok"], 1)
            own(v.tensor_reduce(gs, ge, AX.X, ALU.add))
            own(v.reciprocal(gs, gs))
            own(v.tensor_tensor(ge, ge, bc(gs, TOPK), ALU.mult))
            for k in range(TOPK):
                last = v.tensor_tensor(tmp4[:, k], oh[:, k], bc(ge[:, :, k], E), ALU.mult)
            own(last)
            v.tensor_reduce(Gg, tmp4[:, :, :, :].rearrange("p k i e -> p i e k"), AX.X, ALU.add).then_inc(S["g_ok"], 1)
            dve.wait_ge(S["g_ok"], 1)
            dve.wait_ge(S["rk_done"], 1)
            v.tensor_copy(rk, PS[:, 0, 0:96].rearrange("p (i e) -> p i e", i=NT))
            v.memset(zero, 0.0)
            own(v.tensor_copy(cn, PS[:, 0, 96:96 + E]))
            v.tensor_scalar(fl, rk, float(SLOTS), None, ALU.is_ge)
            own(v.tensor_scalar(nb, cn, float(SLOTS), 1.0, ALU.is_gt, ALU.add))
            for b in range(2, XB + 1):
                v.scalar_tensor_tensor(fl, rk, float(SLOTS * b), fl, ALU.is_ge, ALU.add).then_inc(S["vec"], 1)
                v.scalar_tensor_tensor(nb, cn, float(SLOTS * b), nb, ALU.is_gt, ALU.add).then_inc(S["vec"], 1)
                step[0] += 2
                dve.wait_ge(S["vec"], step[0])
            own(v.tensor_tensor_scan(inc, nb, zero, 0.0, ALU.add, ALU.add))
            own(v.tensor_tensor(first, inc, nb, ALU.subtract))
            v.tensor_copy(cnt_i[0:1, 0:E], nb[0:1, :]).then_inc(S["tab_ok"], 1)
            v.tensor_copy(cnt_i[0:1, E:2 * E], first[0:1, :]).then_inc(S["tab_ok"], 1)
            v.tensor_copy(cnt_i[0:1, 2 * E:2 * E + 1], inc[0:1, E - 1:E]).then_inc(S["tab_ok"], 1)
            v.tensor_tensor(bk, fl, first.unsqueeze(1).to_broadcast([P, NT, E]), ALU.add)
            own(v.scalar_tensor_tensor(rk, fl, -float(SLOTS), rk, ALU.mult, ALU.add))
            for k in range(TOPK):
                last = v.tensor_tensor(tmp4[:, k], oh[:, k], bk, ALU.mult)
            own(last)
            own(v.tensor_reduce(mk, tmp4[:, :, :, :], AX.X, ALU.add))
            for k in range(TOPK):
                last = v.tensor_tensor(tmp4[:, k], oh[:, k], rk, ALU.mult)
            own(last)
            v.tensor_reduce(sk, tmp4[:, :, :, :], AX.X, ALU.add)
            own(v.tensor_tensor(mk, mk, C[:, C_PAD:C_PAD + NT].unsqueeze(1).to_broadcast([P, TOPK, NT]), ALU.add))
            dve.wait_ge(added, 16)
            dve.wait_ge(acc_init, 16 * (NT - 1))
            for k in range(TOPK):
                v.tensor_tensor(ohm[:, k], C[:, C_IM:C_IM + MAXB].unsqueeze(1).to_broadcast([P, NT, MAXB]), bc(mk[:, k, :], MAXB),
                                ALU.is_equal)
                last = v.tensor_tensor(ohs[:, k], C[:, C_IS:C_IS + P].unsqueeze(1).to_broadcast([P, NT, P]), bc(sk[:, k, :], P),
                                       ALU.is_equal)
            own(last)
            for k in range(TOPK):
                v.tensor_tensor(rhs[:, k, :, 0, :], ohm[:, k], bc(C[:, C_TK:C_TK + NT], MAXB), ALU.mult)
                last = v.tensor_tensor(rhs[:, k, :, 1, :], ohm[:, k], bc(ge[:, :, k], MAXB), ALU.mult)
            last.then_inc(S["route_ok"], 1)
            dve.wait_ge(S["tab_done"], 1)
            v.tensor_copy(wtab[:, :], PS[:, 1, MAXB:2 * MAXB]).then_inc(S["tab_ok"], 1)
            own(v.tensor_copy(t1, PS[:, 1, 0:MAXB]))
            v.tensor_scalar(inv, t1, 0.0, C[:, C_S1:C_S1 + 1], ALU.is_equal, ALU.mult)
            v.tensor_scalar(gtab[:, :], t1[0:SLOTS], -1.0, 0.0, ALU.add, ALU.max).then_inc(S["tab_ok"], 1)
            own(v.tensor_scalar(t2, t1, 2.0, C[:, C_S2:C_S2 + 1], ALU.mult, ALU.add))
            v.tensor_tensor(stab[:, :], t2, inv, ALU.add).then_inc(S["tab_ok"], 1)
            dve.wait_ge(S["tab_ok"], 6)

            def gain_x():
                v.tensor_tensor(xTe.rearrange("p (k s) -> p k s", k=KD), PS[:, 0, :].rearrange("p (k s) -> p k s", k=KD),
                                bc(par[:, 8:16], SLOTS), ALU.mult).then_inc(xT_ready, 1)

            dve.wait_ge(xtp_ready, 1)
            gain_x()
            with dve.Fori(0, E) as e:
                nblk = dve.value_load(cnt_i[0:1, bass.ds(e, 1)], min_val=1, max_val=XB + 1)
                at = dve.value_load(cnt_i[0:1, bass.ds(E + e, 1)], min_val=0, max_val=MAXB - 3)
                with dve.Fori(0, nblk) as b:
                    m = at + b
                    v.tensor_copy(sel, bc(C[:, bass.ds(4 * e + C_ID, 4)], SLOTS)).then_inc(sel_ready, 1)
                    dve.wait_ge(gate_done, m + 1)
                    v.tensor_scalar(gate, PS[:, 1, :], LIMIT, None, ALU.min).then_inc(g_ready, 1)
                    dve.wait_ge(sig_ready, m + 1)
                    v.tensor_tensor(swi, gate, sig, ALU.mult).then_inc(vstep, 1)
                    dve.wait_ge(lin_done, m + 1)
                    for c in range(2):
                        o = slice(256 * c, 256 * c + 256)
                        v.tensor_scalar(lin[:, o], PS[:, 2, o], LIMIT, -LIMIT, ALU.min, ALU.max).then_inc(vstep, 1)
                    for c in range(2):
                        o = slice(256 * c, 256 * c + 256)
                        dve.wait_ge(vstep, 3 * m + c + 2)
                        v.scalar_tensor_tensor(act_h[:, o], lin[:, o], 1.0, swi[:, o], ALU.add, ALU.mult).then_inc(h_ready, 1)
                    dve.wait_ge(xtp_ready, m + 2)
                    gain_x()

            def add_b2(i):
                dve.wait_ge(fin_in[i], 16)
                dve.wait_ge(b2_done, i + 1)
                for n in range(2):
                    f = fin[:, i, 512 * n:512 * n + 512]
                    v.tensor_tensor(f, PS[:, BB[i][n], :], f, ALU.add).then_inc(fsum, 1)

            dve.wait_ge(tail_in, 16)
            add_b2(0)
            for i in range(NT):
                if i + 1 < NT:
                    add_b2(i + 1)
                dve.wait_ge(fssq, i + 1)
                v.tensor_scalar(var[:, i:i + 1], ssq[:, i:i + 1], 1.0 / D, EPS, ALU.mult, ALU.add).then_inc(fvar, 1)
                dve.wait_ge(fstd, i + 1)
                own(v.reciprocal(rstd[:, i:i + 1], std[:, i:i + 1]))
                v.scalar_tensor_tensor(fin[:, i, :], fin[:, i, :], rstd[:, i:i + 1], gfin, ALU.mult, ALU.mult).then_inc(y_ok, 1)

        @block.gpsimd
        def _(pool):
            g = nc.gpsimd
            for src, dst in ((cache_k, nk_s), (cache_v, nv_s)):
                pool.dma_start(dst[0, :, 0:W - NS].rearrange("b w h d -> b (w h d)"),
                               src[0, :, NS:W].rearrange("b w h d -> b (w h d)")).then_inc(out_done, 16)
            pool.dma_start(nc_s[0, :, 0:CTX - NS, :].rearrange("b t n -> b (t n)"),
                           state_conv[0, :, NS:CTX, :].rearrange("b t n -> b (t n)")).then_inc(out_done, 16)
            sums = 0
            for n in range(1, 2 * TAPS - TAP3):
                if n == TAPS:
                    pool.wait_ge(S["conv_add"], sums)
                    pool.sem_inc(S["conv_ok"], 1)
                    continue
                pool.wait_ge(S["conv_prod"], n + 1)
                if sums:
                    pool.wait_ge(S["conv_add"], sums)
                dst = yc[:, 0, :] if n < TAPS else part3
                g.tensor_tensor(dst, dst, prod[:, n % 3, :], ALU.add).then_inc(S["conv_add"], 1)
                sums += 1
            pool.wait_ge(S["conv_add"], sums)
            pool.sem_inc(S["part_ok"], 1)
            for j in range(CJ):
                pool.wait_ge(S["a_ok"], j + 1)
                g.tensor_copy(a_new[:, j, :].rearrange("p (b t) -> p b t", b=NB), aS[:, j, :, CTX:CTX + NS]).then_inc(S["an_ok"], 1)
            pool.wait_ge(aconsts_in, 16)
            pool.wait_ge(S["kv_ok"], 1)
            k4 = kv[:, :, 0:P].rearrange("p i (h d) -> p i h d", h=2)
            x1, x2 = k4[:, :, :, 0:8], k4[:, :, :, 8:16]
            cs, sn = (A[:, o:o + 24].rearrange("p (i d) -> p i d", i=NT).unsqueeze(2).to_broadcast([P, NT, 2, 8]) for o in (A_CK, A_SK))
            for n, (a, c) in enumerate(((x1, cs), (x2, sn), (x2, cs), (x1, sn))):
                g.tensor_tensor(krt[:, n], a, c, ALU.mult).then_inc(S["pool"], 1)
            pool.wait_ge(S["pool"], 4)
            g.tensor_tensor(x1, krt[:, 0], krt[:, 1], ALU.subtract).then_inc(S["pool"], 1)
            pool.wait_ge(S["pool"], 5)
            g.tensor_tensor(x2, krt[:, 2], krt[:, 3], ALU.add).then_inc(S["krot_ok"], 1)
            for n in range(G):
                pool.wait_ge(S["rq_ok"], n + 1)
                g.tensor_tensor(q_sb[:, n, :], q_sb[:, n, :], A[:, A_COS:A_COS + TOK], ALU.mult).then_inc(S["pool"], 1)
                g.tensor_tensor(rq_sb[:, n, :], rq_sb[:, n, :], A[:, A_SIN:A_SIN + TOK], ALU.mult).then_inc(S["pool"], 1)
                pool.wait_ge(S["pool"], 5 + 2 * n + 2)
                g.tensor_tensor(qT[:, n, :], q_sb[:, n, 0:PROMPT], rq_sb[:, n, 0:PROMPT], ALU.add)
                g.tensor_tensor(qS[:, :, n, :], *(x[:, n, PROMPT:TOK].rearrange("p (b t) -> p b t", b=NB) for x in (q_sb, rq_sb)),
                                ALU.add).then_inc(S["qT_ok"], 1)
            pool.wait_ge(out_done, 16 * 3)
            pool.sem_inc(turn, 1)
            for i in range(NT):
                pool.wait_ge(S["x2_ok"], 2 * i + 2)
                pool.dma_start(acc_t[:, i, :], X[:, i, :]).then_inc(acc_init if i < NT - 1 else added, 16)
                pool.wait_ge(S["h_ok"], i + 1)
                pool.dma_start(h_dram[P * i:P * i + P, :], Hs(i)).then_inc(h_out[i], 16)

            pool.wait_ge(S["tab_ok"], 6)
            for i in range(NT):
                pool.wait_ge(h_out[i], 16)
            pool.wait_ge(acc_init, 16 * (NT - 1))
            total = pool.value_load(cnt_i[0:1, 2 * E:2 * E + 1], min_val=E, max_val=MAXB - 2)
            hmax = pool.to_reg(TPAD - 1)
            amax = pool.to_reg(2 * TPAD - 1)

            def gather(m):
                g.indirect_dma_start(out=xg, out_offset=None, in_=h_dram[:, :],
                                     in_offset=bass.IndirectOffsetOnAxis(ap=gcol[:, 0:1], axis=0),
                                     bounds_check=hmax, oob_is_err=True).then_inc(xg_ready, 16)

            for m in range(2):
                if m:
                    pool.wait_ge(xg_ready, 16)
                    pool.wait_ge(xtp_ready, 1)
                g.tensor_copy(gcol[:, :], gtab[:, m:m + 1]).then_inc(turn, 1)
                pool.wait_ge(turn, m + 2)
                gather(m)
            with pool.Fori(0, total) as m:
                pool.wait_ge(xg_ready, 16 * m + 32)
                pool.wait_ge(xtp_ready, m + 2)
                pool.sem_inc(turn, 1)
                g.tensor_copy(gcol[:, :], gtab[:, bass.ds(m + 2, 1)]).then_inc(turn, 1)
                pool.wait_ge(turn, 3 * m + 5)
                pool.sem_inc(pool_step, 1)
                gather(m + 2)
                pool.wait_ge(added, 16 * m + 16)
                pool.sem_inc(y_free, 1)
                g.tensor_copy(scol[:, :], stab[:, bass.ds(m, 1)]).then_inc(turn, 1)
                pool.wait_ge(turn, 3 * m + 6)
                pool.wait_ge(y_ready, m + 1)
                pool.sem_inc(pool_step, 1)
                g.indirect_dma_start(out=acc_dram[:, :], out_offset=bass.IndirectOffsetOnAxis(ap=scol[:, 0:1], axis=0),
                                     in_=ysb, in_offset=None, bounds_check=amax, oob_is_err=True,
                                     compute_op=ALU.add).then_inc(added, 16)
            pool.wait_ge(added, 16 * total + 16)
            pool.wait_ge(xg_ready, 16 * total + 32)
            pool.sem_inc(all_added, 1)


_INS = ["x_prompt", "x_sample", "cache_k", "cache_v", "state_conv", "attn_norm_g", "w_in", "attn_sinks",
        "conv_w", "conv_b", "conv_ln_g", "conv_ln_b", "w_out", "ffn_norm_g", "router_w", "router_b",
        "w1", "b1", "w2", "b2", "final_norm_g"]
_OUTS = [(1, PROMPT, D), (NB, NS, D), (1, 1, W, 2, HD), (1, 1, W, 2, HD), (1, 1, CTX, CW),
         (1, NB, W, 2, HD), (1, NB, W, 2, HD), (1, NB, CTX, CW)]


def kernel(**inputs):
    import numpy as _np
    import concourse.bacc as _bacc
    from concourse import mybir as _mybir
    from concourse.bass_utils import run_bass_kernel_spmd as _run

    nc = _bacc.Bacc("TRN2", target_bir_lowering=False, num_devices=1)
    arrays, args = {}, []
    consts, aconsts = tables()
    for name, a in [*((n, inputs[n]) for n in _INS), ("consts", consts), ("aconsts", aconsts)]:
        a = _np.ascontiguousarray(a)
        arrays[f"in_{name}_dram"] = a
        args.append(nc.dram_tensor(f"in_{name}_dram", a.shape, _mybir.dt.from_np(a.dtype), kind="ExternalInput").ap())
    for i, shape in enumerate(_OUTS):
        args.append(nc.dram_tensor(f"out_{i}_dram", shape, F32, kind="ExternalOutput").ap())
    args.append(nc.dram_tensor("h_rows", (TPAD, D), F32, kind="Internal").ap())
    args.append(nc.dram_tensor("acc_rows", (2 * TPAD, D // 2), F32, kind="Internal").ap())
    hybrid_step(nc, *args)
    r = _run(nc, [arrays], core_ids=[0])
    return tuple(r.results[0][f"out_{i}_dram"] for i in range(len(_OUTS)))
```

```python
from contextlib import ExitStack

import concourse.bass as bass
from concourse import mybir

F32 = mybir.dt.float32
U32 = mybir.dt.uint32
I32 = mybir.dt.int32
ALU = mybir.AluOpType
ACT = mybir.ActivationFunctionType
AX = mybir.AxisListType

P = 128
D = 1024
KD = D // P
NT = 3
TOK = 320
TPAD = NT * P
PROMPT = 256
NB = 8
NS = 8
W = 128
HD = 64
G = 4
CW = 512
CJ = CW // P
TAPS = 31
CTX = TAPS - 1
TAP3 = 25
E = 32
F = 1024
FT = F // P
SLOTS = 64
TOPK = 4
XB = 4
MAXB = 54
TRASH = 2 * TOK
EPS = 1e-5
LIMIT = 7.0
ALPHA = 1.702

C_ID, C_UP, C_ONE, C_ROT, C_IS = 0, 128, 256, 384, 512
C_IM = 640
C_IE = C_IM + MAXB
C_TK = C_IE + E
C_PAD = C_TK + NT
C_S1 = C_PAD + NT
C_S2 = C_S1 + 1
C_SG = C_S2 + 1
C_N = C_SG + G
A_COS, A_SIN = 0, TOK
A_CK = 2 * TOK
A_SK = A_CK + NT * 8
A_MP = A_SK + NT * 8
A_MS = A_MP + 2 * W
A_N = A_MS + 2 * 192

OUTS = 2 * (1 + NB) + 1 + NB
GROUPS = [(0, 4, 128, 0, 0), (1, 4, 128, 512, 1), (0, 4, 256, 1024, 2), (1, 4, 256, 2048, 4),
          (0, 2, 192, 3072, 6), (1, 2, 192, 3584, 7)]


def tables():
    import numpy as np
    c = np.zeros((P, C_N), np.float32)
    p = np.arange(P)
    c[:, C_ID:C_ID + P] = np.eye(P)
    c[:, C_UP:C_UP + P] = p[:, None] < p[None, :]
    c[:, C_ONE:C_ONE + P] = 1
    for o in (0, HD):
        for i in range(8):
            c[o + 8 + i, C_ROT + o + i] = -1
            c[o + i, C_ROT + o + 8 + i] = 1
    c[:, C_IS:C_IS + P] = p[None, :] % SLOTS
    c[:, C_IM:C_IM + MAXB] = np.arange(MAXB)[None, :]
    c[:, C_IE:C_IE + E] = np.arange(E)[None, :]
    tok = np.arange(NT)[None, :] * P + p[:, None]
    c[:, C_TK:C_TK + NT] = tok + 1
    c[:, C_PAD:C_PAD + NT] = np.where(tok < TOK, 0, -1000)
    half = p // SLOTS
    c[:, C_S1] = TRASH + p - half + 2
    c[:, C_S2] = half - 2
    c[:, C_SG:C_SG + G] = (p[:, None] // NS) % G == np.arange(G)[None, :]
    a = np.zeros((P, A_N), np.float32)
    pos = np.concatenate([np.arange(PROMPT), np.tile(2048 + np.arange(NS), NB)]).astype(np.float32)
    inv = np.power(np.float32(500000.0), -np.arange(8, dtype=np.float32) * np.float32(2.0) / np.float32(16))
    ang = (pos[:, None] * inv[None, :].astype(np.float32)).astype(np.float32)
    cos, sin = np.cos(ang.astype(np.float64)), np.sin(ang.astype(np.float64))
    scale = HD ** -0.5
    a[:, A_COS:A_COS + TOK] = scale
    for o in (0, 8, HD, HD + 8):
        a[o:o + 8, A_COS:A_COS + TOK] = (cos.astype(np.float32) * scale).T
        a[o:o + 8, A_SIN:A_SIN + TOK] = (sin.astype(np.float32) * scale).T
    for t in range(NT):
        n = min(P, TOK - t * P)
        a[:n, A_CK + 8 * t:A_CK + 8 * t + 8] = cos[t * P:t * P + n]
        a[:n, A_SK + 8 * t:A_SK + 8 * t + 8] = sin[t * P:t * P + n]
    no = -1e30
    j = np.arange(W)
    a[:, A_MP:A_MP + W] = np.where(j[None, :] > p[:, None], 0, no)
    a[:, A_MP + W:A_MP + 2 * W] = np.where(j[None, :] <= p[:, None], 0, no)
    b4, t = p // 32, p % 8
    for q in range(2):
        m = a[:, A_MS + 192 * q:A_MS + 192 * q + 192]
        m[:, :W] = np.where(j[None, :] > t[:, None], 0, no)
        n = np.arange(64)
        m[:, W:] = np.where((n[None, :] // 8 == (4 * q + b4)[:, None]) & (n[None, :] % 8 <= t[:, None]), 0, no)
    return c, a


def hybrid_step(nc, x_prompt, x_sample, cache_k, cache_v, state_conv, attn_norm_g, w_in, attn_sinks,
                conv_w, conv_b, conv_ln_g, conv_ln_b, w_out, ffn_norm_g, router_w, router_b,
                w1, b1, w2, b2, final_norm_g, consts, aconsts,
                y_prompt, y_sample, nk_p, nv_p, nc_p, nk_s, nv_s, nc_s, h_dram, acc_dram):
    with ExitStack() as ctx:
        def sb(name, shape, dt=F32):
            return ctx.enter_context(nc.sbuf_tensor(name, shape, dt))

        def sem(name):
            return ctx.enter_context(nc.semaphore(name))

        def bc(ap, n):
            return ap.unsqueeze(len(ap.shape)).to_broadcast([*ap.shape, n])

        WA = sb("WA", [P, 16384])
        WB = sb("WB", [P, 16384])
        W2 = sb("W2", [P, 8192])
        w1buf = [WA[:, :].rearrange("p (c k n) -> p c k n", c=4, k=4),
                 WB[:, :].rearrange("p (c k n) -> p c k n", c=4, k=4)]
        w2buf = W2[:, :].rearrange("p (k n) -> p k n", k=KD)
        win = WB[:, 0:KD * 1792].rearrange("p (k n) -> p k n", k=KD)
        ck_rows = WB[:, 14336:15360].rearrange("p (b n) -> p b n", b=NB)
        cv_rows = WB[:, 15360:16384].rearrange("p (b n) -> p b n", b=NB)
        wout = w2buf
        aP = W2[:, 0:4 * 286].rearrange("p (j t) -> p j t", j=CJ)
        aS = W2[:, 1144:1144 + 4 * 304].rearrange("p (j b t) -> p j b t", j=CJ, b=NB)
        c2 = WA[:, 8192:12288]
        c3 = WA[:, 12288:16384]
        xn = c2[:, 0:3072].rearrange("p (i n) -> p i n", i=NT)
        qT = c2[:, 0:1024].rearrange("p (g t) -> p g t", g=G)
        qS = c2[:, 1024:1280].rearrange("p (b g t) -> p b g t", b=NB, g=G)
        yc = c2[:, 1280:2560].rearrange("p (j t) -> p j t", j=CJ)
        kcT = c2[:, 2560:3584].rearrange("p (b n) -> p b n", b=NB)
        kT = c2[:, 3584:3968]
        st_rows = c3[0:120, 2048:3072].rearrange("p (q n) -> p q n", q=2)
        cw_rows = c3[0:TAPS, 3072:3584]
        par_rows = c3[0:28, 3584:3712]
        q_sb = c3[:, 0:1280].rearrange("p (g t) -> p g t", g=G)
        rq_sb = c3[:, 1280:2560].rearrange("p (g t) -> p g t", g=G)
        krt = c3[:, 2560:2560 + 192].rearrange("p (n i h d) -> p n i h d", n=4, i=NT, h=2)
        a_new = c3[:, 2752:3008].rearrange("p (j n) -> p j n", j=CJ)
        SALL = c3

        C = sb("C", [P, C_N])
        ident = C[:, C_ID:C_ID + P]
        ones = C[:, C_ONE:C_ONE + P]
        X = sb("X", [P, NT, D])
        XT = sb("XT", [P, KD, TPAD])
        mixT = XT
        M1 = sb("M1", [P, 2752])
        A = M1[:, 0:A_N]
        kv = M1[:, 1344:2112].rearrange("p (i n) -> p i n", i=NT)
        sg = M1[:, 2112:2752].rearrange("p (j t) -> p j t", j=2)
        part3 = sg[:, 0, :]
        H = [M1[:, 0:1024], M1[:, 1024:2048]]
        hTr = sb("hTr", [P, KD, P])
        ct_out = hTr[:, :, :].rearrange("p k t -> p (k t)")
        junk2 = M1[:, 2112:2752].bitcast(mybir.dt.bfloat16)[:, 0:D]
        prod = hTr[:, :, :].rearrange("p k t -> p (k t)")[:, 0:3 * TOK].rearrange("p (r t) -> p r t", r=3)
        par = sb("par", [P, 28])
        cwT = sb("cwT", [P, CJ, TAPS])
        b1q = sb("b1q", [P, 512])
        rw = sb("rw", [P, KD, E])
        rb = sb("rb", [P, E])
        sinks = sb("sinks", [P, 6, 4])
        GT = M1[0:E, 2112:2112 + TPAD]
        small = sb("small", [P, 160])
        ssq, var, std, rstd = (small[:, 3 * n:3 * n + 3] for n in range(4))
        sinks8 = small[:, 136:144]
        picked = small[:, 144:152].rearrange("p (h g) -> p h g", h=2)
        mx, nm, sd, rs, den = (small[:, 16 + 24 * n:40 + 24 * n].rearrange("p (g r) -> p g r", g=6) for n in range(5))
        cnt_i = sb("cnt_i", [1, 2 * E + 1], I32)
        gtab = sb("gtab", [SLOTS, MAXB], U32)
        stab = sb("stab", [P, MAXB], U32)
        wtab = sb("wtab", [P, MAXB])
        gcol = sb("gcol", [SLOTS, 1], U32)
        scol = sb("scol", [P, 1], U32)
        XTf = XT[:, :, :].rearrange("p k t -> p (k t)")
        Xf = X[:, :, :].rearrange("p i n -> p (i n)")
        lg = M1[:, 2624:2720].rearrange("p (i e) -> p i e", i=NT)
        v8 = M1[:, 2720:2744].rearrange("p (i k) -> p i k", i=NT)
        i8 = sb("i8", [P, NT, 8], U32)
        idf = XTf[:, 120:132].rearrange("p (i k) -> p i k", i=NT)
        ge = XTf[:, 132:144].rearrange("p (i k) -> p i k", i=NT)
        gs = XTf[:, 144:147]
        mk = XTf[:, 148:160].rearrange("p (k i) -> p k i", k=TOPK)
        sk = XTf[:, 160:172].rearrange("p (k i) -> p k i", k=TOPK)
        oh = XTf[:, 192:576].rearrange("p (k i e) -> p k i e", k=TOPK, i=NT)
        tmp4 = XTf[:, 576:960].rearrange("p (k i e) -> p k i e", k=TOPK, i=NT)
        Mm = XTf[:, 960:1056].rearrange("p (i e) -> p i e", i=NT)
        Gg = XTf[:, 1056:1152].rearrange("p (i e) -> p i e", i=NT)
        rc, fc = XTf[:, 2728:2856], XTf[:, 2856:2984]
        rk = rc[:, 0:NT * E].rearrange("p (i e) -> p i e", i=NT)
        fl = fc[:, 0:NT * E].rearrange("p (i e) -> p i e", i=NT)
        bk = XTf[:, 1344:1440].rearrange("p (i e) -> p i e", i=NT)
        cum = XTf[:, 2600:2600 + (NT + 1) * E].rearrange("p (i e) -> p i e", i=NT + 1)
        nb, inc, first, zero, cn = (XTf[:, 1440 + 32 * n:1472 + 32 * n] for n in range(5))
        ohm = XTf[:, 1600:1600 + 12 * MAXB].rearrange("p (k i m) -> p k i m", k=TOPK, i=NT)
        rhs = Xf[:, 0:24 * MAXB].rearrange("p (k i v m) -> p k i v m", k=TOPK, i=NT, v=2)
        ohs = Xf[:, 1296:2064].rearrange("p (k i s) -> p k i s", k=TOPK, i=NT)
        t1, inv, t2 = (XTf[:, 2300 + MAXB * n:2300 + MAXB * (n + 1)] for n in range(3))
        xg = Xf[0:SLOTS, 0:1024]
        xTe = Xf[:, 1024:1536]
        gate, lin = Xf[:, 1536:2048], Xf[:, 2048:2560]
        sig = Xf[:, 2560:3072]
        ysb = XTf[:, 0:512]
        swi = XTf[:, 512:1024]
        act_h = XTf[:, 1024:1536]
        hT = XTf[:, 1536:2048].rearrange("p (s h t) -> p s h t", s=4, h=2)
        sel = XTf[:, 2048:2304].rearrange("p (q s) -> p q s", q=4)
        fin = WA[:, 0:3072].rearrange("p (i n) -> p i n", i=NT)
        junk = WA[:, 6144:9216].rearrange("p (i n) -> p i n", i=NT)
        gfin = WA[:, 4096:5120]
        b2_sb = WA[0:E, 5120:6144]

        PS = ctx.enter_context(nc.psum_tensor("PS", [P, 8, 512], F32))
        KVP = PS[:, 0:2, :].rearrange("p b n -> p (b n)")[:, 0:768].rearrange("p (i n) -> p i n", i=NT)

        consts_in, aconsts_in, x_in, rows_in = sem("consts_in"), sem("aconsts_in"), sem("x_in"), sem("rows_in")
        caches_in, late_in = sem("caches_in"), sem("late_in")
        ug_in = [sem("ug_in0"), sem("ug_in1")]
        kv_in, q_in, wout_in, wout2_in = (sem(n) for n in ("kv_in", "q_in", "wout_in", "wout2_in"))
        w1_in = [[sem(f"w1_in{u}{c}") for c in range(4)] for u in range(2)]
        w2_in = [sem("w2_in0"), sem("w2_in1")]
        tail_in = sem("tail_in")
        fin_in = [sem(f"fin_in{i}") for i in range(NT)]
        out_done, new_out, acc_init, y_out = sem("out_done"), sem("new_out"), sem("acc_init"), sem("y_out")
        h_out = [sem(f"h_out{i}") for i in range(NT)]
        names = ("pads early_tp par_ok st_ok pad_ok ssq_ok var_ok std_ok xn_ok xt_tp xt_v xt_a ug_done sg_ok a_ok "
                 "conv_prod conv_add part_ok conv_ok kv_done kv_ok q_done q_ok rot_done rq_ok qT_ok krot_ok kT_tp kT_ok kc_tp kc_ok s_done s_evac nm_ok "
                 "exp_ok p_ok pt_done pt_ok pt_ok2 o_done o_ok ln1 xc_ok sq_ok ln2 lnv_ok lns_ok z_ok mixc_ok "
                 "ct_tp ct_ok op_done x2_ok ssq2_ok var2_ok std2_ok h_ok h_tp hT_ok lg_done d_ok ge_ok m_ok g_ok rk_done an_ok "
                 "ohm_ok rhs_ok route_ok tab_done tab_ok gt_tp gt_ok vec act pool").split()
        S = {n: sem(n) for n in names}
        xg_ready, pool_step, xtp_ready, xT_ready = sem("xg_ready"), sem("pool_step"), sem("xtp_ready"), sem("xT_ready")
        gate_half = sem("gate_half")
        gate_done, lin_done, g_ready, sig_ready = sem("gate_done"), sem("lin_done"), sem("g_ready"), sem("sig_ready")
        h_ready, htp_ready, hT_ready = sem("h_ready"), sem("htp_ready"), sem("hT_ready")
        sel_ready, yp_ready, y_ready, y_free, added = sem("sel_ready"), sem("yp_ready"), sem("y_ready"), sem("y_free"), sem("added")
        b1_in, vstep, turn, all_added, b2_in = (sem(n) for n in ("b1_in", "vstep", "turn", "all_added", "b2_in"))
        turned = sem("turned")
        fsum, fssq, fvar, fstd, b2_done, y_ok = sem("fsum"), sem("fssq"), sem("fvar"), sem("fstd"), sem("b2_done"), sem("y_ok")

        w1_v = w1.rearrange("l e (k p) n -> p (l e) k n", p=P)
        w2_v = w2.rearrange("l e (k p) n -> p (l e) k n", p=P)
        win_v = w_in[0].rearrange("(k p) n -> p k n", p=P)
        acc_t = acc_dram.rearrange("(i p h) n -> p i (h n)", p=P, h=2)
        nk_sv = nk_s[0].rearrange("b w h d -> b w (h d)")
        nv_sv = nv_s[0].rearrange("b w h d -> b w (h d)")

        def load_w1(eng, u, e, chunks=range(4)):
            for c in chunks:
                k0, n0 = 4 * (c % 2), F * (c // 2)
                src = w1_v[:, e, k0:k0 + 4, n0:n0 + F] if isinstance(e, int) else \
                    w1_v[:, bass.ds(e, 1), k0:k0 + 4, n0:n0 + F].rearrange("p o k n -> p (o k) n")
                eng.dma_start(w1buf[u][:, c], src).then_inc(w1_in[u][c], 16)

        def load_w2(eng, e):
            for c in range(2):
                src = w2_v[:, e, 4 * c:4 * c + 4, :] if isinstance(e, int) else \
                    w2_v[:, bass.ds(e, 1), 4 * c:4 * c + 4, :].rearrange("p o k n -> p (o k) n")
                eng.dma_start(w2buf[:, 4 * c:4 * c + 4, :], src).then_inc(w2_in[c], 16)

        rows = [(par_rows[0:8, :], attn_norm_g[0].rearrange("(k p) -> k p", p=P)),
                (par_rows[8:16, :], ffn_norm_g[0].rearrange("(k p) -> k p", p=P)),
                (par_rows[16:20, :], conv_b[0].rearrange("(k p) -> k p", p=P)),
                (par_rows[20:24, :], conv_ln_g[0].rearrange("(k p) -> k p", p=P)),
                (par_rows[24:28, :], conv_ln_b[0].rearrange("(k p) -> k p", p=P)),
                (cw_rows, conv_w[0]),
                (st_rows, state_conv[0].rearrange("b t n -> (b t) n").rearrange("(q p) n -> p q n", q=2))]

        def Hs(i):
            return H[i % 2]

        PT_ORDER = [(0, 0), (1, 0), (2, 0), (2, 1), (3, 0), (3, 1), (4, 0), (5, 0)]
        PT_BANK = [0, 1, 6, 7, 6, 7, 6, 7]
        PT_N = len(PT_ORDER)

        def pt_moves(n):
            g, kb = PT_ORDER[n]
            o, b = GROUPS[g][3], PT_BANK[n]
            if g < 4:
                return [(SALL[:, o + 512 * kb:o + 512 * kb + 512], PS[:, b, :])]
            return [(SALL[:, o:o + 256], PS[:, b, 0:256]), (SALL[0:64, o + 256:o + 512], PS[0:64, b, 256:512])]

        def turned_p(eng, copy, n):
            eng.wait_ge(S["pt_done"], n + 2 if n in (2, 4) else n + 1)
            for dst, src in pt_moves(n):
                last = copy(dst, src)
            return last

        OB = [(2, 3), (4, 5)]
        BB = [(1, 2), (4, 5), (6, 7)]

        block = ctx.enter_context(nc.Block())

        @block.sync
        def _(sp):
            sp.dma_start(X[:, 0:2, :], x_prompt[0].rearrange("(i p) n -> p i n", p=P)).then_inc(x_in, 16)
            sp.dma_start(X[0:64, 2, :], x_sample.rearrange("b t n -> (b t) n")).then_inc(x_in, 16)
            for dst, src in rows:
                sp.dma_start(dst, src).then_inc(rows_in, 16)
            for n in range(2):
                for o in (768, 1280):
                    o += 256 * n
                    sp.dma_start(win[:, :, o:o + 256], win_v[:, :, o:o + 256]).then_inc(ug_in[n], 16)
            sp.dma_start(win[:, :, 512:768], win_v[:, :, 512:768]).then_inc(kv_in, 16)
            sp.dma_start(win[:, :, 0:512], win_v[:, :, 0:512]).then_inc(q_in, 16)
            sp.dma_start(A, aconsts).then_inc(aconsts_in, 16)
            sp.dma_start(ck_rows, cache_k[0].rearrange("b w h d -> w b (h d)")).then_inc(caches_in, 16)
            sp.dma_start(cv_rows, cache_v[0].rearrange("b w h d -> w b (h d)")).then_inc(caches_in, 16)
            sp.dma_start(sinks8, attn_sinks[0].partition_broadcast(P)).then_inc(caches_in, 16)
            sp.dma_start(rw[:, :, :], router_w[0].rearrange("(k p) e -> p k e", p=P)).then_inc(late_in, 16)
            sp.dma_start(rb[:, :], router_b[0].partition_broadcast(P)).then_inc(late_in, 16)
            sp.dma_start(b1q[:, :], b1[0].rearrange("e (q n) -> (e q) n", n=512)).then_inc(b1_in, 16)
            load_w1(sp, 0, 0, range(2))
            sp.dma_start(wout[:, G:KD, :], w_out[0, 512:1024, :].rearrange("(j p) n -> p j n", p=P)).then_inc(wout2_in, 16)
            sp.wait_ge(S["conv_ok"], CJ)
            sp.wait_ge(S["ct_tp"], 2)
            for h in range(2):
                sp.dma_start(wout[64 * h:64 * h + 64, 0:G, :],
                             w_out[0, 256 * h:256 * h + 256, :].rearrange("(g d) n -> d g n", g=G)).then_inc(wout_in, 16)
            sp.wait_ge(S["q_done"], 4)
            load_w1(sp, 1, 1, range(3))
            sp.wait_ge(S["krot_ok"], 1)
            for n, (dst_p, dst_s) in enumerate(((nk_p, nk_sv), (nv_p, nv_sv))):
                sp.dma_start(dst_p[0, 0].rearrange("w h d -> w (h d)"), kv[:, 1, P * n:P * n + P]).then_inc(new_out, 16)
                for b in range(NB):
                    sp.dma_start(dst_s[b, W - NS:W, :], kv[NS * b:NS * b + NS, 2, P * n:P * n + P]).then_inc(new_out, 16)
            sp.wait_ge(S["ct_ok"], 2)
            sp.dma_start(nc_p[0, 0], ct_out[0:CTX, 0:512]).then_inc(new_out, 16)
            for b in range(NB):
                sp.dma_start(nc_s[0, b, CTX - NS:CTX, :], ct_out[NS * b:NS * b + NS, 512:1024]).then_inc(new_out, 16)
            sp.wait_ge(S["o_done"], 6)
            sp.wait_ge(S["mixc_ok"], CJ)
            load_w1(sp, 0, 0, range(2, 4))
            load_w1(sp, 1, 1, range(3, 4))
            sp.wait_ge(S["op_done"], NT)
            load_w2(sp, 0)
            sp.wait_ge(S["tab_ok"], 6)
            with sp.Fori(0, E // 2 - 2) as i:
                for u in range(2):
                    end = sp.value_load(cnt_i[0:1, bass.ds(2 * i + (E + u + 1), 1)], min_val=1, max_val=MAXB - 2)
                    sp.wait_ge(gate_half, end)
                    load_w1(sp, u, 2 * i + u + 2, [0])
                    sp.wait_ge(gate_done, end)
                    load_w1(sp, u, 2 * i + u + 2, [1])
                    sp.wait_ge(lin_done, end)
                    load_w1(sp, u, 2 * i + u + 2, range(2, 4))
                    sp.wait_ge(yp_ready, end)
                    load_w2(sp, 2 * i + u + 1)
            for e in range(E - 4, E - 1):
                end = sp.value_load(cnt_i[0:1, E + e + 1:E + e + 2], min_val=1, max_val=MAXB - 2)
                if e < E - 2:
                    sp.wait_ge(gate_half, end)
                    load_w1(sp, e % 2, e + 2, [0])
                    sp.wait_ge(gate_done, end)
                    load_w1(sp, e % 2, e + 2, [1])
                if e == E - 3:
                    sp.wait_ge(yp_ready, end)
                    load_w2(sp, e + 1)
                if e < E - 2:
                    sp.wait_ge(lin_done, end)
                    load_w1(sp, e % 2, e + 2, range(2, 4))
                if e == E - 4:
                    sp.wait_ge(yp_ready, end)
                    load_w2(sp, e + 1)
            sp.wait_ge(lin_done, end)
            sp.wait_ge(yp_ready, end)
            load_w2(sp, E - 1)
            sp.dma_start(gfin, final_norm_g.partition_broadcast(P)).then_inc(tail_in, 16)
            sp.dma_start(b2_sb, b2[0]).then_inc(b2_in, 16)
            sp.wait_ge(all_added, 1)
            for i in range(NT):
                sp.dma_start(fin[:, i, :], acc_t[:, i, :]).then_inc(fin_in[i], 16)
            for i in range(NT):
                sp.wait_ge(y_ok, i + 1)
                if i < 2:
                    sp.dma_start(y_prompt[0, P * i:P * i + P, :], fin[:, i, :]).then_inc(y_out, 16)
                else:
                    sp.dma_start(y_sample.rearrange("b t n -> (b t) n"), fin[0:64, i, :]).then_inc(y_out, 16)
            sp.wait_ge(y_out, 16 * NT)

        @block.scalar
        def _(act):
            step = [0]

            def own(ins):
                step[0] += 1
                ins.then_inc(S["act"], 1)
                act.wait_ge(S["act"], step[0])

            act.dma_start(C[:, :], consts).then_inc(consts_in, 16)
            for i in range(NT):
                if i == 0:
                    act.wait_ge(x_in, 32)
                if i == 2:
                    act.wait_ge(S["pads"], 1)
                act.activation(XTf[:, 0:1024], X[:, i, :], ACT.Square, accum_out=ssq[:, i:i + 1]).then_inc(S["ssq_ok"], 1)
                act.wait_ge(S["ssq_ok"], i + 1)
            act.wait_ge(S["var_ok"], 1)
            act.activation(std, var, ACT.Sqrt).then_inc(S["std_ok"], 1)
            act.wait_ge(S["early_tp"], 1)
            act.copy(par[:, :], PS[:, 7, 0:28]).then_inc(S["par_ok"], 1)
            act.copy(cwT[:, :, :], PS[:, 7, 32:32 + CJ * TAPS].rearrange("p (j t) -> p j t", j=CJ)).then_inc(S["par_ok"], 1)
            for j in range(CJ):
                act.copy(aS[:, j, :, 0:CTX],
                         PS[:, 5 + j // 2, 256 * (j % 2):256 * (j % 2) + 240].rearrange("p (b t) -> p b t", b=NB))\
                    .then_inc(S["st_ok"], 1)
            act.wait_ge(S["par_ok"], 2)
            for k in range(1, KD, 2):
                act.wait_ge(S["xt_tp"], k + 1)
                act.activation(XT[:, k, :], PS[:, k, 0:TPAD], ACT.Copy, scale=par[:, k:k + 1]).then_inc(S["xt_a"], 1)
            def products(n0, n1):
                for n in range(n0, n1):
                    j, t = (1, n) if n < TAPS else (CJ - 1, TAP3 + n - TAPS)
                    first = n in (0, TAPS)
                    dst = prod[:, n % 3, :] if not first else part3 if n else yc[:, 1, :]
                    if n == TAPS:
                        act.wait_ge(S["a_ok"], CJ)
                    if n > 3:
                        act.wait_ge(S["conv_add"], n - 3 - (n - 3 >= TAPS))
                    for d, a in ((dst[:, 0:PROMPT], aP[:, j, t:t + PROMPT]),
                                 (dst[:, PROMPT:TOK].rearrange("p (b t) -> p b t", b=NB), aS[:, j, :, t:t + NS])):
                        if n == 0:
                            last = act.activation(d, a, ACT.Identity, scale=cwT[:, 1, t:t + 1], bias=par[:, 17:18])
                        else:
                            last = act.activation(d, a, ACT.Copy, scale=cwT[:, j, t:t + 1])
                    last.then_inc(S["conv_prod"], 1)

            for j in range(CJ):
                act.wait_ge(S["ug_done"], j + 1)
                if j >= 2:
                    act.wait_ge(S["a_ok"], j - 1)
                act.activation(sg[:, j % 2, :], PS[:, 2 * j + 1, 0:TOK], ACT.Sigmoid).then_inc(S["sg_ok"], 1)
                if j == 1:
                    act.wait_ge(S["a_ok"], 2)
                if j:
                    products(9 * (j - 1), 9 * j if j < 3 else TAPS)
            act.wait_ge(S["kv_done"], 1)
            act.copy(kv[:, :, :], KVP).then_inc(S["kv_ok"], 1)
            done = TAPS
            for g in range(G):
                more = (TAPS - TAP3) * (g + 1) // G
                products(done, TAPS + more)
                done = TAPS + more
                act.wait_ge(S["q_done"], g + 1)
                act.copy(q_sb[:, g, :], PS[:, 2 + g, 0:TOK]).then_inc(S["q_ok"], 1)
            act.wait_ge(S["kc_tp"], 1)
            act.copy(kcT[:, :, :], PS[:, 0:2, :].rearrange("p b n -> p (b n)").rearrange("p (b n) -> p b n", b=NB))\
                .then_inc(S["kc_ok"], 1)
            act.wait_ge(S["kT_tp"], 1)
            act.copy(kT, PS[:, 6, 0:TPAD]).then_inc(S["kT_ok"], 1)
            def square(j):
                act.wait_ge(S["xc_ok"], j + 1)
                if j >= 2:
                    act.wait_ge(S["ln2"], j - 1)
                act.activation(sg[:, j % 2, :], yc[:, j, :], ACT.Square).then_inc(S["sq_ok"], 1)

            for g in range(G):
                act.wait_ge(S["rot_done"], g + 1)
                act.copy(qT[:, g, :], PS[:, 2 + g, 0:PROMPT])
                act.copy(qS[:, :, g, :], PS[:, 2 + g, PROMPT:TOK].rearrange("p (b t) -> p b t", b=NB)).then_inc(S["qT_ok"], 1)
                if g in (1, 2):
                    square(g - 1)
            for j in range(2, CJ):
                square(j)
            act.wait_ge(S["lnv_ok"], 1)
            act.activation(sg[:, 0, :], sg[:, 0, :], ACT.Sqrt).then_inc(S["lns_ok"], 1)
            act.wait_ge(S["conv_add"], 2 * TAPS - TAP3 - 2)
            act.wait_ge(S["ct_tp"], 1)
            act.copy(ct_out[0:CTX, 0:512], PS[0:CTX, 6, :]).then_inc(S["ct_ok"], 1)
            act.wait_ge(S["ct_tp"], 2)
            act.copy(ct_out[0:64, 512:1024], PS[0:64, 5, :]).then_inc(S["ct_ok"], 1)
            for j in range(CJ):
                act.wait_ge(S["z_ok"], j + 1)
                act.activation(mixT[:, G + j, 0:TOK], yc[:, j, :], ACT.Silu, scale=par[:, 20 + j:21 + j],
                               bias=par[:, 24 + j:25 + j]).then_inc(S["mixc_ok"], 1)
            for g, (h, R, K, o, _) in enumerate(GROUPS):
                act.wait_ge(S["nm_ok"], g + 1)
                for r in range(R):
                    s = SALL[:, o + K * r:o + K * r + K]
                    act.activation(s, s, ACT.Exp, bias=nm[:, g, r:r + 1], accum_out=rs[:, g, r:r + 1])
                act.activation(sd[:, g, 0:R], sd[:, g, 0:R], ACT.Exp).then_inc(S["exp_ok"], 1)
                if g >= 4:
                    turned_p(act, act.copy, g - 4).then_inc(S["pt_ok2"], 1)
            for n in range(4, PT_N):
                turned_p(act, act.copy, n).then_inc(S["pt_ok2"], 1)
            for i in range(NT):
                act.wait_ge(S["x2_ok"], 2 * i + 2)
                act.activation(junk2, X[:, i, :], ACT.Square, accum_out=ssq[:, i:i + 1]).then_inc(S["ssq2_ok"], 1)
                act.wait_ge(S["var2_ok"], i + 1)
                act.activation(std[:, i:i + 1], var[:, i:i + 1], ACT.Sqrt).then_inc(S["std2_ok"], 1)
            act.wait_ge(S["d_ok"], 1)
            act.activation(ge, ge, ACT.Exp).then_inc(S["ge_ok"], 1)
            act.wait_ge(S["ohm_ok"], 1)
            for i in range(NT):
                last = act.activation(rhs[:, :, i, 0, :], ohm[:, :, i, :], ACT.Copy, scale=C[:, C_TK + i:C_TK + i + 1])
            last.then_inc(S["rhs_ok"], 1)
            act.wait_ge(S["gt_tp"], 1)
            act.copy(GT[:, :], PS[0:E, 5, 0:TPAD]).then_inc(S["gt_ok"], 1)

            act.wait_ge(S["tab_ok"], 6)
            total = act.value_load(cnt_i[0:1, 2 * E:2 * E + 1], min_val=E, max_val=MAXB - 2)
            with act.Fori(0, total) as m:
                act.wait_ge(g_ready, m + 1)
                act.activation(sig, gate, ACT.Sigmoid, scale=ALPHA).then_inc(sig_ready, 1)
                for c in range(2):
                    act.wait_ge(htp_ready, 2 * m + c + 1)
                    act.copy(hT[:, 2 * c:2 * c + 2], PS[:, 4 + c, 0:256].rearrange("p (s h t) -> p s h t", s=2, h=2))\
                        .then_inc(hT_ready, 1)
                act.wait_ge(y_free, m + 1)
                act.wait_ge(yp_ready, m + 1)
                act.activation(ysb, PS[:, 3, :], ACT.Copy, scale=wtab[:, bass.ds(m, 1)]).then_inc(y_ready, 1)

            for i in range(NT + 1):
                if i < NT:
                    act.wait_ge(fsum, 2 * i + 2)
                    act.activation(junk[:, i, :], fin[:, i, :], ACT.Square, accum_out=ssq[:, i:i + 1]).then_inc(fssq, 1)
                if i:
                    act.wait_ge(fvar, i)
                    act.activation(std[:, i - 1:i], var[:, i - 1:i], ACT.Sqrt).then_inc(fstd, 1)

        @block.tensor
        def _(pe):
            mm = nc.tensor.matmul
            tp = nc.tensor.transpose

            def keep_clock(n):
                for _ in range(n):
                    mm(PS[:, 3, :], ident, b1q[:, :], start=True, stop=True)

            def router(i):
                pe.wait_ge(S["x2_ok"], 2 * i + 2)
                pair = [6, 7]
                if i:
                    pe.wait_ge(S["hT_ok"], i)
                for k in range(KD):
                    last = nc.tensor.transpose(PS[:, pair[k // 4], P * (k % 4):P * (k % 4) + P], X[:, i, P * k:P * k + P], ident)
                last.then_inc(S["h_tp"], 1)
                keep_clock(1)
                pe.wait_ge(S["hT_ok"], i + 1)
                for k in range(KD):
                    last = nc.tensor.matmul(PS[:, 1, E * i:E * i + E], hTr[:, k, :], rw[:, k, :], start=(k == 0), stop=(k == KD - 1))
                last.then_inc(S["lg_done"], 1)

            def turn_x():
                for k in range(KD):
                    last = tp(PS[:, 0, SLOTS * k:SLOTS * k + SLOTS], xg[:, P * k:P * k + P], ident[0:SLOTS, 0:SLOTS])
                last.then_inc(xtp_ready, 1)

            pe.wait_ge(consts_in, 16)
            pe.wait_ge(rows_in, 16 * 7)
            tp(PS[:, 7, 0:28], par_rows, ident[0:28, 0:28])
            for j in range(CJ):
                tp(PS[:, 7, 32 + TAPS * j:32 + TAPS * (j + 1)], cw_rows[:, P * j:P * j + P], ident[0:TAPS, 0:TAPS])
            for j in range(CJ):
                for q in range(2):
                    o = 256 * (j % 2) + 120 * q
                    last = tp(PS[:, 5 + j // 2, o:o + 120], st_rows[:, q, P * j:P * j + P], ident[0:120, 0:120])
            last.then_inc(S["early_tp"], 1)
            pe.wait_ge(S["xn_ok"], NT)
            for k in range(KD):
                if k == 4:
                    pe.wait_ge(S["st_ok"], CJ)
                    pe.wait_ge(S["par_ok"], 2)
                for i in range(NT):
                    last = tp(PS[:, k, P * i:P * i + P], xn[:, i, P * k:P * k + P], ident)
                last.then_inc(S["xt_tp"], 1)
            pe.wait_ge(S["xt_v"], KD // 2)
            pe.wait_ge(S["xt_a"], KD // 2)
            for j in range(CJ):
                if j % 2 == 0:
                    pe.wait_ge(ug_in[j // 2], 32)
                for n, o in enumerate((768, 1280)):
                    for k in range(KD):
                        last = mm(PS[:, 2 * j + n, 0:TOK], win[:, k, o + P * j:o + P * j + P], XT[:, k, 0:TOK],
                                  start=(k == 0), stop=(k == KD - 1))
                last.then_inc(S["ug_done"], 1)
            pe.wait_ge(kv_in, 16)
            pe.wait_ge(S["a_ok"], 1)
            for i in range(NT):
                for k in range(KD):
                    last = mm(KVP[:, i, :], XT[:, k, P * i:P * i + P], win[:, k, 512:768], start=(k == 0), stop=(k == KD - 1))
            last.then_inc(S["kv_done"], 1)
            pe.wait_ge(q_in, 16)
            for g in range(G):
                pe.wait_ge(S["a_ok"], (2 + g) // 2 + 1)
                for k in range(KD):
                    for h in range(2):
                        o = 256 * h + 64 * g
                        last = mm(PS[64 * h:64 * h + 64, 2 + g, 0:TOK], win[:, k, o:o + 64], XT[:, k, 0:TOK],
                                  start=(k == 0), stop=(k == KD - 1))
                last.then_inc(S["q_done"], 1)
            pe.wait_ge(caches_in, 16 * 3)
            pe.wait_ge(S["kv_ok"], 1)
            for b in range(NB):
                last = tp(PS[:, b // 4, P * (b % 4):P * (b % 4) + P], ck_rows[:, b, :], ident)
            last.then_inc(S["kc_tp"], 1)
            pe.wait_ge(S["krot_ok"], 1)
            for i in range(NT):
                last = tp(PS[:, 6, P * i:P * i + P], kv[:, i, 0:P], ident)
            last.then_inc(S["kT_tp"], 1)
            pe.wait_ge(S["conv_ok"], CJ)
            pe.wait_ge(S["a_ok"], CJ)
            for j in range(CJ):
                last = mm(PS[:, 7, 0:TOK], ones, yc[:, j, :], start=(j == 0), stop=(j == CJ - 1))
            last.then_inc(S["ln1"], 1)
            for g in range(G):
                pe.wait_ge(S["rq_ok"], g + 1)
                mm(PS[:, 2 + g, 0:TOK], ident, q_sb[:, g, :], start=True, stop=False)
                mm(PS[:, 2 + g, 0:TOK], C[:, C_ROT:C_ROT + P], rq_sb[:, g, :], start=False, stop=True).then_inc(S["rot_done"], 1)
            pe.wait_ge(S["kT_ok"], 1)
            for j in range(CJ):
                last = tp(PS[0:CTX, 6, P * j:P * j + P], aP[:, j, PROMPT:PROMPT + CTX], ident)
            last.then_inc(S["ct_tp"], 1)
            pe.wait_ge(S["qT_ok"], G)
            pe.wait_ge(S["an_ok"], CJ)
            for j in range(CJ):
                last = tp(PS[0:64, 5, P * j:P * j + P], a_new[:, j, :], ident)
            last.then_inc(S["ct_tp"], 1)
            pe.wait_ge(S["xc_ok"], CJ)
            for j in range(CJ):
                pe.wait_ge(S["sq_ok"], j + 1)
                mm(PS[:, 7, 0:TOK], ones, sg[:, j % 2, :], start=(j == 0), stop=(j == CJ - 1)).then_inc(S["ln2"], 1)
            pe.wait_ge(S["qT_ok"], G)
            pe.wait_ge(S["kT_ok"], 1)
            pe.wait_ge(S["kc_ok"], 1)
            pe.wait_ge(S["qT_ok"], G)
            for n, (h, R, K, o, bank) in enumerate(GROUPS):
                hp = slice(64 * h, 64 * h + 64)
                if n == 3:
                    pe.wait_ge(S["ct_ok"], 2)
                if n < 4:
                    blk = n // 2
                    out = PS[:, bank:bank + 2, :].rearrange("p b n -> p (b n)") if blk else PS[:, bank, :]
                    for g in range(G):
                        last = mm(out[:, K * g:K * g + K], qT[hp, g, W * blk:W * blk + W], kT[hp, 0:K], start=True, stop=True)
                else:
                    if n == 5:
                        pe.wait_ge(S["lnv_ok"], 1)
                    for q in range(2):
                        for b in range(4):
                            mm(PS[32 * b:32 * b + 32, bank, 192 * q:192 * q + W],
                               qS[hp, 4 * q + b].rearrange("p g t -> p (g t)"),
                               kcT[hp, 4 * q + b, :], start=True, stop=True)
                    for q in range(2):
                        last = mm(PS[:, bank, 192 * q + W:192 * q + 192],
                                  qS[hp, 4 * q:4 * q + 4].rearrange("p b g t -> p (b g t)"),
                                  kT[hp, PROMPT:TOK], start=True, stop=True)
                last.then_inc(S["s_done"], 1)
            def turn_p(n):
                g, kb = PT_ORDER[n]
                _, R, K, o, _ = GROUPS[g]
                pe.wait_ge(S["p_ok"], g + 1)
                if n < 4:
                    pe.wait_ge(S["s_evac"], n + 1 if n < 2 else n + 3)
                elif n < 6:
                    pe.wait_ge(S["pt_ok"], n - 3)
                else:
                    pe.wait_ge(S["pt_ok2"], n - 3)
                b = PT_BANK[n]
                if g < 4:
                    for r in range(R):
                        last = tp(PS[:, b, P * r:P * r + P], SALL[:, o + K * r + P * kb:o + K * r + P * kb + P], ident)
                else:
                    for q in range(2):
                        tp(PS[:, b, P * q:P * q + P], SALL[:, o + K * q:o + K * q + P], ident)
                        last = tp(PS[0:64, b, 256 + P * q:256 + P * q + P], SALL[:, o + K * q + P:o + K * q + 192], ident)
                last.then_inc(S["pt_done"], 1)

            def wait_turned(n):
                if n in (2, 3):
                    pe.wait_ge(S["pt_ok"], n - 1)
                else:
                    pe.wait_ge(S["pt_ok2"], n + 1 if n < 2 else n - 1)

            def values(n, bank, first_kb, last_kb):
                g, kb = PT_ORDER[n]
                h, o = GROUPS[g][0], GROUPS[g][3]
                hp = slice(64 * h, 64 * h + 64)
                wait_turned(n)
                return mm(PS[hp, bank, :], kv[:, kb, P + 64 * h:P + 64 * h + 64], SALL[:, o + 512 * kb:o + 512 * kb + 512],
                          start=first_kb, stop=last_kb)

            def out_projection(i, ks, ns=range(2)):
                for n in ns:
                    for k in ks:
                        last = mm(PS[:, OB[i][n], :], mixT[:, k, P * i:P * i + P], wout[:, k, 512 * n:512 * n + 512],
                                  start=(k == G), stop=(k == G - 1))
                return last

            pe.wait_ge(wout2_in, 16)
            pe.wait_ge(S["mixc_ok"], CJ)
            pe.wait_ge(S["s_evac"], 3)
            out_projection(0, range(G, KD))
            for n in range(2):
                turn_p(n)
            pe.wait_ge(S["s_evac"], 4)
            out_projection(1, range(G, KD), [0])
            for n in range(2):
                values(n, 0, True, True).then_inc(S["o_done"], 1)
            for n in range(2, 4):
                turn_p(n)
            out_projection(1, range(G, KD), [1])
            for n in range(2, 4):
                last = values(n, 1, n == 2, n == 3)
            last.then_inc(S["o_done"], 1)
            for n in range(4, 6):
                turn_p(n)
            for n in range(4, 6):
                last = values(n, 1, n == 4, n == 5)
            last.then_inc(S["o_done"], 1)
            for n in range(6, 8):
                turn_p(n)
            pe.wait_ge(S["o_ok"], 1)
            for n in range(6, 8):
                g, _ = PT_ORDER[n]
                h, o = GROUPS[g][0], GROUPS[g][3]
                hp = slice(64 * h, 64 * h + 64)
                wait_turned(n)
                for q in range(2):
                    mm(PS[hp, 0, P * q:P * q + P], kv[0:64, 2, P + 64 * h:P + 64 * h + 64],
                       SALL[0:64, o + 256 + P * q:o + 256 + P * q + P], start=True, stop=False, skip_group_check=True)
                    for b in range(4):
                        last = mm(PS[hp, 0, P * q + 32 * b:P * q + 32 * b + 32], cv_rows[:, 4 * q + b, 64 * h:64 * h + 64],
                                  SALL[:, o + P * q + 32 * b:o + P * q + 32 * b + 32], start=False, stop=(b == 3),
                                  skip_group_check=True)
                last.then_inc(S["o_done"], 1)
            pe.wait_ge(wout_in, 32)
            pe.wait_ge(late_in, 32)
            pe.wait_ge(b1_in, 16)
            pe.wait_ge(S["o_ok"], 4)
            for i in range(NT):
                if i < 2:
                    last = out_projection(i, range(G))
                else:
                    for k in range(KD):
                        for n in range(2):
                            last = mm(PS[64 * n:64 * n + 64, 0, :], mixT[:, k, PROMPT:TOK], wout[:, k, 512 * n:512 * n + 512],
                                      start=(k == 0), stop=(k == KD - 1))
                last.then_inc(S["op_done"], 1)
                if i >= 1:
                    router(i - 1)
            router(NT - 1)
            pe.wait_ge(S["m_ok"], 1)
            mm(PS[:, 0, 0:E * (NT + 1)], ones, cum[:, :, :].rearrange("p i e -> p (i e)"), start=True, stop=False, skip_group_check=True)
            last = mm(PS[:, 0, 0:E * NT], C[:, C_UP:C_UP + P], Mm[:, :, :].rearrange("p i e -> p (i e)"), start=False, stop=True,
                      skip_group_check=True)
            last.then_inc(S["rk_done"], 1)
            keep_clock(8)
            pe.wait_ge(S["route_ok"], 1)
            pe.wait_ge(S["rhs_ok"], 1)
            for n in range(TOPK * NT):
                k, i = n // NT, n % NT
                for h in range(2):
                    last = mm(PS[64 * h:64 * h + 64, 1, 0:2 * MAXB], ohs[:, k, i, :], rhs[:, k, i, :, :].rearrange("p v m -> p (v m)"),
                              start=(n == 0), stop=(n == TOPK * NT - 1))
            last.then_inc(S["tab_done"], 1)
            pe.wait_ge(S["g_ok"], 1)
            for i in range(NT):
                last = tp(PS[0:E, 5, P * i:P * i + P], Gg[:, i, :], ident)
            last.then_inc(S["gt_tp"], 1)
            keep_clock(6)

            pe.wait_ge(S["tab_ok"], 6)
            pe.wait_ge(xg_ready, 16)
            turn_x()
            with pe.Fori(0, E // 2) as i:
                for u in range(2):
                    nblk = pe.value_load(cnt_i[0:1, bass.ds(2 * i + u, 1)], min_val=1, max_val=XB + 1)
                    at = pe.value_load(cnt_i[0:1, bass.ds(E + 2 * i + u, 1)], min_val=0, max_val=MAXB - 3)
                    with pe.Fori(0, nblk) as b:
                        m = at + b
                        pe.wait_ge(xT_ready, m + 1)
                        pe.wait_ge(sel_ready, 2 * i + u + 1)
                        for s, done in ((0, gate_done), (1, lin_done)):
                            if s:
                                pe.wait_ge(xg_ready, 16 * m + 32)
                                pe.sem_inc(turned, 1)
                                turn_x()
                            for n in range(2):
                                mm(PS[64 * n:64 * n + 64, 1 + s, :], sel[:, 2 * s + n, :], b1q[:, :], start=True, stop=False)
                            for k in range(KD):
                                c = 2 * s + k // 4
                                if k % 4 == 0:
                                    pe.wait_ge(w1_in[u][c], 16 * i + 16)
                                for n in range(2):
                                    last = mm(PS[64 * n:64 * n + 64, 1 + s, :], xTe[:, SLOTS * k:SLOTS * k + SLOTS],
                                              w1buf[u][:, c, k % 4, 512 * n:512 * n + 512], start=False, stop=(k == KD - 1))
                                if s == 0 and k == 3:
                                    last.then_inc(gate_half, 1)
                            last.then_inc(done, 1)
                        for c in range(2):
                            pe.wait_ge(h_ready, 2 * m + c + 1)
                            for s in range(2):
                                o = P * (2 * c + s)
                                last = tp(PS[:, 4 + c, P * s:P * s + P], act_h[:, o:o + P], ident)
                            last.then_inc(htp_ready, 1)
                        for c in range(2):
                            pe.wait_ge(w2_in[c], 16 * (2 * i + u) + 16)
                        for s in range(4):
                            if s % 2 == 0:
                                pe.wait_ge(hT_ready, 2 * m + s // 2 + 1)
                            for h in range(2):
                                for n in range(2):
                                    last = mm(PS[64 * n:64 * n + 64, 3, :], hT[:, s, h, :], w2buf[:, 4 * h + s, 512 * n:512 * n + 512],
                                              start=(s == 0 and h == 0), stop=(s == 3 and h == 1))
                        last.then_inc(yp_ready, 1)
            pe.wait_ge(S["gt_ok"], 1)
            pe.wait_ge(b2_in, 16)
            for i in range(NT):
                for n in range(2):
                    last = mm(PS[:, BB[i][n], :], GT[:, P * i:P * i + P], b2_sb[:, 512 * n:512 * n + 512], start=True, stop=True)
                last.then_inc(b2_done, 1)


        @block.vector
        def _(dve):
            v = nc.vector
            step = [0]

            def own(ins):
                step[0] += 1
                ins.then_inc(S["vec"], 1)
                dve.wait_ge(S["vec"], step[0])

            v.memset(X[64:128, 2, :], 0.0).then_inc(S["pads"], 1)
            v.memset(aP[:, :, 0:CTX], 0.0).then_inc(S["pad_ok"], 1)
            dve.wait_ge(S["ssq_ok"], NT)
            v.tensor_scalar(var, ssq, 1.0 / D, EPS, ALU.mult, ALU.add).then_inc(S["var_ok"], 1)
            dve.wait_ge(S["std_ok"], 1)
            own(v.reciprocal(rstd, std))
            dve.wait_ge(x_in, 32)
            for i in range(NT):
                v.tensor_scalar(xn[:, i, :], X[:, i, :], rstd[:, i:i + 1], None, ALU.mult).then_inc(S["xn_ok"], 1)
            dve.wait_ge(S["par_ok"], 2)
            for k in range(0, KD, 2):
                dve.wait_ge(S["xt_tp"], k + 1)
                v.tensor_scalar(XT[:, k, :], PS[:, k, 0:TPAD], par[:, k:k + 1], None, ALU.mult).then_inc(S["xt_v"], 1)
            dve.wait_ge(S["pad_ok"], 1)
            dve.wait_ge(S["st_ok"], CJ)
            ys = yc[:, :, PROMPT:TOK].rearrange("p j (b t) -> p j b t", b=NB)

            def gated(j):
                dve.wait_ge(S["sg_ok"], j + 1)
                v.tensor_tensor(aP[:, j, CTX:CTX + PROMPT], PS[:, 2 * j, 0:PROMPT], sg[:, j % 2, 0:PROMPT], ALU.mult)
                v.tensor_tensor(aS[:, j, :, CTX:CTX + NS], PS[:, 2 * j, PROMPT:TOK].rearrange("p (b t) -> p b t", b=NB),
                                sg[:, j % 2, PROMPT:TOK].rearrange("p (b t) -> p b t", b=NB), ALU.mult).then_inc(S["a_ok"], 1)

            gated(0)
            for j in (0, 2, 3):
                dve.wait_ge(S["a_ok"], j + 1)
                taps = TAP3 if j == CJ - 1 else TAPS
                for t in range(taps):
                    pin, sin = aP[:, j, t:t + PROMPT], aS[:, j, :, t:t + NS]
                    w = cwT[:, j, t:t + 1]
                    if t == 0:
                        bias = par[:, 16 + j:17 + j]
                        v.tensor_scalar(yc[:, j, 0:PROMPT], pin, w, bias, ALU.mult, ALU.add).then_inc(S["vec"], 1)
                        v.tensor_scalar(ys[:, j], sin, w, bias, ALU.mult, ALU.add).then_inc(S["vec"], 1)
                    else:
                        last = t == TAPS - 1
                        dve.wait_ge(S["vec"], step[0] - 1)
                        v.scalar_tensor_tensor(yc[:, j, 0:PROMPT], pin, w, yc[:, j, 0:PROMPT], ALU.mult, ALU.add)\
                            .then_inc(S["vec"], 1)
                        dve.wait_ge(S["vec"], step[0])
                        v.scalar_tensor_tensor(ys[:, j], sin, w, ys[:, j], ALU.mult, ALU.add)\
                            .then_inc(S["conv_ok"] if last else S["vec"], 1)
                        if last:
                            step[0] -= 1
                    step[0] += 2
                    if j == 0 and t in (12, 26):
                        gated(1 if t == 12 else 2)
                    if j == 2 and t == 12:
                        gated(3)
            dve.wait_ge(S["vec"], step[0])
            dve.wait_ge(S["part_ok"], 1)
            v.tensor_tensor(yc[:, CJ - 1, :], yc[:, CJ - 1, :], part3, ALU.add).then_inc(S["conv_ok"], 1)
            dve.wait_ge(aconsts_in, 16)
            dve.wait_ge(caches_in, 16 * 3)
            for n in range(4):
                v.tensor_copy(sinks[:, n, :], sinks8[:, 4 * (n % 2):4 * (n % 2) + 4])
            own(v.tensor_tensor(picked, sinks8.rearrange("p (h g) -> p h g", h=2),
                                C[:, C_SG:C_SG + G].unsqueeze(1).to_broadcast([P, 2, G]), ALU.mult))
            for n in range(2):
                last = v.tensor_reduce(sinks[:, 4:6, n], picked, AX.X, ALU.add)
            own(last)

            dve.wait_ge(S["ln1"], 1)
            for j in range(CJ):
                v.scalar_tensor_tensor(yc[:, j, :], PS[:, 7, 0:TOK], -1.0 / CW, yc[:, j, :], ALU.mult, ALU.add)\
                    .then_inc(S["xc_ok"], 1)
            dve.wait_ge(S["ln2"], CJ)
            v.tensor_scalar(sg[:, 0, :], PS[:, 7, 0:TOK], 1.0 / CW, EPS, ALU.mult, ALU.add).then_inc(S["lnv_ok"], 1)
            dve.wait_ge(S["lns_ok"], 1)
            own(v.reciprocal(sg[:, 1, :], sg[:, 0, :]))
            dve.wait_ge(S["xc_ok"], CJ)
            for j in range(CJ):
                v.tensor_tensor(yc[:, j, :], yc[:, j, :], sg[:, 1, :], ALU.mult).then_inc(S["z_ok"], 1)
            def scores(g):
                h, R, K, o, bank = GROUPS[g]
                s = SALL[:, o:o + R * K].rearrange("p (r k) -> p r k", r=R)
                dve.wait_ge(S["s_done"], g + 1)
                if g < 4:
                    src = PS[:, bank:bank + 2, :].rearrange("p b n -> p (b n)")[:, 0:R * K].rearrange("p (r k) -> p r k", r=R)
                    mask = A[:, A_MP + 2 * W - K:A_MP + 2 * W].unsqueeze(1).to_broadcast([P, R, K])
                else:
                    src = PS[:, bank, 0:R * K].rearrange("p (r k) -> p r k", r=R)
                    mask = A[:, A_MS:A_MS + 384].rearrange("p (r k) -> p r k", r=2)
                v.tensor_tensor(s, src, mask, ALU.add).then_inc(S["s_evac"], 1)
                dve.wait_ge(S["s_evac"], g + 1)
                own(v.tensor_reduce(mx[:, g, 0:R], s, AX.X, ALU.max))
                own(v.tensor_tensor(mx[:, g, 0:R], mx[:, g, 0:R], sinks[:, g, 0:R], ALU.max))
                v.tensor_tensor(sd[:, g, 0:R], sinks[:, g, 0:R], mx[:, g, 0:R], ALU.subtract)
                v.tensor_scalar(nm[:, g, 0:R], mx[:, g, 0:R], -1.0, None, ALU.mult).then_inc(S["nm_ok"], 1)
            def probs(g):
                h, R, K, o, bank = GROUPS[g]
                s = SALL[:, o:o + R * K].rearrange("p (r k) -> p r k", r=R)
                dve.wait_ge(S["exp_ok"], g + 1)
                own(v.tensor_tensor(den[:, g, 0:R], rs[:, g, 0:R], sd[:, g, 0:R], ALU.add))
                own(v.reciprocal(den[:, g, 0:R], den[:, g, 0:R]))
                v.tensor_tensor(s, s, bc(den[:, g, 0:R], K), ALU.mult).then_inc(S["p_ok"], 1)
            for g in range(len(GROUPS)):
                scores(g)
                if g >= 2:
                    probs(g - 2)
            for g in range(4, 6):
                probs(g)
            for n in range(2, 4):
                turned_p(dve, v.tensor_copy, n).then_inc(S["pt_ok"], 1)
            for n, bank in enumerate((0, 1)):
                dve.wait_ge(S["o_done"], 2 * n + 2)
                v.tensor_copy(mixT[:, 0:G, W * n:W * n + W], PS[:, bank, :].rearrange("p (g t) -> p g t", g=G)).then_inc(S["o_ok"], 1)
            dve.wait_ge(S["o_done"], 6)
            for q in range(2):
                t0 = PROMPT + 32 * q
                v.tensor_copy(mixT[:, 0:G, t0:t0 + 32].rearrange("p g (b t) -> p b g t", b=4),
                              PS[:, 0, P * q:P * q + P].rearrange("p (b g t) -> p b g t", b=4, g=G)).then_inc(S["o_ok"], 1)
            dve.wait_ge(new_out, 16 * OUTS)

            def top(i):
                dve.wait_ge(S["lg_done"], i + 1)
                own(v.scalar_tensor_tensor(lg[:, i, :], PS[:, 1, E * i:E * i + E], rstd[:, i:i + 1], rb[:, :], ALU.mult, ALU.add))
                own(v.max(v8[:, i, :], lg[:, i, :]))
                v.max_index(i8[:, i, :], v8[:, i, :], lg[:, i, :]).then_inc(S["vec"], 1)
                step[0] += 1

            def finish_rows(i):
                for n in range(2):
                    x = X[:, i, 512 * n:512 * n + 512] if i < 2 else X[0:64, i, 512 * n:512 * n + 512]
                    v.tensor_tensor(x, PS[:, OB[i][n], :] if i < 2 else PS[64 * n:64 * n + 64, 0, :], x, ALU.add)\
                        .then_inc(S["x2_ok"], 1)
                dve.wait_ge(S["ssq2_ok"], i + 1)
                v.tensor_scalar(var[:, i:i + 1], ssq[:, i:i + 1], 1.0 / D, EPS, ALU.mult, ALU.add).then_inc(S["var2_ok"], 1)
                if i:
                    top(i - 1)
                dve.wait_ge(S["h_tp"], i + 1)
                if i:
                    dve.wait_ge(S["lg_done"], i)
                v.tensor_tensor(hTr[:, :, :], PS[:, 6:8, :].rearrange("p b (k t) -> p (b k) t", k=4), bc(par[:, 8:16], P), ALU.mult)\
                    .then_inc(S["hT_ok"], 1)
                dve.wait_ge(S["std2_ok"], i + 1)
                own(v.reciprocal(rstd[:, i:i + 1], std[:, i:i + 1]))
                if i == 2:
                    dve.wait_ge(h_out[0], 16)
                v.tensor_scalar(Hs(i), X[:, i, :], rstd[:, i:i + 1], None, ALU.mult).then_inc(S["h_ok"], 1)

            for i in range(NT):
                dve.wait_ge(S["op_done"], i + 1)
                finish_rows(i)
            top(NT - 1)
            dve.wait_ge(S["vec"], step[0])
            v.tensor_tensor(ge, v8[:, :, 0:TOPK], v8[:, :, 0:1].to_broadcast([P, NT, TOPK]), ALU.subtract).then_inc(S["d_ok"], 1)
            own(v.tensor_copy(idf, i8[:, :, 0:TOPK]))
            own(v.tensor_tensor(idf, idf, bc(C[:, C_PAD:C_PAD + NT], TOPK), ALU.add))
            def per_choice(ap):
                return ap.unsqueeze(1).to_broadcast([P, TOPK, *ap.shape[1:]])

            own(v.tensor_tensor(oh, C[:, C_IE:C_IE + E].unsqueeze(1).unsqueeze(1).to_broadcast([P, TOPK, NT, E]),
                                bc(idf.rearrange("p i k -> p k i"), E), ALU.is_equal))
            v.tensor_tensor(tmp4[:, 0], oh[:, 0], oh[:, 1], ALU.add)
            own(v.tensor_tensor(tmp4[:, 1], oh[:, 2], oh[:, 3], ALU.add))
            v.memset(cum[:, 0, :], 0.0)
            own(v.tensor_tensor(Mm, tmp4[:, 0], tmp4[:, 1], ALU.add))
            v.tensor_copy(cum[:, 1, :], Mm[:, 0, :])
            own(v.tensor_tensor(cum[:, 2, :], Mm[:, 0, :], Mm[:, 1, :], ALU.add))
            v.tensor_tensor(cum[:, 3, :], cum[:, 2, :], Mm[:, 2, :], ALU.add).then_inc(S["m_ok"], 1)
            dve.wait_ge(S["m_ok"], 1)
            dve.wait_ge(S["ge_ok"], 1)
            own(v.tensor_reduce(gs, ge, AX.X, ALU.add))
            own(v.reciprocal(gs, gs))
            own(v.tensor_tensor(ge, ge, bc(gs, TOPK), ALU.mult))
            dve.wait_ge(S["rk_done"], 1)
            v.memset(zero, 0.0)
            v.tensor_copy(rc[:, 0:NT * E], PS[:, 0, 0:NT * E])
            own(v.tensor_scalar(rc[:, NT * E:], PS[:, 0, NT * E:(NT + 1) * E], -1.0, None, ALU.add))
            own(v.tensor_scalar(fc, rc, float(SLOTS), None, ALU.is_ge))
            for b in range(2, XB + 1):
                own(v.scalar_tensor_tensor(fc, rc, float(SLOTS * b), fc, ALU.is_ge, ALU.add))
            own(v.tensor_scalar(nb, fc[:, NT * E:], 1.0, None, ALU.add))
            own(v.tensor_tensor_scan(inc, nb, zero, 0.0, ALU.add, ALU.add))
            own(v.tensor_tensor(first, inc, nb, ALU.subtract))
            v.tensor_copy(cnt_i[0:1, 0:E], nb[0:1, :]).then_inc(S["tab_ok"], 1)
            v.tensor_copy(cnt_i[0:1, E:2 * E], first[0:1, :]).then_inc(S["tab_ok"], 1)
            v.tensor_copy(cnt_i[0:1, 2 * E:2 * E + 1], inc[0:1, E - 1:E]).then_inc(S["tab_ok"], 1)
            v.tensor_tensor(bk, fl, first.unsqueeze(1).to_broadcast([P, NT, E]), ALU.add)
            own(v.scalar_tensor_tensor(rk, fl, -float(SLOTS), rk, ALU.mult, ALU.add))
            own(v.tensor_tensor(tmp4, oh, per_choice(bk), ALU.mult))
            own(v.tensor_reduce(mk, tmp4[:, :, :, :], AX.X, ALU.add))
            own(v.tensor_tensor(tmp4, oh, per_choice(rk), ALU.mult))
            v.tensor_reduce(sk, tmp4[:, :, :, :], AX.X, ALU.add)
            own(v.tensor_tensor(mk, mk, C[:, C_PAD:C_PAD + NT].unsqueeze(1).to_broadcast([P, TOPK, NT]), ALU.add))
            dve.wait_ge(added, 16)
            dve.wait_ge(acc_init, 16 * (NT - 1))
            v.tensor_tensor(ohm, C[:, C_IM:C_IM + MAXB].unsqueeze(1).unsqueeze(1).to_broadcast([P, TOPK, NT, MAXB]),
                            bc(mk, MAXB), ALU.is_equal).then_inc(S["ohm_ok"], 1)
            v.tensor_tensor(ohs, C[:, C_IS:C_IS + SLOTS].unsqueeze(1).unsqueeze(1).to_broadcast([P, TOPK, NT, SLOTS]),
                            bc(sk, SLOTS), ALU.is_equal)
            dve.wait_ge(S["ohm_ok"], 1)
            last = v.tensor_tensor(rhs[:, :, :, 1, :], ohm, bc(ge.rearrange("p i k -> p k i"), MAXB), ALU.mult)
            last.then_inc(S["route_ok"], 1)
            own(v.tensor_tensor(tmp4, oh, bc(ge.rearrange("p i k -> p k i"), E), ALU.mult))
            v.tensor_reduce(Gg, tmp4[:, :, :, :].rearrange("p k i e -> p i e k"), AX.X, ALU.add).then_inc(S["g_ok"], 1)
            dve.wait_ge(S["g_ok"], 1)
            dve.wait_ge(S["tab_done"], 1)
            v.tensor_copy(wtab[:, :], PS[:, 1, MAXB:2 * MAXB]).then_inc(S["tab_ok"], 1)
            own(v.tensor_copy(t1, PS[:, 1, 0:MAXB]))
            v.tensor_scalar(inv, t1, 0.0, C[:, C_S1:C_S1 + 1], ALU.is_equal, ALU.mult)
            v.tensor_scalar(gtab[:, :], t1[0:SLOTS], -1.0, 0.0, ALU.add, ALU.max).then_inc(S["tab_ok"], 1)
            own(v.tensor_scalar(t2, t1, 2.0, C[:, C_S2:C_S2 + 1], ALU.mult, ALU.add))
            v.tensor_tensor(stab[:, :], t2, inv, ALU.add).then_inc(S["tab_ok"], 1)
            dve.wait_ge(S["tab_ok"], 6)

            def gain_x():
                v.tensor_tensor(xTe.rearrange("p (k s) -> p k s", k=KD), PS[:, 0, :].rearrange("p (k s) -> p k s", k=KD),
                                bc(par[:, 8:16], SLOTS), ALU.mult).then_inc(xT_ready, 1)

            dve.wait_ge(xtp_ready, 1)
            gain_x()
            with dve.Fori(0, E) as e:
                v.tensor_copy(sel, bc(C[:, bass.ds(4 * e + C_ID, 4)], SLOTS)).then_inc(sel_ready, 1)
                nblk = dve.value_load(cnt_i[0:1, bass.ds(e, 1)], min_val=1, max_val=XB + 1)
                at = dve.value_load(cnt_i[0:1, bass.ds(E + e, 1)], min_val=0, max_val=MAXB - 3)
                with dve.Fori(0, nblk) as b:
                    m = at + b
                    dve.wait_ge(gate_done, m + 1)
                    v.tensor_scalar(gate, PS[:, 1, :], LIMIT, None, ALU.min).then_inc(g_ready, 1)
                    dve.wait_ge(sig_ready, m + 1)
                    v.tensor_tensor(swi, gate, sig, ALU.mult).then_inc(vstep, 1)
                    dve.wait_ge(lin_done, m + 1)
                    for c in range(2):
                        o = slice(256 * c, 256 * c + 256)
                        v.tensor_scalar(lin[:, o], PS[:, 2, o], LIMIT, -LIMIT, ALU.min, ALU.max).then_inc(vstep, 1)
                    for c in range(2):
                        o = slice(256 * c, 256 * c + 256)
                        dve.wait_ge(vstep, 3 * m + c + 2)
                        v.scalar_tensor_tensor(act_h[:, o], lin[:, o], 1.0, swi[:, o], ALU.add, ALU.mult).then_inc(h_ready, 1)
                    dve.wait_ge(xtp_ready, m + 2)
                    gain_x()

            def add_b2(i):
                dve.wait_ge(fin_in[i], 16)
                dve.wait_ge(b2_done, i + 1)
                for n in range(2):
                    f = fin[:, i, 512 * n:512 * n + 512]
                    v.tensor_tensor(f, PS[:, BB[i][n], :], f, ALU.add).then_inc(fsum, 1)

            dve.wait_ge(tail_in, 16)
            add_b2(0)
            for i in range(NT):
                if i + 1 < NT:
                    add_b2(i + 1)
                dve.wait_ge(fssq, i + 1)
                v.tensor_scalar(var[:, i:i + 1], ssq[:, i:i + 1], 1.0 / D, EPS, ALU.mult, ALU.add).then_inc(fvar, 1)
                dve.wait_ge(fstd, i + 1)
                own(v.reciprocal(rstd[:, i:i + 1], std[:, i:i + 1]))
                v.scalar_tensor_tensor(fin[:, i, :], fin[:, i, :], rstd[:, i:i + 1], gfin, ALU.mult, ALU.mult).then_inc(y_ok, 1)

        @block.gpsimd
        def _(pool):
            g = nc.gpsimd
            pool.wait_ge(S["ug_done"], 1)
            for src, dst in ((cache_k, nk_s), (cache_v, nv_s)):
                pool.dma_start(dst[0, :, 0:W - NS].rearrange("b w h d -> b (w h d)"),
                               src[0, :, NS:W].rearrange("b w h d -> b (w h d)")).then_inc(out_done, 16)
            pool.dma_start(nc_s[0, :, 0:CTX - NS, :].rearrange("b t n -> b (t n)"),
                           state_conv[0, :, NS:CTX, :].rearrange("b t n -> b (t n)")).then_inc(out_done, 16)
            sums = [0]

            def add_product(n):
                pool.wait_ge(S["conv_prod"], n + 1)
                if sums[0]:
                    pool.wait_ge(S["conv_add"], sums[0])
                dst = yc[:, 1, :] if n < TAPS else part3
                g.tensor_tensor(dst, dst, prod[:, n % 3, :], ALU.add).then_inc(S["conv_add"], 1)
                sums[0] += 1

            for n in range(1, TAPS):
                add_product(n)
            pool.wait_ge(S["conv_add"], sums[0])
            pool.sem_inc(S["conv_ok"], 1)
            for j in range(CJ):
                pool.wait_ge(S["a_ok"], j + 1)
                g.tensor_copy(a_new[:, j, :].rearrange("p (b t) -> p b t", b=NB), aS[:, j, :, CTX:CTX + NS]).then_inc(S["an_ok"], 1)
            pool.wait_ge(aconsts_in, 16)
            pool.wait_ge(S["kv_ok"], 1)
            k4 = kv[:, :, 0:P].rearrange("p i (h d) -> p i h d", h=2)
            x1, x2 = k4[:, :, :, 0:8], k4[:, :, :, 8:16]
            cs, sn = (A[:, o:o + 24].rearrange("p (i d) -> p i d", i=NT).unsqueeze(2).to_broadcast([P, NT, 2, 8]) for o in (A_CK, A_SK))
            for n, (a, c) in enumerate(((x1, cs), (x2, sn), (x2, cs), (x1, sn))):
                g.tensor_tensor(krt[:, n], a, c, ALU.mult).then_inc(S["pool"], 1)
            pool.wait_ge(S["pool"], 4)
            g.tensor_tensor(x1, krt[:, 0], krt[:, 1], ALU.subtract).then_inc(S["pool"], 1)
            pool.wait_ge(S["pool"], 5)
            g.tensor_tensor(x2, krt[:, 2], krt[:, 3], ALU.add).then_inc(S["krot_ok"], 1)
            n = TAPS + 1
            for h in range(G):
                while n < TAPS + 1 + (2 * TAPS - TAP3 - TAPS - 1) * (h + 1) // G:
                    add_product(n)
                    n += 1
                pool.wait_ge(S["q_ok"], h + 1)
                g.tensor_tensor(rq_sb[:, h, :], q_sb[:, h, :], A[:, A_SIN:A_SIN + TOK], ALU.mult).then_inc(S["pool"], 1)
                g.tensor_tensor(q_sb[:, h, :], q_sb[:, h, :], A[:, A_COS:A_COS + TOK], ALU.mult).then_inc(S["rq_ok"], 1)
            pool.wait_ge(S["conv_add"], sums[0])
            pool.sem_inc(S["part_ok"], 1)
            pool.wait_ge(out_done, 16 * 3)
            pool.sem_inc(turn, 1)
            for i in range(NT):
                pool.wait_ge(S["x2_ok"], 2 * i + 2)
                pool.dma_start(acc_t[:, i, :], X[:, i, :]).then_inc(acc_init if i < NT - 1 else added, 16)
                pool.wait_ge(S["h_ok"], i + 1)
                pool.dma_start(h_dram[P * i:P * i + P, :], Hs(i)).then_inc(h_out[i], 16)

            pool.wait_ge(S["tab_ok"], 6)
            for i in range(NT):
                pool.wait_ge(h_out[i], 16)
            pool.wait_ge(acc_init, 16 * (NT - 1))
            total = pool.value_load(cnt_i[0:1, 2 * E:2 * E + 1], min_val=E, max_val=MAXB - 2)
            hmax = pool.to_reg(TPAD - 1)
            amax = pool.to_reg(2 * TPAD - 1)

            def gather(m):
                g.indirect_dma_start(out=xg, out_offset=None, in_=h_dram[:, :],
                                     in_offset=bass.IndirectOffsetOnAxis(ap=gcol[:, 0:1], axis=0),
                                     bounds_check=hmax, oob_is_err=True).then_inc(xg_ready, 16)

            for m in range(2):
                if m:
                    pool.wait_ge(xg_ready, 16)
                    pool.wait_ge(xtp_ready, 1)
                g.tensor_copy(gcol[:, :], gtab[:, m:m + 1]).then_inc(turn, 1)
                pool.wait_ge(turn, m + 2)
                gather(m)
            with pool.Fori(0, total) as m:
                pool.wait_ge(xg_ready, 16 * m + 32)
                pool.wait_ge(xtp_ready, m + 2)
                pool.sem_inc(turn, 1)
                g.tensor_copy(gcol[:, :], gtab[:, bass.ds(m + 2, 1)]).then_inc(turn, 1)
                pool.wait_ge(turn, 3 * m + 5)
                pool.sem_inc(pool_step, 1)
                gather(m + 2)
                pool.wait_ge(added, 16 * m + 16)
                pool.sem_inc(y_free, 1)
                g.tensor_copy(scol[:, :], stab[:, bass.ds(m, 1)]).then_inc(turn, 1)
                pool.wait_ge(turn, 3 * m + 6)
                pool.wait_ge(y_ready, m + 1)
                pool.sem_inc(pool_step, 1)
                g.indirect_dma_start(out=acc_dram[:, :], out_offset=bass.IndirectOffsetOnAxis(ap=scol[:, 0:1], axis=0),
                                     in_=ysb, in_offset=None, bounds_check=amax, oob_is_err=True,
                                     compute_op=ALU.add).then_inc(added, 16)
            pool.wait_ge(added, 16 * total + 16)
            pool.wait_ge(xg_ready, 16 * total + 32)
            pool.sem_inc(all_added, 1)


_INS = ["x_prompt", "x_sample", "cache_k", "cache_v", "state_conv", "attn_norm_g", "w_in", "attn_sinks",
        "conv_w", "conv_b", "conv_ln_g", "conv_ln_b", "w_out", "ffn_norm_g", "router_w", "router_b",
        "w1", "b1", "w2", "b2", "final_norm_g"]
_OUTS = [(1, PROMPT, D), (NB, NS, D), (1, 1, W, 2, HD), (1, 1, W, 2, HD), (1, 1, CTX, CW),
         (1, NB, W, 2, HD), (1, NB, W, 2, HD), (1, NB, CTX, CW)]


def kernel(**inputs):
    import numpy as _np
    import concourse.bacc as _bacc
    from concourse import mybir as _mybir
    from concourse.bass_utils import run_bass_kernel_spmd as _run

    nc = _bacc.Bacc("TRN2", target_bir_lowering=False, num_devices=1)
    arrays, args = {}, []
    consts, aconsts = tables()
    for name, a in [*((n, inputs[n]) for n in _INS), ("consts", consts), ("aconsts", aconsts)]:
        a = _np.ascontiguousarray(a)
        arrays[f"in_{name}_dram"] = a
        args.append(nc.dram_tensor(f"in_{name}_dram", a.shape, _mybir.dt.from_np(a.dtype), kind="ExternalInput").ap())
    for i, shape in enumerate(_OUTS):
        args.append(nc.dram_tensor(f"out_{i}_dram", shape, F32, kind="ExternalOutput").ap())
    args.append(nc.dram_tensor("h_rows", (TPAD, D), F32, kind="Internal").ap())
    args.append(nc.dram_tensor("acc_rows", (2 * TPAD, D // 2), F32, kind="Internal").ap())
    hybrid_step(nc, *args)
    r = _run(nc, [arrays], core_ids=[0])
    return tuple(r.results[0][f"out_{i}_dram"] for i in range(len(_OUTS)))
```
